# Optimizing a Trainium2 kernel written in Bass

```python
import math
import jax, jax.numpy as jnp
from jax import lax
import numpy as np

D_MODEL = 1024
BATCH = 1
SEQ = 128
DEPTH = 2
DEC_BATCH = 1
DEC_SEQ = 512
PAST_LEN = 128

GRID_W = 64
N_EVEN = (DEPTH + 1) // 2
N_ODD = DEPTH // 2
Q_BLOCK = 128
LN_EPS = 1e-5
RMS_EPS = 1e-6
DEEPNORM_ALPHA = (2.0 * DEPTH) ** 0.25
DEEPNORM_BETA = (8.0 * DEPTH) ** -0.25
ADA_INIT = 0.5
ROPE_BASE = 10000.0
RET_HEADS = 8
RET_DK = 64
RET_DV = 128
RET_CHUNK = 128
MLA_HEADS = 8
MLA_NOPE = 64
MLA_ROPE = 32
MLA_DV = 64
MLA_KV_RANK = 256
DIFF_HEADS = 8
DIFF_DH = 64
DIFF_DV = 2 * DIFF_DH
MOE_GROUPS = 4
MOE_PER_GROUP = 4
MOE_EXPERTS = MOE_GROUPS * MOE_PER_GROUP
MOE_TOPK = 2
MOE_FF = 256
EV_WIDTHS = (RET_HEADS * RET_DK, RET_HEADS * RET_DK, RET_HEADS * RET_DV, RET_HEADS * RET_DV,
             MLA_HEADS * (MLA_NOPE + MLA_ROPE), MLA_KV_RANK, MLA_ROPE)
EV_IN = sum(EV_WIDTHS)
EV_OUT = RET_HEADS * RET_DV + MLA_HEADS * MLA_DV
OD_WIDTHS = (DIFF_HEADS * 2 * DIFF_DH, DIFF_HEADS * 2 * DIFF_DH, DIFF_HEADS * DIFF_DV)
OD_IN = sum(OD_WIDTHS)
OD_OUT = DIFF_HEADS * DIFF_DV

kernel_name = 'hybrid_retention_mla_diffattn_hmoe_dit_step'

def _layer_norm(x, g, b):
    xf = x.astype(jnp.float32)
    mu = jnp.mean(xf, -1, keepdims=True)
    var = jnp.mean(jnp.square(xf - mu), -1, keepdims=True)
    y = (xf - mu) * lax.rsqrt(var + LN_EPS)
    return (y * g.astype(jnp.float32) + b.astype(jnp.float32)).astype(x.dtype)

def _head_norm(x):
    xf = x.astype(jnp.float32)
    mu = jnp.mean(xf, -1, keepdims=True)
    var = jnp.mean(jnp.square(xf - mu), -1, keepdims=True)
    return ((xf - mu) * lax.rsqrt(var + LN_EPS)).astype(x.dtype)

def _rms_norm(x, g):
    xf = x.astype(jnp.float32)
    y = xf * lax.rsqrt(jnp.mean(jnp.square(xf), -1, keepdims=True) + RMS_EPS)
    return (y * g.astype(jnp.float32)).astype(x.dtype)

def _split_cols(z, widths):
    cuts = [int(v) for v in np.cumsum(widths)[:-1]]
    return jnp.split(z, cuts, axis=-1)

def _heads(x, n):
    b, t, w = x.shape
    return x.reshape(b, t, n, w // n).transpose(0, 2, 1, 3)

def _merge_heads(x):
    b, n, t, d = x.shape
    return x.transpose(0, 2, 1, 3).reshape(b, t, n * d)

def _axial_rope(n_tokens, rot_dim):
    rows = n_tokens // GRID_W
    row = jnp.repeat(jnp.arange(rows, dtype=jnp.float32), GRID_W)
    col = jnp.tile(jnp.arange(GRID_W, dtype=jnp.float32), rows)
    n_freq = rot_dim // 4
    inv_freq = ROPE_BASE ** (-jnp.arange(n_freq, dtype=jnp.float32) / n_freq)
    ang = jnp.concatenate([row[:, None] * inv_freq, col[:, None] * inv_freq], axis=-1)
    return jnp.cos(ang), jnp.sin(ang)

def _apply_rope(x, cos, sin):
    x1, x2 = jnp.split(x, 2, axis=-1)
    cos = cos.astype(x.dtype)
    sin = sin.astype(x.dtype)
    return jnp.concatenate([x1 * cos - x2 * sin, x1 * sin + x2 * cos], axis=-1)

def _query_blocks(x):
    b, h, t, d = x.shape
    return jnp.moveaxis(x.reshape(b, h, t // Q_BLOCK, Q_BLOCK, d), 2, 0)

def _merge_blocks(y):
    nb, b, h, qb, d = y.shape
    return jnp.moveaxis(y, 0, 2).reshape(b, h, nb * qb, d)

def _softmax_attention(q, k, v, scale):
    def one(qb):
        s = jnp.einsum('bhqd,bhkd->bhqk', qb, k).astype(jnp.float32) * scale
        p = jax.nn.softmax(s, axis=-1)
        return jnp.einsum('bhqk,bhkd->bhqd', p.astype(v.dtype), v)
    return _merge_blocks(lax.map(one, _query_blocks(q)))

def _diff_attention(q1, q2, k1, k2, v, lam, scale):
    def one(qs):
        qa, qb = qs
        p1 = jax.nn.softmax(jnp.einsum('bhqd,bhkd->bhqk', qa, k1).astype(jnp.float32) * scale, axis=-1)
        p2 = jax.nn.softmax(jnp.einsum('bhqd,bhkd->bhqk', qb, k2).astype(jnp.float32) * scale, axis=-1)
        return jnp.einsum('bhqk,bhkd->bhqd', (p1 - lam * p2).astype(v.dtype), v)
    return _merge_blocks(lax.map(one, (_query_blocks(q1), _query_blocks(q2))))

def _retention_scan(q, k, v, log_gamma, s0):
    dtype = q.dtype
    b, h, t, dk = q.shape
    dv = v.shape[-1]
    c = RET_CHUNK
    n = t // c
    qc = q.astype(jnp.float32).reshape(b, h, n, c, dk)
    kc = k.astype(jnp.float32).reshape(b, h, n, c, dk)
    vc = v.astype(jnp.float32).reshape(b, h, n, c, dv)
    lg = log_gamma.astype(jnp.float32)
    idx = jnp.arange(c, dtype=jnp.float32)
    rel = idx[:, None] - idx[None, :]
    decay = jnp.where(rel >= 0, jnp.exp(lg[:, None, None] * jnp.maximum(rel, 0.0)), 0.0)
    scores = jnp.einsum('bhnid,bhnjd->bhnij', qc, kc) * decay[:, None]
    o_inner = jnp.einsum('bhnij,bhnje->bhnie', scores, vc)
    k_w = jnp.exp(lg[:, None] * (c - 1.0 - idx))
    kv = jnp.einsum('bhnjd,bhnje->bhnde', kc * k_w[:, None, :, None], vc)
    chunk_decay = jnp.exp(lg * c)[None, :, None, None]

    def step(s, kv_n):
        return chunk_decay * s + kv_n, s

    s_final, s_prev = lax.scan(step, s0.astype(jnp.float32), jnp.moveaxis(kv, 2, 0))
    q_w = jnp.exp(lg[:, None] * (idx + 1.0))
    o_cross = jnp.einsum('bhnid,nbhde->bhnie', qc * q_w[:, None, :, None], s_prev)
    o = (o_inner + o_cross).reshape(b, h, t, dv)
    return o.astype(dtype), s_final.astype(dtype)

def _bidir_retention(q, k, v, lg_f, lg_b, s_f0, s_b0):
    o_f, s_f = _retention_scan(q, k, v, lg_f, s_f0)
    o_b, s_b = _retention_scan(q[:, :, ::-1], k[:, :, ::-1], v[:, :, ::-1], lg_b, s_b0)
    return o_f + o_b[:, :, ::-1], s_f, s_b

def _even_mixer(h, wts, ctx=None, rope=None):
    w_in, w_out, dec_f, dec_b, kv_norm_g, w_uk, w_uv = wts
    b, t, _ = h.shape
    rq, rk, rv, rg, mq, ckv, kr = _split_cols(h @ w_in, EV_WIDTHS)
    q = _heads(rq, RET_HEADS)
    k = _heads(rk, RET_HEADS) * (RET_DK ** -0.5)
    v = _heads(rv, RET_HEADS)
    lg_f = jax.nn.log_sigmoid(dec_f.astype(jnp.float32))
    lg_b = jax.nn.log_sigmoid(dec_b.astype(jnp.float32))
    if ctx is None:
        s_f0 = jnp.zeros((b, RET_HEADS, RET_DK, RET_DV), jnp.float32)
        s_b0 = s_f0
    else:
        s_f0, s_b0, ckv_ctx, kr_ctx = ctx
    o, s_f, s_b = _bidir_retention(q, k, v, lg_f, lg_b, s_f0, s_b0)
    ret_out = jax.nn.silu(rg) * _merge_heads(_head_norm(o))
    ckv = _rms_norm(ckv, kv_norm_g)
    mq = _heads(mq, MLA_HEADS)
    q_nope, q_rope = mq[..., :MLA_NOPE], mq[..., MLA_NOPE:]
    ckv_all, kr_all = ckv, kr
    if ctx is not None:
        cos, sin = rope
        q_rope = _apply_rope(q_rope, cos, sin)
        ckv_all = jnp.concatenate([ckv_ctx.astype(ckv.dtype), ckv], axis=1)
        kr_all = jnp.concatenate([kr_ctx.astype(kr.dtype), _apply_rope(kr, cos, sin)], axis=1)
    n_k = ckv_all.shape[1]
    k_m = jnp.concatenate([_heads(ckv_all @ w_uk, MLA_HEADS),
                           jnp.broadcast_to(kr_all[:, None], (b, MLA_HEADS, n_k, MLA_ROPE))], axis=-1)
    v_m = _heads(ckv_all @ w_uv, MLA_HEADS)
    q_m = jnp.concatenate([q_nope, q_rope], axis=-1)
    mla_out = _merge_heads(_softmax_attention(q_m, k_m, v_m, (MLA_NOPE + MLA_ROPE) ** -0.5))
    out = jnp.concatenate([ret_out, mla_out], axis=-1) @ w_out
    extras = (s_f, s_b, ckv, kr) if ctx is None else None
    return out, extras

def _odd_mixer(h, wts, ctx=None, rope=None):
    w_in, w_out, lam_p, norm_g, lam_init = wts
    qa, ka, va = _split_cols(h @ w_in, OD_WIDTHS)
    q = _heads(qa, DIFF_HEADS)
    k = _heads(ka, DIFF_HEADS)
    v = _heads(va, DIFF_HEADS)
    extras = (k, v) if ctx is None else None
    q1, q2 = q[..., :DIFF_DH], q[..., DIFF_DH:]
    k1, k2 = k[..., :DIFF_DH], k[..., DIFF_DH:]
    if ctx is not None:
        cos, sin = rope
        k_ctx, v_ctx = ctx
        k_ctx = k_ctx.astype(k.dtype)
        q1, q2 = _apply_rope(q1, cos, sin), _apply_rope(q2, cos, sin)
        k1 = jnp.concatenate([k_ctx[..., :DIFF_DH], _apply_rope(k1, cos, sin)], axis=2)
        k2 = jnp.concatenate([k_ctx[..., DIFF_DH:], _apply_rope(k2, cos, sin)], axis=2)
        v = jnp.concatenate([v_ctx.astype(v.dtype), v], axis=2)
    lp = lam_p.astype(jnp.float32)
    lam = jnp.exp(jnp.sum(lp[0] * lp[1])) - jnp.exp(jnp.sum(lp[2] * lp[3])) + lam_init
    o = _diff_attention(q1, q2, k1, k2, v, lam, DIFF_DH ** -0.5)
    o = _rms_norm(o, norm_g) * (1.0 - lam_init)
    return _merge_heads(o) @ w_out, extras

def _hier_moe(x, w_group, b_group, w_expert, b_expert, w1, w3, w2):
    b, t, d = x.shape
    xt = x.reshape(b * t, d)
    g_prob = jax.nn.softmax((xt @ w_group + b_group).astype(jnp.float32), axis=-1)
    g_p, g_idx = lax.top_k(g_prob, 1)
    e_logits = (xt @ w_expert + b_expert).astype(jnp.float32).reshape(b * t, MOE_GROUPS, MOE_PER_GROUP)
    e_sel = jnp.einsum('ngp,ng->np', e_logits, jax.nn.one_hot(g_idx[:, 0], MOE_GROUPS, dtype=jnp.float32))
    e_p, e_idx = lax.top_k(jax.nn.softmax(e_sel, axis=-1), MOE_TOPK)
    gate_w = g_p * e_p / jnp.sum(e_p, axis=-1, keepdims=True)
    expert_ids = g_idx * MOE_PER_GROUP + e_idx
    combine = jnp.sum(jax.nn.one_hot(expert_ids, MOE_EXPERTS, dtype=jnp.float32) * gate_w[..., None], axis=1)
    hidden = jax.nn.silu(jnp.einsum('nd,edf->nef', xt, w1)) * jnp.einsum('nd,edf->nef', xt, w3)
    y = jnp.einsum('nef,efd->nd', hidden * combine[:, :, None].astype(hidden.dtype), w2)
    return y.reshape(b, t, d)

def _modulation(cond, w, b):
    return jax.nn.silu(cond) @ w + b

def _block(x, mod, mixer, ln, moe):
    sh1, sc1, g1, sh2, sc2, g2 = jnp.split(mod[:, None, :], 6, axis=-1)
    y, extras = mixer(x * (1.0 + sc1) + sh1)
    x = _layer_norm(DEEPNORM_ALPHA * x + g1 * y, ln[0], ln[1])
    x = _layer_norm(DEEPNORM_ALPHA * x + g2 * _hier_moe(x * (1.0 + sc2) + sh2, *moe), ln[2], ln[3])
    return x, extras

def setup_inputs(seed: int = 0) -> dict:
    key = jax.random.key(seed)
    ks = jax.random.split(key, 40)

    def nrm(k, shape, s=1.0):
        return s * jax.random.normal(k, shape, jnp.float32)

    gamma_logit = jnp.log(2.0 ** (5.0 + jnp.arange(RET_HEADS, dtype=jnp.float32)) - 1.0)
    return {
        'x_prompt': nrm(ks[0], (BATCH, SEQ, D_MODEL)),
        'x_sample': nrm(ks[1], (DEC_BATCH, DEC_SEQ, D_MODEL)),
        'state_ret_fwd': nrm(ks[2], (DEC_BATCH, N_EVEN, RET_HEADS, RET_DK, RET_DV)),
        'state_ret_bwd': nrm(ks[3], (DEC_BATCH, N_EVEN, RET_HEADS, RET_DK, RET_DV)),
        'cache_mla_ckv': nrm(ks[4], (DEC_BATCH, N_EVEN, PAST_LEN, MLA_KV_RANK)),
        'cache_mla_krope': nrm(ks[5], (DEC_BATCH, N_EVEN, PAST_LEN, MLA_ROPE)),
        'cache_diff_k': nrm(ks[6], (DEC_BATCH, N_ODD, DIFF_HEADS, PAST_LEN, 2 * DIFF_DH)),
        'cache_diff_v': nrm(ks[7], (DEC_BATCH, N_ODD, DIFF_HEADS, PAST_LEN, DIFF_DV)),
        'c': nrm(ks[8], (DEC_BATCH, D_MODEL)),
        'c_ctx': nrm(ks[9], (D_MODEL,)),
        'ada_w': nrm(ks[10], (DEPTH, D_MODEL, 6 * D_MODEL), ADA_INIT * D_MODEL ** -0.5),
        'ada_b': nrm(ks[11], (DEPTH, 6 * D_MODEL), 0.02),
        'ln1_g': 1.0 + nrm(ks[12], (DEPTH, D_MODEL), 0.02),
        'ln1_b': nrm(ks[13], (DEPTH, D_MODEL), 0.02),
        'ln2_g': 1.0 + nrm(ks[14], (DEPTH, D_MODEL), 0.02),
        'ln2_b': nrm(ks[15], (DEPTH, D_MODEL), 0.02),
        'ev_w_in': nrm(ks[16], (N_EVEN, D_MODEL, EV_IN), D_MODEL ** -0.5),
        'ev_w_out': nrm(ks[17], (N_EVEN, EV_OUT, D_MODEL), DEEPNORM_BETA * EV_OUT ** -0.5),
        'ret_decay_fwd': gamma_logit + nrm(ks[18], (N_EVEN, RET_HEADS), 0.1),
        'ret_decay_bwd': gamma_logit + nrm(ks[19], (N_EVEN, RET_HEADS), 0.1),
        'mla_kv_norm_g': 1.0 + nrm(ks[20], (N_EVEN, MLA_KV_RANK), 0.02),
        'mla_w_uk': nrm(ks[21], (N_EVEN, MLA_KV_RANK, MLA_HEADS * MLA_NOPE), MLA_KV_RANK ** -0.5),
        'mla_w_uv': nrm(ks[22], (N_EVEN, MLA_KV_RANK, MLA_HEADS * MLA_DV), MLA_KV_RANK ** -0.5),
        'od_w_in': nrm(ks[23], (N_ODD, D_MODEL, OD_IN), D_MODEL ** -0.5),
        'od_w_out': nrm(ks[24], (N_ODD, OD_OUT, D_MODEL), DEEPNORM_BETA * OD_OUT ** -0.5),
        'diff_lambda': nrm(ks[25], (N_ODD, 4, DIFF_DH), 0.1),
        'diff_norm_g': 1.0 + nrm(ks[26], (N_ODD, DIFF_DV), 0.02),
        'moe_w_group': nrm(ks[27], (DEPTH, D_MODEL, MOE_GROUPS), D_MODEL ** -0.5),
        'moe_b_group': nrm(ks[28], (DEPTH, MOE_GROUPS), 0.01),
        'moe_w_expert': nrm(ks[29], (DEPTH, D_MODEL, MOE_EXPERTS), D_MODEL ** -0.5),
        'moe_b_expert': nrm(ks[30], (DEPTH, MOE_EXPERTS), 0.01),
        'moe_w1': nrm(ks[31], (DEPTH, MOE_EXPERTS, D_MODEL, MOE_FF), D_MODEL ** -0.5),
        'moe_w3': nrm(ks[32], (DEPTH, MOE_EXPERTS, D_MODEL, MOE_FF), D_MODEL ** -0.5),
        'moe_w2': nrm(ks[33], (DEPTH, MOE_EXPERTS, MOE_FF, D_MODEL), DEEPNORM_BETA * MOE_FF ** -0.5),
    }

def reference(x_prompt, x_sample, state_ret_fwd, state_ret_bwd, cache_mla_ckv, cache_mla_krope,
              cache_diff_k, cache_diff_v, c, c_ctx, ada_w, ada_b, ln1_g, ln1_b, ln2_g, ln2_b,
              ev_w_in, ev_w_out, ret_decay_fwd, ret_decay_bwd, mla_kv_norm_g, mla_w_uk, mla_w_uv,
              od_w_in, od_w_out, diff_lambda, diff_norm_g, moe_w_group, moe_b_group, moe_w_expert,
              moe_b_expert, moe_w1, moe_w3, moe_w2):
    t_lat = x_sample.shape[1]
    rope_mla = _axial_rope(t_lat, MLA_ROPE)
    rope_diff = _axial_rope(t_lat, DIFF_DH)
    xp, xs = x_prompt, x_sample
    rf, rb, ck, kro, dk, dv = [], [], [], [], [], []
    for i in range(DEPTH):
        j = i // 2
        mod_p = _modulation(c_ctx[None, :], ada_w[i], ada_b[i])
        mod_s = _modulation(c, ada_w[i], ada_b[i])
        ln = (ln1_g[i], ln1_b[i], ln2_g[i], ln2_b[i])
        moe = (moe_w_group[i], moe_b_group[i], moe_w_expert[i], moe_b_expert[i], moe_w1[i], moe_w3[i], moe_w2[i])
        if i % 2 == 0:
            wts = (ev_w_in[j], ev_w_out[j], ret_decay_fwd[j], ret_decay_bwd[j], mla_kv_norm_g[j], mla_w_uk[j], mla_w_uv[j])
            ctx = (state_ret_fwd[:, j], state_ret_bwd[:, j], cache_mla_ckv[:, j], cache_mla_krope[:, j])
            xp, (s_f, s_b, ckv_new, kr_new) = _block(xp, mod_p, lambda h: _even_mixer(h, wts), ln, moe)
            xs, _ = _block(xs, mod_s, lambda h: _even_mixer(h, wts, ctx, rope_mla), ln, moe)
            rf.append(s_f)
            rb.append(s_b)
            ck.append(ckv_new)
            kro.append(kr_new)
        else:
            lam_init = 0.8 - 0.6 * math.exp(-0.3 * i)
            wts = (od_w_in[j], od_w_out[j], diff_lambda[j], diff_norm_g[j], lam_init)
            ctx = (cache_diff_k[:, j], cache_diff_v[:, j])
            xp, (k_new, v_new) = _block(xp, mod_p, lambda h: _odd_mixer(h, wts), ln, moe)
            xs, _ = _block(xs, mod_s, lambda h: _odd_mixer(h, wts, ctx, rope_diff), ln, moe)
            dk.append(k_new)
            dv.append(v_new)
    new_state_ret_fwd = jnp.stack(rf, axis=1)
    new_state_ret_bwd = jnp.stack(rb, axis=1)
    new_cache_mla_ckv = jnp.stack(ck, axis=1)
    new_cache_mla_krope = jnp.stack(kro, axis=1)
    new_cache_diff_k = jnp.stack(dk, axis=1)
    new_cache_diff_v = jnp.stack(dv, axis=1)
    return (xp, xs, new_state_ret_fwd, new_state_ret_bwd, new_cache_mla_ckv, new_cache_mla_krope, new_cache_diff_k, new_cache_diff_v)


_drawn_inputs = setup_inputs


def setup_inputs(seed=0):
    import zlib

    import numpy as np

    out = dict(_drawn_inputs(seed))
    spreads = {}
    factors = {'state_ret_fwd': 6.009,
     'state_ret_bwd': 5.815,
     'cache_mla_ckv': 8.0,
     'cache_mla_krope': 8.0,
     'cache_diff_k': 5.377,
     'cache_diff_v': 5.044,
     'mla_kv_norm_g': 2.897,
     'mla_w_uk': 7.018,
     'mla_w_uv': 3.166,
     'diff_lambda': 8.0,
     'diff_norm_g': 50.932,
     'moe_b_group': 61.043,
     'moe_b_expert': 64.0}
    for name, (base, spread) in spreads.items():
        noise = np.random.default_rng([zlib.crc32(name.encode()), seed]).standard_normal(out[name].shape)
        drawn = base * np.exp(spread * noise) if base else spread * noise
        out[name] = __import__('jax').numpy.asarray(drawn.astype(out[name].dtype))
    for name, factor in factors.items():
        out[name] = (out[name] * factor).astype(out[name].dtype)
    return out
```

```python
import math
from contextlib import ExitStack

import numpy as np
import concourse.bass as bass
from concourse import mybir

F32 = mybir.dt.float32
ALU = mybir.AluOpType
ACT = mybir.ActivationFunctionType
AX = mybir.AxisListType

P = 128
D = 1024
KD = D // P
SEQ, LAT, PAST = 128, 512, 128
NT = (SEQ + LAT) // P
TOK = NT * P
NK = NT + 1
KEYS = PAST + LAT
DEPTH = 2
GRID_W = 64
LN_EPS, RMS_EPS = 1e-5, 1e-6
ALPHA = (2.0 * DEPTH) ** 0.25
RH, RDK, RDV, RC = 8, 64, 128, 128
MH, MN, MR, MDV, MKV = 8, 64, 32, 64, 256
MQD = MN + MR
DH, DDH = 8, 64
DDV = 2 * DDH
G, EG = 4, 4
NE = G * EG
FF = 256
EV_W = (RH * RDK, RH * RDK, RH * RDV, RH * RDV, MH * MQD, MKV, MR)
EV_AT = [sum(EV_W[:n]) for n in range(len(EV_W))]
EV_IN = sum(EV_W)
EV_OUT = RH * RDV + MH * MDV
RQ, RK, RV, RG, MQ, CKV, KR = EV_AT
OD_IN = 3 * D
LAM_INIT = 0.8 - 0.6 * math.exp(-0.3)
NMOD = 6 * KD
BANK = 512
RET_SCALE = RDK ** -0.5
MLA_SCALE = MQD ** -0.5
DIFF_SCALE = DDH ** -0.5

C_ID, C_ONE, C_REL, C_MASK, C_POS, C_TIE, C_EPS = 0, 128, 256, 512, 768, 772, 776
C_N = 780


def constants():
    i = np.arange(P, dtype=np.float32)
    c = np.zeros((P, C_N), np.float32)
    c[:, C_ID:C_ID + P] = np.eye(P)
    c[:, C_ONE:C_ONE + P] = 1.0
    rel = i[None, :] - i[:, None]
    c[:, C_REL:C_REL + P] = np.maximum(rel, 0)
    c[:, C_REL + P:C_REL + 2 * P] = np.maximum(-rel, 0)
    c[:, C_MASK:C_MASK + P] = (rel >= 0) * RET_SCALE
    c[:, C_MASK + P:C_MASK + 2 * P] = (rel <= 0) * RET_SCALE
    for n, pos in enumerate((i + 1, RC - i, RC - 1 - i, i)):
        c[:, C_POS + n] = pos
    c[:, C_TIE:C_TIE + 4] = np.arange(4, 0, -1)
    c[:, C_EPS], c[:, C_EPS + 1] = LN_EPS, RMS_EPS

    def rope(dim):
        row = np.repeat(np.arange(LAT // GRID_W, dtype=np.float32), GRID_W)
        col = np.tile(np.arange(GRID_W, dtype=np.float32), LAT // GRID_W)
        nf = dim // 4
        inv = np.float32(10000.0) ** (-np.arange(nf, dtype=np.float32) / np.float32(nf))
        ang = np.concatenate([row[:, None] * inv, col[:, None] * inv], -1).astype(np.float32)
        return np.stack([np.cos(ang), np.sin(ang)]).astype(np.float32)

    return c, rope(MR), rope(DDH)


class Chain:

    def __init__(self, sem):
        self.sem, self.n = sem, 0

    def step(self, ins):
        self.n += 1
        ins.then_inc(self.sem, 1)
        return ins

    def join(self, eng):
        eng.wait_ge(self.sem, self.n)


def bc(ap, dim, n):
    a = ap.unsqueeze(dim)
    shape = list(a.shape)
    shape[dim] = n
    return a.to_broadcast(shape)


def build(nc, I, O):
    ctx = ExitStack()
    with ctx:
        arena = ctx.enter_context(nc.sbuf_tensor("arena", [P, 53200], F32))
        psum = ctx.enter_context(nc.psum_tensor("psum", [P, 8 * BANK], F32))

        def lasting_sem(name):
            return ctx.enter_context(nc.semaphore(name))

        stage_sems = []

        def sem(name):
            stage_sems.append(nc.alloc_semaphore(name=name))
            return stage_sems[-1]

        def recycle_sems():
            with nc.Block(no_gpsimd_drain=True) as block:
                @block.gpsimd
                def _(pool):
                    nc.clear_and_free_semaphores(stage_sems)
            stage_sems.clear()

        def at(off, *dims):
            n = int(np.prod(dims))
            v = arena[:, off:off + n]
            if len(dims) == 1:
                return v
            names = "abcd"[:len(dims)]
            return v.rearrange(f"p ({' '.join(names)}) -> p {' '.join(names)}",
                               **{names[i]: dims[i] for i in range(1, len(dims))})

        def bank(b, n=1):
            return psum[:, b * BANK:(b + n) * BANK]

        off = [0]

        def keep(*dims):
            o = off[0]
            off[0] += int(np.prod(dims))
            return at(o, *dims)

        x = keep(NT, D)
        const = keep(C_N)
        modc = keep(NMOD, 2)
        adab = keep(2, NMOD)
        cond = keep(KD, 2)
        kvg = keep(MKV)
        dng = keep(DDV)
        wr = keep(DEPTH, KD, G + NE)
        br = keep(DEPTH, G + NE)
        comb = keep(NT, NE)
        lam = keep(4)
        small = keep(256)
        BIG = off[0]
        proj = at(BIG, NT, EV_IN)
        R = BIG + NT * EV_IN
        assert R + 25000 <= 53200, R
        ident = const[:, C_ID:C_ID + P]
        ones = const[:, C_ONE:C_ONE + P]
        eps_ln, eps_rms = const[:, C_EPS:C_EPS + 1], const[:, C_EPS + 1:C_EPS + 2]

        dchain, achain, pchain = Chain(lasting_sem("vector_step")), Chain(lasting_sem("scalar_step")), Chain(lasting_sem("pool_step"))
        stored = lasting_sem("stored")
        stores = [0]

        def store(eng, out, in_):
            eng.dma_start(out, in_).then_inc(stored, 16)
            stores[0] += 16

        V, A, T = nc.vector, nc.scalar, nc.tensor

        def setup():
            loaded, rows_in = sem("inputs_loaded"), sem("rows_loaded")
            rows_t, cond_done = sem("rows_transposed"), sem("cond_done")
            crow = at(BIG, P)
            brow = at(BIG + P, 2, P)
            with nc.Block(no_gpsimd_drain=True) as block:
                @block.sync
                def _(sp):
                    sp.dma_start(const, I["consts"]).then_inc(rows_in, 16)
                    sp.dma_start(crow[0:KD, :], I["c_ctx"].rearrange("(k p) -> k p", p=P)).then_inc(rows_in, 16)
                    sp.dma_start(crow[KD:2 * KD, :], I["c"].rearrange("a (k p) -> (a k) p", p=P)).then_inc(rows_in, 16)
                    sp.dma_start(brow[0:NMOD, :, :], I["ada_b"].rearrange("i (k p) -> k i p", p=P)).then_inc(rows_in, 16)
                    sp.dma_start(x[:, 0, :], I["x_prompt"].rearrange("a p d -> p (a d)")).then_inc(loaded, 16)
                    sp.dma_start(x[:, 1:NT, :], I["x_sample"].rearrange("a (t p) d -> p (a t) d", p=P)).then_inc(loaded, 16)
                    sp.dma_start(kvg, I["mla_kv_norm_g"][0].partition_broadcast(P)).then_inc(loaded, 16)
                    sp.dma_start(dng, I["diff_norm_g"][0].partition_broadcast(P)).then_inc(loaded, 16)
                    for i in range(DEPTH):
                        sp.dma_start(wr[:, i, :, 0:G], I["moe_w_group"][i].rearrange("(k p) n -> p k n", p=P)).then_inc(loaded, 16)
                        sp.dma_start(wr[:, i, :, G:], I["moe_w_expert"][i].rearrange("(k p) n -> p k n", p=P)).then_inc(loaded, 16)
                        sp.dma_start(br[:, i, 0:G], I["moe_b_group"][i].partition_broadcast(P)).then_inc(loaded, 16)
                        sp.dma_start(br[:, i, G:], I["moe_b_expert"][i].partition_broadcast(P)).then_inc(loaded, 16)
                    sp.wait_ge(loaded, 16 * (4 + 4 * DEPTH))

                @block.tensor
                def _(pe):
                    pe.wait_ge(rows_in, 64)
                    T.transpose(bank(0)[:, 0:2 * KD], crow[0:2 * KD, :], ident[0:2 * KD, 0:2 * KD])
                    for i in range(DEPTH):
                        T.transpose(bank(0)[:, 64 + i * 64:64 + i * 64 + NMOD], brow[0:NMOD, i, :],
                                    ident[0:NMOD, 0:NMOD]).then_inc(rows_t, 1)

                @block.scalar
                def _(act):
                    act.wait_ge(rows_t, DEPTH)
                    A.activation(cond.rearrange("p k c -> p c k"), bank(0)[:, 0:2 * KD].rearrange("p (c k) -> p c k", c=2),
                                 ACT.Silu).then_inc(cond_done, 1)
                    for i in range(DEPTH):
                        A.activation(adab[:, i, :], bank(0)[:, 64 + i * 64:64 + i * 64 + NMOD], ACT.Copy)
                    act.drain()

        def modulation(i):
            NB, CW = 4, 768
            CH = 6 * D // CW
            TPC = CW // P
            wbuf = [at(R + b * KD * CW, KD, CW) for b in range(3)] + [at(BIG, KD, CW)]
            chunk_in = [sem(f"ada{i}_in{b}") for b in range(NB)]
            used, done = sem(f"ada{i}_used"), sem(f"mod{i}_done")
            w = I["ada_w"][i].rearrange("(k p) n -> p k n", p=P)
            with nc.Block(no_gpsimd_drain=True) as block:
                @block.sync
                def _(sp):
                    for c in range(CH):
                        if c >= NB:
                            sp.wait_ge(used, c - NB + 1)
                        sp.dma_start(wbuf[c % NB], w[:, :, c * CW:(c + 1) * CW]).then_inc(chunk_in[c % NB], 16)

                @block.tensor
                def _(pe):
                    for c in range(CH):
                        pe.wait_ge(chunk_in[c % NB], 16 * (c // NB + 1))
                        for j in range(TPC):
                            n = c * TPC + j
                            for k in range(KD):
                                last = T.matmul(bank(0)[:, 2 * n:2 * n + 2], wbuf[c % NB][:, k, j * P:(j + 1) * P],
                                                cond[:, k, :], start=(k == 0), stop=(k == KD - 1))
                        last.then_inc(used, 1)

                @block.vector
                def _(dve):
                    dve.wait_ge(used, CH)
                    dchain.step(V.tensor_tensor(modc, bank(0)[:, 0:2 * NMOD].rearrange("p (n c) -> p n c", c=2),
                                                bc(adab[:, i, :], 2, 2), ALU.add))
                    dchain.join(dve)
                    for s in (1, 4):
                        dchain.step(V.tensor_scalar(modc[:, s * KD:(s + 1) * KD, :], modc[:, s * KD:(s + 1) * KD, :],
                                                    1.0, None, ALU.add))
                    dchain.join(dve)

        def modulated(name, ht, sh, sc):
            tr, ev_a, ev_d = sem(f"{name}_tr"), sem(f"{name}_eva"), sem(f"{name}_evd")
            with nc.Block(no_gpsimd_drain=True) as block:
                @block.tensor
                def _(pe):
                    for k in range(KD):
                        if k >= 4:
                            pe.wait_ge((ev_a, ev_d)[k % 2], (k - 4) // 2 + 1)
                        for t in range(NT):
                            last = T.transpose(bank(2 * (k % 4), 2)[:, t * P:(t + 1) * P], x[:, t, k * P:(k + 1) * P], ident)
                        last.then_inc(tr, 1)

                @block.scalar
                def _(act):
                    for k in range(0, KD, 2):
                        act.wait_ge(tr, k + 1)
                        src = bank(2 * (k % 4), 2)
                        A.activation(ht[:, k, 0:P], src[:, 0:P], ACT.Identity,
                                     bias=modc[:, sh * KD + k, 0:1], scale=modc[:, sc * KD + k, 0:1])
                        A.activation(ht[:, k, P:TOK], src[:, P:TOK], ACT.Identity,
                                     bias=modc[:, sh * KD + k, 1:2], scale=modc[:, sc * KD + k, 1:2]).then_inc(ev_a, 1)

                @block.vector
                def _(dve):
                    for k in range(1, KD, 2):
                        dve.wait_ge(tr, k + 1)
                        src = bank(2 * (k % 4), 2)
                        V.tensor_scalar(ht[:, k, 0:P], src[:, 0:P], modc[:, sc * KD + k, 0:1],
                                        modc[:, sh * KD + k, 0:1], ALU.mult, ALU.add)
                        V.tensor_scalar(ht[:, k, P:TOK], src[:, P:TOK], modc[:, sc * KD + k, 1:2],
                                        modc[:, sh * KD + k, 1:2], ALU.mult, ALU.add).then_inc(ev_d, 1)
                    dve.drain()

        def project(name, w, width, ht, dst, wb):
            CW = 512
            cuts = [(c, min(CW, width - c)) for c in range(0, width, CW)]
            NB = 4
            chunk_in = [sem(f"{name}_in{b}") for b in range(NB)]
            used, group, ev_a, ev_d = (sem(f"{name}_{n}") for n in ("used", "group", "eva", "evd"))
            wv = w.rearrange("(k p) n -> p k n", p=P)
            wbuf = [at(wb + b * KD * CW, KD, CW) for b in range(NB)]
            with nc.Block(no_gpsimd_drain=True) as block:
                @block.sync
                def _(sp):
                    for c, (n0, cw) in enumerate(cuts):
                        if c >= NB:
                            sp.wait_ge(used, c - NB + 1)
                        sp.dma_start(wbuf[c % NB][:, :, 0:cw], wv[:, :, n0:n0 + cw]).then_inc(chunk_in[c % NB], 16)

                @block.tensor
                def _(pe):
                    for c, (n0, cw) in enumerate(cuts):
                        pe.wait_ge(chunk_in[c % NB], 16 * (c // NB + 1))
                        for t in range(NT):
                            g = c * NT + t
                            if g >= 8:
                                pe.wait_ge((ev_a, ev_d)[g % 2], (g - 8) // 2 + 1)
                            for k in range(KD):
                                last = T.matmul(bank(g % 8)[:, 0:cw], ht[:, k, t * P:(t + 1) * P],
                                                wbuf[c % NB][:, k, 0:cw], start=(k == 0), stop=(k == KD - 1))
                            last.then_inc(group, 1)
                        pe.wait_ge(group, NT * (c + 1))
                        pe.nop().then_inc(used, 1)

                def copies(eng, copy, first, done):
                    for g in range(first, NT * len(cuts), 2):
                        (n0, cw), t = cuts[g // NT], g % NT
                        eng.wait_ge(group, g + 1)
                        copy(dst[:, t, n0:n0 + cw], bank(g % 8)[:, 0:cw]).then_inc(done, 1)
                    eng.drain()

                @block.scalar
                def _(act):
                    copies(act, A.copy, 0, ev_a)

                @block.vector
                def _(dve):
                    copies(dve, V.tensor_copy, 1, ev_d)

        def gate_rows(name, g, rows, diag):
            made, summed, copied = sem(f"{name}_diag"), sem(f"{name}_sum"), sem(f"{name}_copy")
            with nc.Block(no_gpsimd_drain=True) as block:
                @block.vector
                def _(dve):
                    for c in range(2):
                        for k in range(KD):
                            V.tensor_scalar(diag[:, c, k, :], ident, modc[:, g * KD + k, c:c + 1], None,
                                            ALU.mult).then_inc(made, 1)

                @block.tensor
                def _(pe):
                    for n in range(4):
                        pe.wait_ge(made, 4 * (n + 1))
                        c, h = n // 2, n % 2
                        T.matmul(bank(n), ones, diag[:, c, 4 * h:4 * h + 4, :], start=True, stop=True).then_inc(summed, 1)

                @block.scalar
                def _(act):
                    for n in range(4):
                        c, h = n // 2, n % 2
                        act.wait_ge(summed, n + 1)
                        A.copy(rows[:, c, h * BANK:(h + 1) * BANK], bank(n)).then_inc(copied, 1)
                    act.drain()

        class Norm:
            def __init__(self, name, gb):
                self.var, self.root = sem(f"{name}_var"), sem(f"{name}_root")
                self.done = sem(f"{name}_done")
                self.g, self.b = gb[:, 0, :], gb[:, 1, :]
                self.stats, self.mv, self.rt = small[:, 0:12], small[:, 16:18], small[:, 20:22]

            def vector(self, dve, t, n):
                dchain.join(dve)
                for h in range(2):
                    dchain.step(V.bn_stats(self.stats[:, 6 * h:6 * h + 6], x[:, t, h * BANK:(h + 1) * BANK]))
                dchain.join(dve)
                V.bn_aggr(self.mv, self.stats).then_inc(self.var, 1)
                dve.wait_ge(self.root, n + 1)
                dchain.step(V.reciprocal(self.rt[:, 1:2], self.rt[:, 0:1]))
                dchain.join(dve)
                dchain.step(V.tensor_scalar(x[:, t, :], x[:, t, :], self.mv[:, 0:1], self.rt[:, 1:2], ALU.subtract, ALU.mult))
                dchain.join(dve)
                dchain.step(V.tensor_tensor(x[:, t, :], x[:, t, :], self.g, ALU.mult))
                dchain.join(dve)
                V.tensor_tensor(x[:, t, :], x[:, t, :], self.b, ALU.add).then_inc(self.done, 1)
                dve.wait_ge(self.done, n + 1)

            def scalar(self, act, n):
                act.wait_ge(self.var, n + 1)
                A.activation(self.rt[:, 0:1], self.mv[:, 1:2], ACT.Sqrt, bias=eps_ln).then_inc(self.root, 1)

        def mix_out(name, i, w, srcs):
            kt = len(srcs)
            catT = at(R, kt, TOK)
            wout = at(R + kt * TOK, kt, D)
            HTO = R + kt * TOK + kt * D
            rows = at(HTO, 2, D)
            gb = at(HTO + 2 * D, 2, D)
            diag = at(R, 2, KD, P)
            assert HTO + 4 * D <= 53200
            gate_rows(f"{name}_g1", 2, rows, diag)
            w_in = [sem(f"{name}_win{j}") for j in range(2)]
            ln_in, tr, ev_a, ev_d = (sem(f"{name}_{n}") for n in ("lnin", "tr", "eva", "evd"))
            half, gated = sem(f"{name}_half"), sem(f"{name}_gated")
            norm = Norm(f"{name}_ln", gb)
            wv = w.rearrange("(k p) n -> p k n", p=P)
            ytmp = at(BIG + (0 if name == "never" else 0), 1)
            with nc.Block(no_gpsimd_drain=True) as block:
                @block.sync
                def _(sp):
                    for j in range(2):
                        sp.dma_start(wout[:, :, j * BANK:(j + 1) * BANK], wv[:, :, j * BANK:(j + 1) * BANK]).then_inc(w_in[j], 16)
                    sp.dma_start(gb[:, 0, :], I["ln1_g"][i].partition_broadcast(P)).then_inc(ln_in, 16)
                    sp.dma_start(gb[:, 1, :], I["ln1_b"][i].partition_broadcast(P)).then_inc(ln_in, 16)

                @block.tensor
                def _(pe):
                    for k in range(kt):
                        if k >= 4:
                            pe.wait_ge((ev_a, ev_d)[k % 2], (k - 4) // 2 + 1)
                        for t in range(NT):
                            last = T.transpose(bank(2 * (k % 4), 2)[:, t * P:(t + 1) * P],
                                               srcs[k][:, t, :], ident)
                        last.then_inc(tr, 1)
                    pe.wait_ge(ev_a, (kt + 1) // 2)
                    pe.wait_ge(ev_d, kt // 2)
                    for j in range(2):
                        pe.wait_ge(w_in[j], 16)
                    for t in range(NT):
                        for j in range(2):
                            g = 2 * t + j
                            if g >= 8:
                                pe.wait_ge(gated, g - 7)
                            for k in range(kt):
                                last = T.matmul(bank(g % 8), catT[:, k, t * P:(t + 1) * P],
                                                wout[:, k, j * BANK:(j + 1) * BANK], start=(k == 0), stop=(k == kt - 1))
                            last.then_inc(half, 1)

                @block.scalar
                def _(act):
                    for k in range(0, kt, 2):
                        act.wait_ge(tr, k + 1)
                        A.copy(catT[:, k, :], bank(2 * (k % 4), 2)[:, 0:TOK]).then_inc(ev_a, 1)
                    for t in range(NT):
                        norm.scalar(act, t)

                @block.vector
                def _(dve):
                    for k in range(1, kt, 2):
                        dve.wait_ge(tr, k + 1)
                        V.tensor_copy(catT[:, k, :], bank(2 * (k % 4), 2)[:, 0:TOK]).then_inc(ev_d, 1)
                    dve.wait_ge(ln_in, 32)
                    for t in range(NT):
                        for j in range(2):
                            g = 2 * t + j
                            dve.wait_ge(half, g + 1)
                            tmp = at(BIG, 2, BANK)[:, j, :]
                            V.tensor_tensor(tmp, bank(g % 8), rows[:, min(t, 1), j * BANK:(j + 1) * BANK],
                                            ALU.mult).then_inc(gated, 1)
                            dve.wait_ge(gated, g + 1)
                            dchain.step(V.scalar_tensor_tensor(x[:, t, j * BANK:(j + 1) * BANK], x[:, t, j * BANK:(j + 1) * BANK],
                                                               ALPHA, tmp, ALU.mult, ALU.add))
                        norm.vector(dve, t, t)

        def retention():
            o = R
            dt = at(o, RH, P); o += RH * P
            tab = at(o, 2, 2, RH); o += 4 * RH
            lg = at(o, 2, RH); o += 2 * RH
            cd = at(o, RH); o += RH
            tl = at(o, 8, 2 * RH); o += 16 * RH
            st = at(o, NT - 1, RH, RDV); o += (NT - 1) * RH * RDV
            kv = at(o, NT, RH, RDV); o += NT * RH * RDV
            qq = at(o, NT - 1, RH, 2, RDK); o += (NT - 1) * RH * 2 * RDK
            SH = o
            kk = at(o, NT, RH, 2, RDK); o += NT * RH * 2 * RDK
            ex = at(o, 2, RH, P); o += 2 * RH * P
            assert o <= 53200, o
            qv = proj[:, :, RQ:RQ + RH * RDK].rearrange("p t (h d) -> p t h d", h=RH)
            kvw = proj[:, :, RK:RK + RH * RDK].rearrange("p t (h d) -> p t h d", h=RH)
            dec_in, st_in = sem("dec_in"), sem("state_in")
            dv, ac = sem("decay_v"), sem("decay_a")
            kk_done, kv_done, kv_out = sem("kk_done"), sem("kv_done"), sem("kv_copied")
            with nc.Block(no_gpsimd_drain=True) as block:
                @block.sync
                def _(sp):
                    sp.dma_start(tl[:, 0, 0:RH], I["ret_decay_fwd"][0].partition_broadcast(P)).then_inc(dec_in, 16)
                    sp.dma_start(tl[:, 0, RH:2 * RH], I["ret_decay_bwd"][0].partition_broadcast(P)).then_inc(dec_in, 16)
                    sp.dma_start(st[0:RDK, 0], I["state_ret_fwd"][0, 0].rearrange("h k v -> k h v")).then_inc(st_in, 16)
                    sp.dma_start(st[RDK:P, NT - 2], I["state_ret_bwd"][0, 0].rearrange("h k v -> k h v")).then_inc(st_in, 16)
                    sp.wait_ge(kv_out, 1)
                    store(sp, O["new_state_ret_fwd"][0, 0].rearrange("h k v -> k h v"), kv[0:RDK, 0])
                    store(sp, O["new_state_ret_bwd"][0, 0].rearrange("h k v -> k h v"), kv[RDK:P, 0])

                @block.vector
                def _(dve):
                    X, AXX, E, U, Dd, Rr, L, Mn = (tl[:, n, :] for n in range(8))
                    lgf = lg.rearrange("p a h -> p (a h)")
                    dve.wait_ge(dec_in, 32)
                    V.scalar_tensor_tensor(AXX, X, -1.0, X, ALU.mult, ALU.max).then_inc(dv, 1)
                    dve.wait_ge(ac, 1)
                    V.tensor_scalar(U, E, 1.0, None, ALU.add).then_inc(dv, 1)
                    dve.wait_ge(dv, 2)
                    dchain.step(V.tensor_scalar(Dd, U, 1.0, None, ALU.subtract))
                    dchain.step(V.tensor_scalar(Mn, X, 0.0, None, ALU.min))
                    dchain.join(dve)
                    dchain.step(V.tensor_tensor(Rr, E, Dd, ALU.subtract))
                    dchain.step(V.reciprocal(AXX, U))
                    dchain.join(dve)
                    dchain.step(V.tensor_tensor(Rr, Rr, AXX, ALU.mult))
                    dchain.join(dve)
                    dve.wait_ge(ac, 2)
                    dchain.step(V.tensor_tensor(L, L, Rr, ALU.add))
                    dchain.join(dve)
                    dchain.step(V.tensor_tensor(lgf, Mn, L, ALU.subtract))
                    dchain.join(dve)
                    for qk in range(2):
                        for d in range(2):
                            n = C_POS + 2 * qk + d
                            dchain.step(V.tensor_scalar(tab[:, qk, d, :], lg[:, d, :], const[:, n:n + 1], None, ALU.mult))
                    dchain.step(V.tensor_scalar(cd[0:RDK, :], lg[0:RDK, 0, :], float(RC), None, ALU.mult))
                    V.tensor_scalar(cd[RDK:P, :], lg[RDK:P, 1, :], float(RC), None, ALU.mult).then_inc(dv, 1)
                    dve.wait_ge(ac, 4)
                    dchain.step(V.tensor_scalar(tab[:, 1], tab[:, 1], RET_SCALE, None, ALU.mult))
                    dchain.join(dve)
                    for t in range(NT):
                        V.tensor_tensor(kk[:, t], bc(kvw[:, t], 2, 2), bc(tab[:, 1].rearrange("p d h -> p h d"), 3, RDK),
                                        ALU.mult).then_inc(kk_done, 1)
                    for t in range(1, NT):
                        dchain.step(V.tensor_tensor(qq[:, t - 1], bc(qv[:, t], 2, 2),
                                                    bc(tab[:, 0].rearrange("p d h -> p h d"), 3, RDK), ALU.mult))
                    dve.wait_ge(ac, 4 + 2 * RH)
                    for d in range(2):
                        dchain.step(V.tensor_tensor(ex[:, d], ex[:, d], bc(const[:, C_MASK + d * P:C_MASK + (d + 1) * P], 1, RH), ALU.mult))
                    dchain.join(dve)
                    dchain.step(V.tensor_tensor(dt, ex[:, 0], ex[:, 1], ALU.add))
                    dve.wait_ge(st_in, 32)
                    dve.wait_ge(kv_out, NT)
                    for n in range(NT - 2):
                        f, b = n, NT - 2 - n
                        dchain.step(V.tensor_tensor(st[0:RDK, f + 1], st[0:RDK, f], bc(cd[0:RDK], 2, RDV), ALU.mult))
                        dchain.step(V.tensor_tensor(st[RDK:P, b - 1], st[RDK:P, b], bc(cd[RDK:P], 2, RDV), ALU.mult))
                        dchain.join(dve)
                        dchain.step(V.tensor_tensor(st[0:RDK, f + 1], st[0:RDK, f + 1], kv[0:RDK, f + 1], ALU.add))
                        dchain.step(V.tensor_tensor(st[RDK:P, b - 1], st[RDK:P, b - 1], kv[RDK:P, b + 1], ALU.add))
                        dchain.join(dve)

                @block.tensor
                def _(pe):
                    for t in range(NT):
                        pe.wait_ge(kk_done, t + 1)
                        if t >= 4:
                            pe.wait_ge(kv_out, t - 3)
                        for h in range(RH):
                            last = T.matmul(bank(2 * (t % 4), 2)[:, h * RDV:(h + 1) * RDV],
                                            kk[:, t, h].rearrange("p d k -> p (d k)"),
                                            proj[:, t, RV + h * RDV:RV + (h + 1) * RDV], start=True, stop=True)
                        last.then_inc(kv_done, 1)

                @block.scalar
                def _(act):
                    act.wait_ge(dv, 1)
                    A.activation(tl[:, 2, :], tl[:, 1, :], ACT.Exp, scale=-1.0).then_inc(ac, 1)
                    act.wait_ge(dv, 2)
                    A.activation(tl[:, 6, :], tl[:, 3, :], ACT.Ln).then_inc(ac, 1)
                    act.wait_ge(dv, 3)
                    A.activation(tab, tab, ACT.Exp).then_inc(ac, 1)
                    A.activation(cd, cd, ACT.Exp).then_inc(ac, 1)
                    for d in range(2):
                        for h in range(RH):
                            A.activation(ex[:, d, h], const[:, C_REL + d * P:C_REL + (d + 1) * P], ACT.Exp,
                                         scale=lg[:, d, h:h + 1]).then_inc(ac, 1)
                    for t in range(NT):
                        act.wait_ge(kv_done, t + 1)
                        A.copy(kv[:, t], bank(2 * (t % 4), 2).rearrange("p (h v) -> p h v", h=RH)).then_inc(kv_out, 1)
                    for t in range(NT):
                        A.activation(proj[:, t, RG:RG + RH * RDV], proj[:, t, RG:RG + RH * RDV], ACT.Silu)
                    act.drain()

            o = SH
            qt = at(o, 2, 4, P); o += 8 * P
            ktt = at(o, 2, 4, P); o += 8 * P
            qqt = at(o, 2, RH, P); o += 2 * RH * P
            sm = at(o, 2, RH, P); o += 2 * RH * P
            cen = at(o, RH, RDV); o += RH * RDV
            bst = at(o, RH, 6); o += RH * 6
            bmv = at(o, RH, 2); o += RH * 2
            rt = at(o, 2, RH); o += 2 * RH
            assert o <= 53200
            trq, trc, scored, masked = sem("ret_tr"), sem("ret_trc"), sem("ret_scored"), sem("ret_masked")
            summed, centred, var, root = sem("ret_summed"), sem("ret_centred"), sem("ret_var"), sem("ret_root")
            with nc.Block(no_gpsimd_drain=True) as block:
                @block.tensor
                def _(pe):
                    def turn(t):
                        if t:
                            pe.wait_ge(trc, t)
                        for j in range(4):
                            T.transpose(bank(0)[:, j * P:(j + 1) * P], proj[:, t, RQ + j * P:RQ + (j + 1) * P], ident)
                            last = T.transpose(bank(1)[:, j * P:(j + 1) * P], proj[:, t, RK + j * P:RK + (j + 1) * P], ident)
                        if t:
                            for h in range(RH):
                                last = T.transpose(bank(2, 2)[:, h * P:(h + 1) * P], qq[:, t - 1, h].rearrange("p d k -> p (d k)"), ident)
                        last.then_inc(trq, 1)

                    turn(0)
                    for t in range(NT):
                        pe.wait_ge(trc, t + 1)
                        if t:
                            pe.wait_ge(masked, t)
                        for h in range(RH):
                            r, j = RDK * (h % 2), h // 2
                            last = T.matmul(bank(4 + h % 2)[:, j * P:(j + 1) * P], ktt[r:r + RDK, t % 2, j, :],
                                            qt[r:r + RDK, t % 2, j, :], start=True, stop=True)
                        last.then_inc(scored, 1)
                        if t + 1 < NT:
                            turn(t + 1)
                        pe.wait_ge(masked, t + 1)
                        if t:
                            pe.wait_ge(centred, t)
                        for h in range(RH):
                            out = bank(6, 2)[:, h * P:(h + 1) * P]
                            last = T.matmul(out, sm[:, t % 2, h, :], proj[:, t, RV + h * RDV:RV + (h + 1) * RDV],
                                            start=True, stop=(t == 0))
                            if t:
                                last = T.matmul(out, qqt[:, t % 2, h, :], st[:, t - 1, h, :], start=False, stop=True)
                        last.then_inc(summed, 1)

                @block.scalar
                def _(act):
                    for t in range(NT):
                        act.wait_ge(trq, t + 1)
                        if t >= 2:
                            act.wait_ge(summed, t - 1)
                        A.copy(qt[:, t % 2], bank(0).rearrange("p (j i) -> p j i", j=4))
                        last = A.copy(ktt[:, t % 2], bank(1).rearrange("p (j i) -> p j i", j=4))
                        if t:
                            last = A.copy(qqt[:, t % 2], bank(2, 2).rearrange("p (h i) -> p h i", h=RH))
                        last.then_inc(trc, 1)
                        if t:
                            act.wait_ge(var, t)
                            A.activation(rt[:, 0, :], bmv[:, :, 1], ACT.Sqrt, bias=eps_ln).then_inc(root, 1)
                    act.wait_ge(var, NT)
                    A.activation(rt[:, 0, :], bmv[:, :, 1], ACT.Sqrt, bias=eps_ln).then_inc(root, 1)

                @block.vector
                def _(dve):
                    def mask(t):
                        dve.wait_ge(scored, t + 1)
                        if t >= 2:
                            dve.wait_ge(summed, t - 1)
                        V.tensor_tensor(sm[:, t % 2].rearrange("p (j r) i -> p r j i", r=2),
                                        bank(4, 2).rearrange("p (r j i) -> p r j i", r=2, j=4),
                                        dt.rearrange("p (j r) i -> p r j i", r=2), ALU.mult).then_inc(masked, 1)

                    def norm(t):
                        dve.wait_ge(summed, t + 1)
                        src = bank(6, 2).rearrange("p (h v) -> p h v", h=RH)
                        for h in range(RH):
                            dchain.step(V.bn_stats(bst[:, h], src[:, h]))
                        dchain.join(dve)
                        for h in range(RH):
                            last = V.bn_aggr(bmv[:, h], bst[:, h])
                        last.then_inc(var, 1)
                        dve.wait_ge(var, t + 1)
                        V.tensor_tensor(cen, src, bc(bmv[:, :, 0], 2, RDV), ALU.subtract).then_inc(centred, 1)
                        dve.wait_ge(root, t + 1)
                        dchain.step(V.reciprocal(rt[:, 1, :], rt[:, 0, :]))
                        dchain.join(dve)
                        dve.wait_ge(centred, t + 1)
                        dchain.step(V.tensor_tensor(cen, cen, bc(rt[:, 1, :], 2, RDV), ALU.mult))
                        dchain.join(dve)
                        g = proj[:, t, RG:RG + RH * RDV].rearrange("p (h v) -> p h v", h=RH)
                        dchain.step(V.tensor_tensor(g, g, cen, ALU.mult))
                        dchain.join(dve)

                    mask(0)
                    for t in range(NT):
                        if t + 1 < NT:
                            mask(t + 1)
                        norm(t)

        def heads_attention(name, units, qT, kT, value, width, e_buf, halves, lamr, put, rsum, nmax, pT):
            scored, maxed, expd = sem(f"{name}_scored"), sem(f"{name}_maxed"), sem(f"{name}_expd")
            mixed = sem(f"{name}_mixed")
            turned, c_a, c_d, valued, put_s = (sem(f"{name}_{n}") for n in ("turned", "ca", "cd", "valued", "put"))
            U = len(units)
            tiles = [[NT] if t == 0 else list(range(NT)) for t, _ in units]

            def view(b, nk):
                if nk == 1:
                    return bank(2 * b)[:, 0:P]
                return bank(2 * b, 2).rearrange("p (a n) -> p a n", a=2)[:, :, 0:KEYS // 2]

            def flat(b, nk):
                e = e_buf[:, b, 0:nk * P]
                return e if nk == 1 else e.rearrange("p (a n) -> p a n", a=2)

            with nc.Block(no_gpsimd_drain=True) as block:
                @block.tensor
                def _(pe):
                    def score(u):
                        t, h = units[u]
                        for s in range(halves):
                            v = halves * u + s
                            if v >= 2:
                                pe.wait_ge(expd, v - 1)
                            q = qT(t, h, s)
                            if t == 0:
                                T.matmul(view(v % 2, 1), q, kT(h, s, NT * P, P), start=True, stop=True).then_inc(scored, 1)
                            else:
                                for a in range(2):
                                    last = T.matmul(view(v % 2, NT)[:, a], q, kT(h, s, a * KEYS // 2, KEYS // 2), start=True, stop=True)
                                last.then_inc(scored, 1)

                    def turn(u):
                        pe.wait_ge(mixed if halves == 2 else expd, u + 1)
                        if u:
                            pe.wait_ge(c_d, u)
                            pe.wait_ge(c_a, u)
                        src = e_buf[:, (u % 2) * halves, :]
                        for n in range(len(tiles[u])):
                            b, c = (4, n) if n < 3 else (5, n - 3)
                            last = T.transpose(bank(b)[:, c * P:(c + 1) * P], src[:, n * P:(n + 1) * P], ident)
                        last.then_inc(turned, 1)

                    def values(u):
                        t, h = units[u]
                        pe.wait_ge(c_d, u + 1)
                        pe.wait_ge(c_a, u + 1)
                        if u >= 2:
                            pe.wait_ge(put_s, u - 1)
                        for n, kt in enumerate(tiles[u]):
                            last = T.matmul(bank(6 + u % 2)[:, 0:width], pT[:, u % 2, n, :], value(h, kt),
                                            start=(n == 0), stop=(n == len(tiles[u]) - 1))
                        last.then_inc(valued, 1)

                    for u in range(U + 2):
                        if u < U:
                            score(u)
                        if u >= 2:
                            values(u - 2)
                        if 1 <= u <= U:
                            turn(u - 1)

                @block.vector
                def _(dve):
                    def top(u):
                        for s in range(halves):
                            v = halves * u + s
                            nk = len(tiles[u])
                            dve.wait_ge(scored, v + 1)
                            src = view(v % 2, nk)
                            V.tensor_reduce(nmax[:, v:v + 1], src, AX.X if nk == 1 else AX.XY, ALU.max,
                                            negate=True).then_inc(maxed, 1)

                    def mix(u):
                        dve.wait_ge(expd, halves * (u + 1))
                        dchain.step(V.reciprocal(rsum[:, 1, halves * u:halves * (u + 1)], rsum[:, 0, halves * u:halves * (u + 1)]))
                        dchain.join(dve)
                        if halves == 2:
                            nk = len(tiles[u]) * P
                            r = rsum[:, 1, 2 * u:2 * u + 2]
                            e1, e2 = (e_buf[:, 2 * (u % 2) + s, 0:nk] for s in range(2))
                            dchain.step(V.tensor_tensor(r[:, 1:2], r[:, 1:2], lamr, ALU.mult))
                            dchain.join(dve)
                            dchain.step(V.tensor_scalar(e2, e2, r[:, 1:2], None, ALU.mult))
                            dchain.join(dve)
                            V.scalar_tensor_tensor(e1, e1, r[:, 0:1], e2, ALU.mult, ALU.subtract).then_inc(mixed, 1)

                    def copy_p(u):
                        dve.wait_ge(turned, u + 1)
                        if u >= 2:
                            dve.wait_ge(valued, u - 1)
                        nd = min(3, len(tiles[u]))
                        V.tensor_copy(pT[:, u % 2, 0:nd], bank(4)[:, 0:nd * P].rearrange("p (n q) -> p n q", n=nd)).then_inc(c_d, 1)

                    def out(u):
                        dve.wait_ge(valued, u + 1)
                        src = bank(6 + u % 2)[:, 0:width]
                        if halves == 2:
                            V.tensor_copy(put(*units[u]), src).then_inc(put_s, 1)
                        else:
                            V.tensor_scalar(put(*units[u]), src, rsum[:, 1, u:u + 1], None, ALU.mult).then_inc(put_s, 1)

                    for u in range(U + 2):
                        if u < U:
                            top(u)
                        if 1 <= u <= U:
                            mix(u - 1)
                        if u >= 2:
                            out(u - 2)
                        if 1 <= u <= U:
                            copy_p(u - 1)
                    dve.drain()

                @block.scalar
                def _(act):
                    def exps(u):
                        for s in range(halves):
                            v = halves * u + s
                            nk = len(tiles[u])
                            act.wait_ge(maxed, v + 1)
                            if u >= 2:
                                act.wait_ge(turned, u - 1)
                            A.activation(flat((u % 2) * halves + s, nk), view(v % 2, nk), ACT.Exp,
                                         bias=nmax[:, v:v + 1], accum_out=rsum[:, 0, v:v + 1]).then_inc(expd, 1)

                    def copy_p(u):
                        act.wait_ge(turned, u + 1)
                        if u >= 2:
                            act.wait_ge(valued, u - 1)
                        n = len(tiles[u])
                        if n > 3:
                            A.copy(pT[:, u % 2, 3:n], bank(5)[:, 0:(n - 3) * P].rearrange("p (n q) -> p n q", q=P)).then_inc(c_a, 1)
                        else:
                            act.nop().then_inc(c_a, 1)

                    for u in range(U + 1):
                        if u < U:
                            exps(u)
                        if u >= 1:
                            copy_p(u - 1)

        UNITS = [(t, h) for t in range(1, NT) for h in range(8)] + [(0, h) for h in range(8)]

        def latent_attention():
            o = R
            kT = at(o, MH, NK * P); o += MH * NK * P
            qT = at(o, MH, TOK); o += MH * TOK
            vm = at(o, NK, MH * MDV); o += NK * MH * MDV
            E_AT = o
            ckc = at(o, MKV); o += MKV
            krp = at(o, NK, MQD); o += NK * MQD
            rope = at(o, 2, NT - 1, MR // 2); o += (NT - 1) * MR
            tmp = at(o, 4, NT - 1, MH, MR // 2); o += 4 * (NT - 1) * MH * MR // 2
            tmk = at(o, 4, NT - 1, MR // 2); o += 4 * (NT - 1) * MR // 2
            ckT = at(o, 2, NK * P); o += 2 * NK * P
            wuk = at(o, 2, MH * MN); o += 2 * MH * MN
            wuv = at(o, 2, MH * MDV); o += 2 * MH * MDV
            junk = at(o, MKV); o += MKV
            ss = at(o, 2, NT); o += 2 * NT
            assert o <= 53200, o
            loaded, w_in, kr_in = sem("mla_loaded"), sem("mla_win"), sem("mla_krin")
            squared, normed, roped, padded = sem("mla_sq"), sem("mla_norm"), sem("mla_rope"), sem("mla_pad")
            tr, ev_a, ev_d = sem("mla_tr"), sem("mla_eva"), sem("mla_evd")
            ck = proj[:, :, CKV:CKV + MKV]
            kr = proj[:, :, KR:KR + MR]
            mq = proj[:, :, MQ:MQ + MH * MQD].rearrange("p t (h d) -> p t h d", h=MH)
            H2 = MR // 2

            items = []
            for c in range(2):
                items.append(("ck", c))
            items.append(("kr", 0))
            for h in range(MH):
                items.append(("q", h))
            for j in range(MH // 2):
                items.append(("k", j))
            for n in range(NK // 2):
                items.append(("v", n))
            def evac(eng, who):
                copy = A.copy if who == 0 else V.tensor_copy
                done = (ev_a, ev_d)[who]
                for n, (kind, j) in enumerate(items):
                    if n % 2 != who:
                        continue
                    eng.wait_ge(tr, n + 1)
                    src = bank(2 * (n % 4), 2)
                    if kind == "ck":
                        copy(ckT[:, j, :], src[:, 0:NK * P]).then_inc(done, 1)
                    elif kind == "kr":
                        copy(kT[MN:MQD], bc(src[MN:MQD, 0:NK * P], 1, MH)).then_inc(done, 1)
                    elif kind == "q":
                        if who == 0:
                            A.mul(qT[0:MQD, j, :], src[0:MQD, 0:TOK], MLA_SCALE).then_inc(done, 1)
                        else:
                            V.tensor_scalar(qT[0:MQD, j, :], src[0:MQD, 0:TOK], MLA_SCALE, None, ALU.mult).then_inc(done, 1)
                    elif kind == "k":
                        s2 = src.rearrange("p (a n) -> p a n", a=2)[:, :, 0:NK * P // 2]
                        for r in range(2):
                            last = copy(kT[0:MN, 2 * j + r, :].rearrange("p (a n) -> p a n", a=2), s2[MN * r:MN * (r + 1)])
                        last.then_inc(done, 1)
                    else:
                        copy(vm[:, 2 * j:2 * j + 2, :], src.rearrange("p (a n) -> p a n", a=2)).then_inc(done, 1)

            with nc.Block(no_gpsimd_drain=True) as block:
                @block.sync
                def _(sp):
                    sp.dma_start(krp[:, 0, MN:MQD], I["cache_mla_krope"][0, 0]).then_inc(kr_in, 16)
                    sp.dma_start(ckc, I["cache_mla_ckv"][0, 0]).then_inc(kr_in, 16)
                    sp.dma_start(rope, I["rope_mla"].rearrange("a (t p) n -> p a t n", p=P)).then_inc(loaded, 16)
                    sp.dma_start(wuk, I["mla_w_uk"][0].rearrange("(k p) n -> p k n", p=P)).then_inc(w_in, 16)
                    sp.dma_start(wuv, I["mla_w_uv"][0].rearrange("(k p) n -> p k n", p=P)).then_inc(w_in, 16)
                    store(sp, O["new_cache_mla_krope"][0, 0], kr[:, 0, :])
                    sp.wait_ge(normed, 1)
                    store(sp, O["new_cache_mla_ckv"][0, 0], ck[:, 0, :])

                @block.scalar
                def _(act):
                    for t in range(NT):
                        achain.step(A.activation(junk, ck[:, t, :], ACT.Square, accum_out=ss[:, 0, t:t + 1]))
                        achain.join(act)
                    A.activation(ss[:, 1, :], ss[:, 0, :], ACT.Sqrt, bias=eps_rms, scale=1.0 / MKV).then_inc(squared, 1)
                    evac(act, 0)
                    act.drain()

                @block.vector
                def _(dve):
                    V.memset(krp[:, :, 0:MN], 0.0).then_inc(padded, 1)
                    dve.wait_ge(squared, 1)
                    dchain.step(V.reciprocal(ss[:, 0, :], ss[:, 1, :]))
                    dchain.join(dve)
                    for t in range(NT):
                        V.scalar_tensor_tensor(ck[:, t, :], ck[:, t, :], ss[:, 0, t:t + 1], kvg, ALU.mult, ALU.mult).then_inc(normed, 1)
                    dve.wait_ge(loaded, 16)
                    for x1, x2, y1, y2, tm, cs in (
                            (mq[:, 1:NT, :, MN:MN + H2], mq[:, 1:NT, :, MN + H2:MQD], mq[:, 1:NT, :, MN:MN + H2],
                             mq[:, 1:NT, :, MN + H2:MQD], tmp, [bc(rope[:, s], 2, MH) for s in range(2)]),
                            (kr[:, 1:NT, 0:H2], kr[:, 1:NT, H2:MR], krp[:, 1:NT, MN:MN + H2], krp[:, 1:NT, MN + H2:MQD],
                             tmk, [rope[:, s] for s in range(2)])):
                        for n, (src, s) in enumerate(((x1, 0), (x2, 1), (x1, 1), (x2, 0))):
                            dchain.step(V.tensor_tensor(tm[:, n], src, cs[s], ALU.mult))
                        dchain.join(dve)
                        dchain.step(V.tensor_tensor(y1, tm[:, 0], tm[:, 1], ALU.subtract))
                        V.tensor_tensor(y2, tm[:, 2], tm[:, 3], ALU.add).then_inc(roped, 1)
                    V.tensor_copy(krp[:, NT, MN:MQD], kr[:, 0, :]).then_inc(roped, 1)
                    evac(dve, 1)
                    dve.drain()

                @block.tensor
                def _(pe):
                    for n, (kind, j) in enumerate(items):
                        if n >= 4:
                            pe.wait_ge((ev_a, ev_d)[n % 2], (n - 4) // 2 + 1)
                        dst = bank(2 * (n % 4), 2)
                        if kind == "ck":
                            if j == 0:
                                pe.wait_ge(kr_in, 32)
                                pe.wait_ge(normed, NT)
                            for m in range(NK):
                                src = ckc if m == 0 else ck[:, m % NT, :]
                                last = T.transpose(dst[:, m * P:(m + 1) * P], src[:, j * P:(j + 1) * P], ident)
                        elif kind == "kr":
                            pe.wait_ge(roped, 3)
                            pe.wait_ge(padded, 1)
                            for m in range(NK):
                                last = T.transpose(dst[0:MQD, m * P:(m + 1) * P], krp[:, m, :], ident)
                        elif kind == "q":
                            for t in range(NT):
                                last = T.transpose(dst[0:MQD, t * P:(t + 1) * P], mq[:, t, j, :], ident)
                        elif kind == "k":
                            if j == 0:
                                pe.wait_ge(ev_a, 1)
                                pe.wait_ge(ev_d, 1)
                                pe.wait_ge(w_in, 32)
                            for a in range(2):
                                for k in range(2):
                                    last = T.matmul(dst[:, a * BANK:a * BANK + NK * P // 2], wuk[:, k, j * P:(j + 1) * P],
                                                    ckT[:, k, a * NK * P // 2:(a + 1) * NK * P // 2], start=(k == 0), stop=(k == 1))
                        else:
                            for a in range(2):
                                m = 2 * j + a
                                for k in range(2):
                                    last = T.matmul(dst[:, a * BANK:(a + 1) * BANK], ckT[:, k, m * P:(m + 1) * P],
                                                    wuv[:, k, :], start=(k == 0), stop=(k == 1))
                        last.then_inc(tr, 1)

            o = E_AT
            e_buf = at(o, 2, KEYS); o += 2 * KEYS
            pT = at(o, 2, NT, P); o += 2 * NT * P
            rsum = at(o, 2, len(UNITS)); o += 2 * len(UNITS)
            nmax = at(o, len(UNITS)); o += len(UNITS)
            heads_attention(
                "mla", UNITS,
                lambda t, h, s: qT[0:MQD, h, t * P:(t + 1) * P],
                lambda h, s, k0, n: kT[0:MQD, h, k0:k0 + n],
                lambda h, kt: vm[:, kt, h * MDV:(h + 1) * MDV],
                MDV, e_buf, 1, None,
                lambda t, h: proj[:, t, MQ + h * MDV:MQ + (h + 1) * MDV], rsum, nmax, pT)

        def differential_attention(pj):
            o = R
            kT = at(o, DH, NK * P); o += DH * NK * P
            qT = at(o, DH, TOK); o += DH * TOK
            vc = at(o, DH, DDV); o += DH * DDV
            kc = at(o, DH, DDV)
            rope = at(o + DH * DDV, 2, NT - 1, DDH // 2)
            tmp = at(o + 2 * DH * DDV, 4, 32, DDH // 2)
            lp = at(o + 2 * DH * DDV + 4096, 4, DDH)
            assert o + 2 * DH * DDV + 4096 + 256 <= 53200
            H2 = DDH // 2
            QS = 4 * DH
            loaded, k_in = sem("diff_loaded"), sem("diff_kin")
            roped, tr, ev_a, ev_d, lam_v, lam_a = (sem(f"diff_{n}") for n in ("roped", "tr", "eva", "evd", "lamv", "lama"))
            lam1 = small[:, 32:34]
            def evac(eng, who):
                done = (ev_a, ev_d)[who]
                for n, (kind, h) in enumerate(items):
                    if n % 2 != who:
                        continue
                    eng.wait_ge(tr, n + 1)
                    src = bank(2 * (n % 4), 2)
                    dst, w, scale = (qT[:, h, :], TOK, DIFF_SCALE) if kind == "q" else (kT[:, h, :], NK * P, 1.0)
                    if who == 0:
                        A.mul(dst, src[:, 0:w], scale).then_inc(done, 1)
                    else:
                        V.tensor_scalar(dst, src[:, 0:w], scale, None, ALU.mult).then_inc(done, 1)

            with nc.Block(no_gpsimd_drain=True) as block:
                @block.sync
                def _(sp):
                    sp.dma_start(rope, I["rope_diff"].rearrange("a (t p) n -> p a t n", p=P)).then_inc(loaded, 16)
                    sp.dma_start(lp, I["diff_lambda"][0].partition_broadcast(P)).then_inc(loaded, 16)
                    sp.dma_start(kc, I["cache_diff_k"][0, 0].rearrange("h p d -> p h d")).then_inc(k_in, 16)
                    sp.dma_start(vc, I["cache_diff_v"][0, 0].rearrange("h p d -> p h d")).then_inc(k_in, 16)
                    store(sp, O["new_cache_diff_k"][0, 0].rearrange("h p d -> p h d"),
                          pj[:, 0, D:2 * D].rearrange("p (h d) -> p h d", h=DH))
                    store(sp, O["new_cache_diff_v"][0, 0].rearrange("h p d -> p h d"),
                          pj[:, 0, 2 * D:3 * D].rearrange("p (h d) -> p h d", h=DH))

                items = [("q", h) for h in range(DH)] + [("k", h) for h in range(DH)]

                @block.vector
                def _(dve):
                    dve.wait_ge(loaded, 32)
                    for t in range(1, NT):
                        xs = pj[:, t, 0:2 * D].rearrange("p (g d) -> p g d", d=DDH)
                        x1, x2 = xs[:, :, 0:H2], xs[:, :, H2:DDH]
                        cs = [bc(rope[:, s, t - 1], 1, QS) for s in range(2)]
                        for n, (src, s) in enumerate(((x1, 0), (x2, 1), (x1, 1), (x2, 0))):
                            dchain.step(V.tensor_tensor(tmp[:, n], src, cs[s], ALU.mult))
                        dchain.join(dve)
                        dchain.step(V.tensor_tensor(x1, tmp[:, 0], tmp[:, 1], ALU.subtract))
                        V.tensor_tensor(x2, tmp[:, 2], tmp[:, 3], ALU.add).then_inc(roped, 1)
                        dve.wait_ge(roped, t)
                    lq = lp.rearrange("p (a b) d -> p a b d", a=2)
                    dchain.step(V.tensor_tensor(lq[:, :, 0], lq[:, :, 0], lq[:, :, 1], ALU.mult))
                    dchain.join(dve)
                    V.tensor_reduce(lam1, lq[:, :, 0], AX.X, ALU.add).then_inc(lam_v, 1)
                    evac(dve, 1)
                    dve.wait_ge(lam_a, 1)
                    dchain.step(V.tensor_tensor(lam[:, 0:1], lam[:, 2:3], lam[:, 3:4], ALU.subtract))
                    dchain.join(dve)
                    dchain.step(V.tensor_scalar(lam[:, 0:1], lam[:, 0:1], LAM_INIT, None, ALU.add))
                    dve.drain()

                @block.scalar
                def _(act):
                    act.wait_ge(lam_v, 1)
                    A.activation(lam[:, 2:4], lam1, ACT.Exp).then_inc(lam_a, 1)
                    evac(act, 0)
                    act.drain()

                @block.tensor
                def _(pe):
                    pe.wait_ge(roped, NT - 1)
                    pe.wait_ge(k_in, 32)
                    for n, (kind, h) in enumerate(items):
                        if n >= 4:
                            pe.wait_ge((ev_a, ev_d)[n % 2], (n - 4) // 2 + 1)
                        dst = bank(2 * (n % 4), 2)
                        if kind == "q":
                            for t in range(NT):
                                last = T.transpose(dst[:, t * P:(t + 1) * P], pj[:, t, h * DDV:(h + 1) * DDV], ident)
                        else:
                            for m in range(NK):
                                src = kc[:, h, :] if m == 0 else pj[:, m % NT, D + h * DDV:D + (h + 1) * DDV]
                                last = T.transpose(dst[:, m * P:(m + 1) * P], src, ident)
                        last.then_inc(tr, 1)

            o = R + DH * NK * P + DH * TOK + DH * DDV
            e_buf = at(o, 4, KEYS); o += 4 * KEYS
            pT = at(o, 2, NT, P); o += 2 * NT * P
            rsum = at(o, 2, 2 * len(UNITS)); o += 4 * len(UNITS)
            nmax = at(o, 2 * len(UNITS)); o += 2 * len(UNITS)
            heads_attention(
                "diff", UNITS,
                lambda t, h, s: qT[DDH * s:DDH * (s + 1), h, t * P:(t + 1) * P],
                lambda h, s, k0, n: kT[DDH * s:DDH * (s + 1), h, k0:k0 + n],
                lambda h, kt: vc[:, h, :] if kt == 0 else pj[:, kt % NT, 2 * D + h * DDV:2 * D + (h + 1) * DDV],
                DDV, e_buf, 2, lam[:, 0:1],
                lambda t, h: pj[:, t, h * DDV:(h + 1) * DDV], rsum, nmax, pT)

            sq = at(R, 2, D)
            ss = at(R + 2 * D, NT, DH)
            rt = at(R + 2 * D + NT * DH, 2, NT, DH)
            squared, rooted, freed, gs = sem("dn_squared"), sem("dn_root"), sem("dn_freed"), sem("dn_sums")
            with nc.Block(no_gpsimd_drain=True) as block:
                @block.scalar
                def _(act):
                    for t in range(NT):
                        if t >= 2:
                            act.wait_ge(freed, t - 1)
                        A.activation(sq[:, t % 2, :], pj[:, t, 0:D], ACT.Square).then_inc(squared, 1)
                    act.wait_ge(freed, NT)
                    A.activation(rt[:, 0], ss, ACT.Sqrt, bias=eps_rms, scale=1.0 / DDV).then_inc(rooted, 1)

                @block.vector
                def _(dve):
                    dchain.step(V.tensor_scalar(dng, dng, 1.0 - LAM_INIT, None, ALU.mult))
                    for t in range(NT):
                        dve.wait_ge(squared, t + 1)
                        V.tensor_reduce(ss[:, t, :], sq[:, t % 2, :].rearrange("p (h v) -> p h v", h=DH), AX.X,
                                        ALU.add).then_inc(freed, 1)
                    dve.wait_ge(rooted, 1)
                    dchain.step(V.reciprocal(rt[:, 1], rt[:, 0]))
                    dchain.join(dve)
                    for t in range(NT):
                        ov = pj[:, t, 0:D].rearrange("p (h v) -> p h v", h=DH)
                        dchain.step(V.tensor_tensor(ov, ov, bc(rt[:, 1, t, :], 2, DDV), ALU.mult))
                        dchain.join(dve)
                        dchain.step(V.tensor_tensor(ov, ov, bc(dng, 1, DH), ALU.mult))
                    dve.drain()

        def router(i, ht):
            logits, mx, tie, oh, eg = (at(R + 256 * n, 256) for n in range(5))
            lo = logits[:, 0:NT * (G + NE)].rearrange("p (t n) -> p t n", t=NT)
            scored, nm, ex = sem(f"r{i}_scored"), sem(f"r{i}_neg"), sem(f"r{i}_exp")
            w = R + 2048

            def b4(n):
                return at(w + n * 64, NT, G)

            def b1(n):
                return at(w + 1024 + n * 8, NT)

            sel, pg, pe_, ohg, oh1, oh2, t4, p2 = (b4(n) for n in range(8))
            gm, gs_, em, s1, s2, gp, a1, a2, tm1 = (b1(n) for n in range(9))
            prod = at(w + 2048, NT, G, EG)
            tie4 = bc(const[:, C_TIE:C_TIE + 4], 1, NT)
            with nc.Block(no_gpsimd_drain=True) as block:
                @block.tensor
                def _(pe):
                    for t in range(NT):
                        for k in range(KD):
                            last = T.matmul(bank(0)[:, t * 32:t * 32 + G + NE], ht[:, k, t * P:(t + 1) * P],
                                            wr[:, i, k, :], start=(k == 0), stop=(k == KD - 1))
                    last.then_inc(scored, 1)

                @block.vector
                def _(dve):
                    def do(ins):
                        dchain.step(ins)
                        dchain.join(dve)

                    def first_of(out, vals, top):
                        do(V.tensor_tensor(out, vals, bc(top, 2, 4), ALU.is_equal))
                        do(V.tensor_tensor(out, out, tie4, ALU.mult))
                        do(V.tensor_reduce(tm1, out, AX.X, ALU.max))
                        do(V.tensor_tensor(out, out, bc(tm1, 2, 4), ALU.is_equal))

                    dve.wait_ge(scored, 1)
                    do(V.tensor_tensor(lo, bank(0)[:, 0:NT * 32].rearrange("p (t n) -> p t n", t=NT)[:, :, 0:G + NE],
                                       bc(br[:, i, :], 1, NT), ALU.add))
                    lgp = lo[:, :, 0:G]
                    do(V.tensor_reduce(gm, lgp, AX.X, ALU.max))
                    first_of(ohg, lgp, gm)
                    V.tensor_tensor(pg, lgp, bc(gm, 2, G), ALU.subtract).then_inc(nm, 1)
                    do(V.tensor_tensor(prod, lo[:, :, G:].rearrange("p t (g e) -> p t g e", g=G), bc(ohg, 3, EG), ALU.mult))
                    do(V.tensor_reduce(sel, prod.rearrange("p t g e -> p t e g"), AX.X, ALU.add))
                    do(V.tensor_reduce(em, sel, AX.X, ALU.max))
                    V.tensor_tensor(pe_, sel, bc(em, 2, EG), ALU.subtract).then_inc(nm, 1)
                    dve.wait_ge(ex, 2)
                    do(V.tensor_reduce(gs_, pg, AX.X, ALU.add))
                    do(V.reciprocal(gp, gs_))
                    do(V.tensor_reduce(s1, pe_, AX.X, ALU.max))
                    first_of(oh1, pe_, s1)
                    do(V.tensor_tensor(t4, pe_, oh1, ALU.mult))
                    do(V.tensor_tensor(p2, pe_, t4, ALU.subtract))
                    do(V.tensor_tensor(p2, p2, oh1, ALU.subtract))
                    do(V.tensor_reduce(s2, p2, AX.X, ALU.max))
                    first_of(oh2, p2, s2)
                    do(V.tensor_tensor(a1, s1, s2, ALU.add))
                    do(V.reciprocal(a2, a1))
                    do(V.tensor_tensor(gp, gp, a2, ALU.mult))
                    do(V.tensor_tensor(a1, gp, s1, ALU.mult))
                    do(V.tensor_tensor(a2, gp, s2, ALU.mult))
                    do(V.tensor_tensor(oh1, oh1, bc(a1, 2, 4), ALU.mult))
                    do(V.tensor_tensor(oh2, oh2, bc(a2, 2, 4), ALU.mult))
                    do(V.tensor_tensor(oh1, oh1, oh2, ALU.add))
                    do(V.tensor_tensor(comb.rearrange("p t (g e) -> p t g e", g=G), bc(oh1, 2, G), bc(ohg, 3, EG), ALU.mult))

                @block.scalar
                def _(act):
                    act.wait_ge(nm, 1)
                    A.activation(pg, pg, ACT.Exp).then_inc(ex, 1)
                    act.wait_ge(nm, 2)
                    A.activation(pe_, pe_, ACT.Exp).then_inc(ex, 1)

        def experts(i, ht, acc):
            TH = TOK // 2
            o = BIG + NT * D
            w13 = [[at(o + (2 * b + m) * KD * FF, KD, FF) for m in range(2)] for b in range(2)]
            o += 4 * KD * FF
            w2b = [at(o + b * 2 * D, 2, D) for b in range(2)]
            o += 4 * D
            hid = [at(o + b * 2 * TOK, 2, TOK) for b in range(2)]
            o += 4 * TOK
            gate = [at(o + b * TH, TH) for b in range(2)]
            o += 2 * TH
            assert o <= R + 8192, (o, R)
            up_in, dn_in = [sem(f"x{i}_up{b}") for b in range(2)], [sem(f"x{i}_dn{b}") for b in range(2)]
            hid_s, silu_s, h_s, y_s, acc_s = (sem(f"x{i}_{n}") for n in ("hid", "silu", "h", "y", "acc"))
            zeroed = sem(f"x{i}_zero")
            W1 = I["moe_w1"][i].rearrange("e (k p) f -> e p k f", p=P)
            W3 = I["moe_w3"][i].rearrange("e (k p) f -> e p k f", p=P)
            W2 = I["moe_w2"][i].rearrange("e (f p) n -> e p f n", p=P)
            NY = 2 * NT

            def one(ap, e):
                return ap[bass.ds(e, 1)].rearrange("a p k f -> p (a k) f")

            with nc.Block(no_gpsimd_drain=True) as block:
                @block.sync
                def _(sp):
                    for b in range(2):
                        sp.dma_start(w13[b][0], W1[b]).then_inc(up_in[b], 16)
                        sp.dma_start(w13[b][1], W3[b]).then_inc(up_in[b], 16)
                        sp.dma_start(w2b[b], W2[b]).then_inc(dn_in[b], 16)
                    with sp.Fori(1, NE // 2) as pair:
                        e = pair * 2
                        for b in range(2):
                            sp.wait_ge(hid_s, (e + (b - 1)) * 4)
                            sp.dma_start(w13[b][0], one(W1, e + b)).then_inc(up_in[b], 16)
                            sp.dma_start(w13[b][1], one(W3, e + b)).then_inc(up_in[b], 16)
                            sp.wait_ge(y_s, (e + (b - 1)) * NY)
                            sp.dma_start(w2b[b], one(W2, e + b)).then_inc(dn_in[b], 16)

                def body(fn):
                    for b in range(2):
                        fn(b, b, None)

                @block.tensor
                def _(pe):
                    def expert(e, b, first):
                        pe.wait_ge(up_in[b], e * 16 + (32 - 16 * b))
                        for s in range(4):
                            f, th = s // 2, s % 2
                            if not (first and s < 2):
                                pe.wait_ge(h_s, e * 4 + (s - 1))
                            for m in range(2):
                                for k in range(KD):
                                    last = T.matmul(bank(2 * (s % 2) + m)[:, 0:TH], w13[b][m][:, k, f * P:(f + 1) * P],
                                                    ht[:, k, th * TH:(th + 1) * TH], start=(k == 0), stop=(k == KD - 1))
                            last.then_inc(hid_s, 1)
                        if b == 0:
                            pe.wait_ge(dn_in[b], e * 8 + 16)
                        else:
                            pe.wait_ge(dn_in[b], e * 8 + 8)
                        pe.wait_ge(h_s, e * 4 + 4)
                        for g in range(NY):
                            t, j = g // 2, g % 2
                            if not (first and g < 4):
                                pe.wait_ge(acc_s, e * NY + (g - 3))
                            for f in range(2):
                                last = T.matmul(bank(4 + g % 4), hid[b][:, f, t * P:(t + 1) * P],
                                                w2b[b][:, f, j * BANK:(j + 1) * BANK], start=(f == 0), stop=(f == 1))
                            last.then_inc(y_s, 1)

                    expert(0, 0, True)
                    expert(1, 1, False)
                    with pe.Fori(1, NE // 2) as pair:
                        expert(pair * 2, 0, False)
                        expert(pair * 2 + 1, 1, False)

                @block.scalar
                def _(act):
                    def expert(e, b, first):
                        for s in range(4):
                            act.wait_ge(hid_s, e * 4 + (s + 1))
                            if not (first and s < 2):
                                act.wait_ge(h_s, e * 4 + (s - 1))
                            A.activation(gate[s % 2], bank(2 * (s % 2))[:, 0:TH], ACT.Silu).then_inc(silu_s, 1)

                    expert(0, 0, True)
                    expert(1, 1, False)
                    with act.Fori(1, NE // 2) as pair:
                        expert(pair * 2, 0, False)
                        expert(pair * 2 + 1, 1, False)

                @block.vector
                def _(dve):
                    V.memset(acc, 0.0).then_inc(zeroed, 1)
                    dve.wait_ge(zeroed, 1)

                    def expert(e, b, first):
                        for s in range(4):
                            f, th = s // 2, s % 2
                            dve.wait_ge(silu_s, e * 4 + (s + 1))
                            V.tensor_tensor(hid[b][:, f, th * TH:(th + 1) * TH], bank(2 * (s % 2) + 1)[:, 0:TH], gate[s % 2],
                                            ALU.mult).then_inc(h_s, 1)
                        for g in range(NY):
                            t, j = g // 2, g % 2
                            dve.wait_ge(y_s, e * NY + (g + 1))
                            cw = comb[:, t, e:e + 1] if isinstance(e, int) else comb[:, t, bass.ds(e, 1)]
                            V.scalar_tensor_tensor(acc[:, t, j * BANK:(j + 1) * BANK], bank(4 + g % 4), cw,
                                                   acc[:, t, j * BANK:(j + 1) * BANK], ALU.mult, ALU.add).then_inc(acc_s, 1)

                    expert(0, 0, True)
                    expert(1, 1, False)
                    with dve.Fori(1, NE // 2) as pair:
                        expert(pair * 2, 0, False)
                        expert(pair * 2 + 1, 1, False)
                    dve.wait_ge(acc_s, NE * NY)

        def moe_norm(i, acc):
            rows = at(R, 2, D)
            gb = at(R + 2 * D, 2, D)
            diag = at(R + 4 * D, 2, KD, P)
            gate_rows(f"l{i}_g2", 5, rows, diag)
            ln_in = sem(f"l{i}_ln2in")
            norm = Norm(f"l{i}_ln2", gb)
            with nc.Block(no_gpsimd_drain=True) as block:
                @block.sync
                def _(sp):
                    sp.dma_start(gb[:, 0, :], I["ln2_g"][i].partition_broadcast(P)).then_inc(ln_in, 16)
                    sp.dma_start(gb[:, 1, :], I["ln2_b"][i].partition_broadcast(P)).then_inc(ln_in, 16)
                    if i == DEPTH - 1:
                        for t in range(NT):
                            sp.wait_ge(norm.done, t + 1)
                            dst = O["y_prompt"][0] if t == 0 else O["y_sample"][0, (t - 1) * P:t * P, :]
                            store(sp, dst, x[:, t, :])

                @block.scalar
                def _(act):
                    for t in range(NT):
                        norm.scalar(act, t)

                @block.vector
                def _(dve):
                    dve.wait_ge(ln_in, 32)
                    for t in range(NT):
                        dchain.step(V.tensor_tensor(acc[:, t, :], acc[:, t, :], rows[:, min(t, 1), :], ALU.mult))
                        dchain.join(dve)
                        dchain.step(V.scalar_tensor_tensor(x[:, t, :], x[:, t, :], ALPHA, acc[:, t, :], ALU.mult, ALU.add))
                        norm.vector(dve, t, t)

        def moe(i):
            acc = at(BIG, NT, D)
            ht = at(R + 8192, KD, TOK)
            modulated(f"l{i}_h2", ht, 3, 4)
            router(i, ht)
            experts(i, ht, acc)
            moe_norm(i, acc)

        setup()
        modulation(0)
        ht = at(R, KD, TOK)
        modulated("l0_h1", ht, 0, 1)
        project("ev", I["ev_w_in"][0], EV_IN, ht, proj, R + KD * TOK)
        retention()
        latent_attention()
        mix_out("ev_out", 0, I["ev_w_out"][0],
                [proj[:, :, RG + k * P:RG + (k + 1) * P] for k in range(RH * RDV // P)]
                + [proj[:, :, MQ + k * P:MQ + (k + 1) * P] for k in range(MH * MDV // P)])
        moe(0)
        recycle_sems()
        modulation(1)
        modulated("l1_h1", ht, 0, 1)
        pj = at(BIG, NT, OD_IN)
        project("od", I["od_w_in"][0], OD_IN, ht, pj, R + KD * TOK)
        differential_attention(pj)
        mix_out("od_out", 1, I["od_w_out"][0], [pj[:, :, k * P:(k + 1) * P] for k in range(KD)])
        moe(1)
        with nc.Block(no_gpsimd_drain=True) as block:
            @block.sync
            def _(sp):
                sp.wait_ge(stored, stores[0])


INPUTS = ["x_prompt", "x_sample", "state_ret_fwd", "state_ret_bwd", "cache_mla_ckv", "cache_mla_krope",
          "cache_diff_k", "cache_diff_v", "c", "c_ctx", "ada_w", "ada_b", "ln1_g", "ln1_b", "ln2_g", "ln2_b",
          "ev_w_in", "ev_w_out", "ret_decay_fwd", "ret_decay_bwd", "mla_kv_norm_g", "mla_w_uk", "mla_w_uv",
          "od_w_in", "od_w_out", "diff_lambda", "diff_norm_g", "moe_w_group", "moe_b_group", "moe_w_expert",
          "moe_b_expert", "moe_w1", "moe_w3", "moe_w2"]
OUTPUTS = [("y_prompt", (1, SEQ, D)), ("y_sample", (1, LAT, D)),
           ("new_state_ret_fwd", (1, 1, RH, RDK, RDV)), ("new_state_ret_bwd", (1, 1, RH, RDK, RDV)),
           ("new_cache_mla_ckv", (1, 1, SEQ, MKV)), ("new_cache_mla_krope", (1, 1, SEQ, MR)),
           ("new_cache_diff_k", (1, 1, DH, SEQ, DDV)), ("new_cache_diff_v", (1, 1, DH, SEQ, DDV))]


def kernel(**inputs):
    import concourse.bacc as bacc
    from concourse.bass_utils import run_bass_kernel_spmd

    nc = bacc.Bacc("TRN2", target_bir_lowering=False, num_devices=1)
    arrays = {f"in_{n}": np.ascontiguousarray(inputs[n]) for n in INPUTS}
    consts, rope_mla, rope_diff = constants()
    arrays.update({"in_consts": consts, "in_rope_mla": rope_mla, "in_rope_diff": rope_diff})
    I = {n[3:]: nc.dram_tensor(n, a.shape, F32, kind="ExternalInput").ap() for n, a in arrays.items()}
    O = {n: nc.dram_tensor(f"out_{n}", s, F32, kind="ExternalOutput").ap() for n, s in OUTPUTS}
    build(nc, I, O)
    r = run_bass_kernel_spmd(nc, [arrays], core_ids=[0])
    return tuple(r.results[0][f"out_{n}"] for n, _ in OUTPUTS)
```

```python
import math
from contextlib import ExitStack

import numpy as np
import concourse.bass as bass
from concourse import mybir

F32 = mybir.dt.float32
I32 = mybir.dt.int32
ALU = mybir.AluOpType
ACT = mybir.ActivationFunctionType
AX = mybir.AxisListType

P = 128
D = 1024
KD = D // P
SEQ, LAT, PAST = 128, 512, 128
NT = (SEQ + LAT) // P
TOK = NT * P
NK = NT + 1
KEYS = PAST + LAT
DEPTH = 2
GRID_W = 64
LN_EPS, RMS_EPS = 1e-5, 1e-6
ALPHA = (2.0 * DEPTH) ** 0.25
RH, RDK, RDV, RC = 8, 64, 128, 128
MH, MN, MR, MDV, MKV = 8, 64, 32, 64, 256
MQD = MN + MR
DH, DDH = 8, 64
DDV = 2 * DDH
G, EG = 4, 4
NE = G * EG
FF = 256
EV_W = (RH * RDK, RH * RDK, RH * RDV, RH * RDV, MH * MQD, MKV, MR)
EV_AT = [sum(EV_W[:n]) for n in range(len(EV_W))]
EV_IN = sum(EV_W)
EV_OUT = RH * RDV + MH * MDV
RQ, RK, RV, RG, MQ, CKV, KR = EV_AT
OD_IN = 3 * D
LAM_INIT = 0.8 - 0.6 * math.exp(-0.3)
NMOD = 6 * KD
BANK = 512
ADA_CW = 512
ADA_CH = 6 * D // ADA_CW
FURTHER = 2 * NT
CHUNKS = NE + FURTHER
RET_SCALE = RDK ** -0.5
MLA_SCALE = MQD ** -0.5
DIFF_SCALE = DDH ** -0.5

C_ID, C_ONE, C_REL, C_MASK, C_TRI, C_POS, C_TIE, C_EPS, C_TOK, C_SLOT = 0, 128, 256, 512, 768, 896, 900, 904, 906, 911
C_N = 928


def constants():
    i = np.arange(P, dtype=np.float32)
    c = np.zeros((P, C_N), np.float32)
    c[:, C_ID:C_ID + P] = np.eye(P)
    c[:, C_ONE:C_ONE + P] = 1.0
    rel = i[None, :] - i[:, None]
    c[:, C_REL:C_REL + P] = np.maximum(rel, 0)
    c[:, C_REL + P:C_REL + 2 * P] = np.maximum(-rel, 0)
    c[:, C_MASK:C_MASK + P] = (rel >= 0) * RET_SCALE
    c[:, C_MASK + P:C_MASK + 2 * P] = (rel <= 0) * RET_SCALE
    for n, pos in enumerate((i + 1, RC - i, RC - 1 - i, i)):
        c[:, C_POS + n] = pos
    c[:, C_TIE:C_TIE + 4] = np.arange(4, 0, -1)
    c[:, C_EPS], c[:, C_EPS + 1] = LN_EPS, RMS_EPS
    c[:, C_TRI:C_TRI + P] = rel > 0
    c[:, C_TOK:C_TOK + NT] = i[:, None] + P * np.arange(NT)
    c[:, C_SLOT:C_SLOT + NE] = P * np.arange(NE)

    def rope(dim):
        row = np.repeat(np.arange(LAT // GRID_W, dtype=np.float32), GRID_W)
        col = np.tile(np.arange(GRID_W, dtype=np.float32), LAT // GRID_W)
        nf = dim // 4
        inv = np.float32(10000.0) ** (-np.arange(nf, dtype=np.float32) / np.float32(nf))
        ang = np.concatenate([row[:, None] * inv, col[:, None] * inv], -1).astype(np.float32)
        return np.stack([np.cos(ang), np.sin(ang)]).astype(np.float32)

    return c, rope(MR), rope(DDH)


class Chain:

    def __init__(self, sem):
        self.sem, self.n = sem, 0

    def step(self, ins):
        self.n += 1
        ins.then_inc(self.sem, 1)
        return ins

    def join(self, eng):
        eng.wait_ge(self.sem, self.n)


def bc(ap, dim, n):
    a = ap.unsqueeze(dim)
    shape = list(a.shape)
    shape[dim] = n
    return a.to_broadcast(shape)


def build(nc, I, O):
    ctx = ExitStack()
    with ctx:
        arena = ctx.enter_context(nc.sbuf_tensor("arena", [P, 53200], F32))
        psum = ctx.enter_context(nc.psum_tensor("psum", [P, 8 * BANK], F32))

        def lasting_sem(name):
            return ctx.enter_context(nc.semaphore(name))

        stage_sems = []

        def sem(name):
            stage_sems.append(nc.alloc_semaphore(name=name))
            return stage_sems[-1]

        def recycle_sems():
            with nc.Block(no_gpsimd_drain=True) as block:
                @block.gpsimd
                def _(pool):
                    nc.clear_and_free_semaphores(stage_sems)
            stage_sems.clear()

        def at(off, *dims):
            n = int(np.prod(dims))
            v = arena[:, off:off + n]
            if len(dims) == 1:
                return v
            names = "abcd"[:len(dims)]
            return v.rearrange(f"p ({' '.join(names)}) -> p {' '.join(names)}",
                               **{names[i]: dims[i] for i in range(1, len(dims))})

        def bank(b, n=1):
            return psum[:, b * BANK:(b + n) * BANK]

        off = [0]

        def keep(*dims):
            o = off[0]
            off[0] += int(np.prod(dims))
            return at(o, *dims)

        x = keep(NT, D)
        const = keep(C_N)
        modc = keep(DEPTH, NMOD, 2)
        adab = keep(2, NMOD)
        cond = keep(KD, 32)
        kvg = keep(MKV)
        dng = keep(DDV)
        br = keep(DEPTH, G + NE)
        gates = keep(2, NT)
        slot_i = keep(2, NT).bitcast(I32)
        tables = keep(3, NE).bitcast(I32)
        tok_i = keep(CHUNKS).bitcast(I32)
        lam = keep(4)
        small = keep(256)
        BIG = off[0]
        proj = at(BIG, NT, EV_IN)
        R = BIG + NT * EV_IN
        assert R + 24100 <= 53200, R
        ident = const[:, C_ID:C_ID + P]
        ones = const[:, C_ONE:C_ONE + P]
        mod_rows = nc.dram_tensor("mod_rows", (DEPTH, 2 * NMOD, P), F32).ap()
        h2_rows = nc.dram_tensor("h2_rows", (TOK, D), F32).ap()
        slot_tok = nc.dram_tensor("slot_tok", (CHUNKS * P, 1), F32).ap()
        y_rows = nc.dram_tensor("y_rows", (CHUNKS * P, D), F32).ap()
        eps_ln, eps_rms = const[:, C_EPS:C_EPS + 1], const[:, C_EPS + 1:C_EPS + 2]

        dchain, achain, pchain = Chain(lasting_sem("vector_step")), Chain(lasting_sem("scalar_step")), Chain(lasting_sem("pool_step"))
        stored = lasting_sem("stored")
        stores = [0]

        def store(eng, out, in_):
            eng.dma_start(out, in_).then_inc(stored, 16)
            stores[0] += 16

        V, A, T = nc.vector, nc.scalar, nc.tensor

        further_zero = lasting_sem("further_chunks_zero")

        def setup():
            loaded, rows_in = sem("inputs_loaded"), sem("rows_loaded")
            rows_t, cond_done, zeroed = sem("rows_transposed"), sem("cond_done"), sem("zeroed")
            nil = at(R + 22528, D)
            crow = at(BIG, P)
            brow = at(BIG + P, 2, P)
            with nc.Block(no_gpsimd_drain=True) as block:
                @block.sync
                def _(sp):
                    sp.dma_start(const, I["consts"]).then_inc(rows_in, 16)
                    sp.dma_start(crow[0:KD, :], I["c_ctx"].rearrange("(k p) -> k p", p=P)).then_inc(rows_in, 16)
                    sp.dma_start(crow[KD:2 * KD, :], I["c"].rearrange("a (k p) -> (a k) p", p=P)).then_inc(rows_in, 16)
                    sp.dma_start(brow[0:NMOD, :, :], I["ada_b"].rearrange("i (k p) -> k i p", p=P)).then_inc(rows_in, 16)
                    sp.dma_start(x[:, 0, :], I["x_prompt"].rearrange("a p d -> p (a d)")).then_inc(loaded, 16)
                    sp.dma_start(x[:, 1:NT, :], I["x_sample"].rearrange("a (t p) d -> p (a t) d", p=P)).then_inc(loaded, 16)
                    sp.dma_start(kvg, I["mla_kv_norm_g"][0].partition_broadcast(P)).then_inc(loaded, 16)
                    sp.dma_start(dng, I["diff_norm_g"][0].partition_broadcast(P)).then_inc(loaded, 16)
                    for i in range(DEPTH):
                        sp.dma_start(br[:, i, 0:G], I["moe_b_group"][i].partition_broadcast(P)).then_inc(loaded, 16)
                        sp.dma_start(br[:, i, G:], I["moe_b_expert"][i].partition_broadcast(P)).then_inc(loaded, 16)
                    sp.wait_ge(zeroed, 2)
                    sp.dma_start(slot_tok.rearrange("(a b) o -> a (b o)", b=P), nil[0:CHUNKS, 0:P]).then_inc(loaded, 16)
                    sp.dma_start(y_rows.rearrange("(c p) n -> p c n", p=P)[:, NE:], bc(nil, 1, FURTHER)).then_inc(further_zero, 16)
                    sp.wait_ge(loaded, 16 * (5 + 2 * DEPTH))

                @block.vector
                def _(dve):
                    V.memset(nil, 0.0).then_inc(zeroed, 1)
                    V.memset(cond, 0.0).then_inc(zeroed, 1)

                @block.tensor
                def _(pe):
                    pe.wait_ge(rows_in, 64)
                    T.transpose(bank(0)[:, 0:2 * KD], crow[0:2 * KD, :], ident[0:2 * KD, 0:2 * KD])
                    for i in range(DEPTH):
                        T.transpose(bank(0)[:, 64 + i * 64:64 + i * 64 + NMOD], brow[0:NMOD, i, :],
                                    ident[0:NMOD, 0:NMOD]).then_inc(rows_t, 1)

                @block.scalar
                def _(act):
                    act.wait_ge(rows_t, DEPTH)
                    act.wait_ge(zeroed, 2)
                    A.activation(cond[:, :, 0:2].rearrange("p k c -> p c k"), bank(0)[:, 0:2 * KD].rearrange("p (c k) -> p c k", c=2),
                                 ACT.Silu).then_inc(cond_done, 1)
                    for i in range(DEPTH):
                        A.activation(adab[:, i, :], bank(0)[:, 64 + i * 64:64 + i * 64 + NMOD], ACT.Copy)
                    act.drain()

        def modulated(name, i, ht, sh, sc):
            tr, ev_a, ev_d = sem(f"{name}_tr"), sem(f"{name}_eva"), sem(f"{name}_evd")
            with nc.Block(no_gpsimd_drain=True) as block:
                @block.tensor
                def _(pe):
                    for k in range(KD):
                        if k >= 4:
                            pe.wait_ge((ev_a, ev_d)[k % 2], (k - 4) // 2 + 1)
                        for t in range(NT):
                            last = T.transpose(bank(2 * (k % 4), 2)[:, t * P:(t + 1) * P], x[:, t, k * P:(k + 1) * P], ident)
                        last.then_inc(tr, 1)

                @block.scalar
                def _(act):
                    for k in range(0, KD, 2):
                        act.wait_ge(tr, k + 1)
                        src = bank(2 * (k % 4), 2)
                        A.activation(ht[:, k, 0:P], src[:, 0:P], ACT.Identity,
                                     bias=modc[:, i, sh * KD + k, 0:1], scale=modc[:, i, sc * KD + k, 0:1])
                        A.activation(ht[:, k, P:TOK], src[:, P:TOK], ACT.Identity,
                                     bias=modc[:, i, sh * KD + k, 1:2], scale=modc[:, i, sc * KD + k, 1:2]).then_inc(ev_a, 1)

                @block.vector
                def _(dve):
                    for k in range(1, KD, 2):
                        dve.wait_ge(tr, k + 1)
                        src = bank(2 * (k % 4), 2)
                        V.tensor_scalar(ht[:, k, 0:P], src[:, 0:P], modc[:, i, sc * KD + k, 0:1],
                                        modc[:, i, sh * KD + k, 0:1], ALU.mult, ALU.add)
                        V.tensor_scalar(ht[:, k, P:TOK], src[:, P:TOK], modc[:, i, sc * KD + k, 1:2],
                                        modc[:, i, sh * KD + k, 1:2], ALU.mult, ALU.add).then_inc(ev_d, 1)
                    dve.drain()

        def stream(name, jobs, ht, dst, wb):
            NB = 4
            chunk_in = [sem(f"{name}_in{b}") for b in range(NB)]
            used_w, used_a, group, ev_a, ev_d = (sem(f"{name}_{n}") for n in ("usedw", "useda", "group", "eva", "evd"))
            copied, turned, added = (sem(f"{name}_{n}") for n in ("acopied", "aturned", "aadded"))
            wbuf = [at(wb + b * KD * ADA_CW, KD, ADA_CW) for b in range(NB)]
            part = at(wb + NB * KD * ADA_CW, 2, ADA_CW)
            W_BANKS = 6
            sums, turns = bank(6), bank(7)
            upto = [(sum(j[0] == "w" for j in jobs[:n + 1]), sum(j[0] == "ada" for j in jobs[:n + 1])) for n in range(len(jobs))]

            def chunk_used(eng, n):
                kind = jobs[n][0]
                if kind == "w":
                    eng.wait_ge(group, NT * upto[n][0])
                else:
                    eng.wait_ge(used_a, upto[n][1])

            def groups(first):
                def of(n):
                    g0 = NT * (upto[n][0] - 1)
                    return [g for g in range(g0, g0 + NT) if g % 2 == first]
                return of

            with nc.Block(no_gpsimd_drain=True) as block:
                @block.sync
                def _(sp):
                    for n, job in enumerate(jobs):
                        if n >= NB:
                            chunk_used(sp, n - NB)
                        if job[0] == "w":
                            _, w, n0, cw = job
                            src = w.rearrange("(k p) n -> p k n", p=P)[:, :, n0:n0 + cw]
                        else:
                            _, i, c = job
                            cw = ADA_CW
                            src = I["ada_w"][i].rearrange("(k p) n -> p k n", p=P)[:, :, c * cw:(c + 1) * cw]
                        sp.dma_start(wbuf[n % NB][:, :, 0:cw], src).then_inc(chunk_in[n % NB], 16)

                @block.tensor
                def _(pe):
                    def turn(n):
                        a = upto[n][1] - 1
                        pe.wait_ge(copied, a + 1)
                        if a:
                            pe.wait_ge(added, a)
                        for q in range(4):
                            last = T.transpose(turns[:, q * P:(q + 1) * P], part[:, a % 2, q * P:(q + 1) * P], ident)
                        last.then_inc(turned, 1)

                    for n, job in enumerate(jobs):
                        pe.wait_ge(chunk_in[n % NB], 16 * (n // NB + 1))
                        if job[0] == "w":
                            cw = job[3]
                            for t in range(NT):
                                g = NT * (upto[n][0] - 1) + t
                                if g >= W_BANKS:
                                    pe.wait_ge((ev_a, ev_d)[g % 2], (g - W_BANKS) // 2 + 1)
                                for k in range(KD):
                                    last = T.matmul(bank(g % W_BANKS)[:, 0:cw], ht[:, k, t * P:(t + 1) * P],
                                                    wbuf[n % NB][:, k, 0:cw], start=(k == 0), stop=(k == KD - 1))
                                last.then_inc(group, 1)
                        else:
                            a = upto[n][1] - 1
                            if a:
                                pe.wait_ge(copied, a)
                            for k in range(KD):
                                q = 32 * (k % 4)
                                last = T.matmul(sums[q:q + 32, :], cond[:, k, :], wbuf[n % NB][:, k, :],
                                                start=(k < 4), stop=(k >= 4))
                            last.then_inc(used_a, 1)
                        if n and jobs[n - 1][0] == "ada":
                            turn(n - 1)
                    if jobs[-1][0] == "ada":
                        turn(len(jobs) - 1)

                @block.scalar
                def _(act):
                    mine = groups(0)
                    for n, job in enumerate(jobs):
                        if job[0] == "w":
                            _, w, n0, cw = job
                            for g in mine(n):
                                act.wait_ge(group, g + 1)
                                A.copy(dst[:, g % NT, n0:n0 + cw], bank(g % W_BANKS)[:, 0:cw]).then_inc(ev_a, 1)
                        else:
                            a = upto[n][1] - 1
                            act.wait_ge(used_a, a + 1)
                            if a >= 2:
                                act.wait_ge(turned, a - 1)
                            A.copy(part[:, a % 2, :], sums).then_inc(copied, 1)
                    act.drain()

                @block.vector
                def _(dve):
                    mine = groups(1)

                    def add(n):
                        _, i, c = jobs[n]
                        dve.wait_ge(turned, upto[n][1])
                        V.tensor_reduce(modc[:, i, 4 * c:4 * c + 4, :],
                                        turns.rearrange("p (q j m) -> p q m j", q=4, j=4)[:, :, 0:2, :],
                                        AX.X, ALU.add).then_inc(added, 1)

                    for n, job in enumerate(jobs):
                        if job[0] == "w":
                            _, w, n0, cw = job
                            for g in mine(n):
                                dve.wait_ge(group, g + 1)
                                V.tensor_copy(dst[:, g % NT, n0:n0 + cw], bank(g % W_BANKS)[:, 0:cw]).then_inc(ev_d, 1)
                        if n and jobs[n - 1][0] == "ada":
                            add(n - 1)
                    if jobs[-1][0] == "ada":
                        add(len(jobs) - 1)
                    dve.drain()

        def w_jobs(w, width):
            return [("w", w, c, min(BANK, width - c)) for c in range(0, width, BANK)]

        def finish_modulation(name, spans, rows_of):
            biased, turned, copied, out_in = (sem(f"{name}_{n}") for n in ("biased", "turned", "copied", "out"))
            rowbuf = at(R, DEPTH, P)
            with nc.Block(no_gpsimd_drain=True) as block:
                @block.vector
                def _(dve):
                    for i, a, b in spans:
                        dchain.step(V.tensor_tensor(modc[:, i, a:b, :], modc[:, i, a:b, :], bc(adab[:, i, a:b], 2, 2), ALU.add))
                    dchain.join(dve)
                    for i, a, b in spans:
                        for s in (1, 4):
                            if a <= s * KD < b:
                                m = modc[:, i, s * KD:(s + 1) * KD, :]
                                dchain.step(V.tensor_scalar(m, m, 1.0, None, ALU.add))
                    dchain.join(dve)
                    dve.drain().then_inc(biased, 1)

                if rows_of:
                    @block.tensor
                    def _(pe):
                        pe.wait_ge(biased, 1)
                        for i in rows_of:
                            T.transpose(bank(i)[0:2 * NMOD, 0:P], modc[:, i].rearrange("p n c -> p (n c)"), ident).then_inc(turned, 1)

                    @block.scalar
                    def _(act):
                        for n, i in enumerate(rows_of):
                            act.wait_ge(turned, n + 1)
                            A.copy(rowbuf[0:2 * NMOD, i, :], bank(i)[0:2 * NMOD, 0:P]).then_inc(copied, 1)

                    @block.sync
                    def _(sp):
                        for n, i in enumerate(rows_of):
                            sp.wait_ge(copied, n + 1)
                            sp.dma_start(mod_rows[i], rowbuf[0:2 * NMOD, i, :]).then_inc(out_in, 16)
                        sp.wait_ge(further_zero, 16)
                        sp.wait_ge(out_in, 16 * len(rows_of))

        def mod_row(i, v, c):
            return mod_rows[i].rearrange("(v k c) m -> v c k m", v=6, c=2)[v, c].partition_broadcast(P)

        class Norm:

            def __init__(self, name, gb):
                self.var, self.root, self.flat = sem(f"{name}_var"), sem(f"{name}_root"), sem(f"{name}_flat")
                self.g, self.b = gb[:, 0, :], gb[:, 1, :]
                self.stats, self.mv, self.rt = small[:, 0:12], small[:, 16:18], small[:, 20:22]

            def vector(self, dve, t):
                dchain.join(dve)
                for h in range(2):
                    dchain.step(V.bn_stats(self.stats[:, 6 * h:6 * h + 6], x[:, t, h * BANK:(h + 1) * BANK]))
                dchain.join(dve)
                V.bn_aggr(self.mv, self.stats).then_inc(self.var, 1)
                dve.wait_ge(self.root, t + 1)
                dchain.step(V.reciprocal(self.rt[:, 1:2], self.rt[:, 0:1]))
                dchain.join(dve)
                V.tensor_scalar(x[:, t, :], x[:, t, :], self.mv[:, 0:1], self.rt[:, 1:2], ALU.subtract, ALU.mult).then_inc(self.flat, 1)

            def scalar(self, act, t):
                act.wait_ge(self.var, t + 1)
                A.activation(self.rt[:, 0:1], self.mv[:, 1:2], ACT.Sqrt, bias=eps_ln).then_inc(self.root, 1)

            def late(self, eng, math, chain, t):
                eng.wait_ge(self.flat, t + 1)
                chain.step(math.tensor_tensor(x[:, t, :], x[:, t, :], self.g, ALU.mult))
                chain.join(eng)
                return math.tensor_tensor(x[:, t, :], x[:, t, :], self.b, ALU.add)

        WOUT, HT2 = R + KD * TOK, R + 19968
        EXP_A = BIG + NT * EV_IN - 6144 - 160
        W_EXP = 2 * KD * FF + 2 * D

        def expert_weights(o):
            return [at(o + m * KD * FF, KD, FF) for m in range(2)], at(o + 2 * KD * FF, 2, D)

        WEIGHTS = [expert_weights(EXP_A), expert_weights(R)]

        def mix_out(name, i, w, srcs, direct):
            ks, kt = len(srcs), len(srcs) + len(direct)
            catT = at(R, ks, TOK)
            feats = [catT[:, k, :] for k in range(ks)] + direct
            wout = at(WOUT, kt, D)
            w_in = [sem(f"{name}_win{j}") for j in range(2)]
            tr, ev_a, ev_d = (sem(f"{name}_{n}") for n in ("tr", "eva", "evd"))
            wv = w.rearrange("(k p) n -> p k n", p=P)
            with nc.Block(no_gpsimd_drain=True) as block:
                @block.sync
                def _(sp):
                    for j in range(2):
                        sp.dma_start(wout[:, :, j * BANK:(j + 1) * BANK], wv[:, :, j * BANK:(j + 1) * BANK]).then_inc(w_in[j], 16)

                @block.tensor
                def _(pe):
                    for k in range(ks):
                        if k >= 4:
                            pe.wait_ge((ev_a, ev_d)[k % 2], (k - 4) // 2 + 1)
                        for t in range(NT):
                            last = T.transpose(bank(2 * (k % 4), 2)[:, t * P:(t + 1) * P], srcs[k][:, t, :], ident)
                        last.then_inc(tr, 1)

                @block.scalar
                def _(act):
                    for k in range(0, ks, 2):
                        act.wait_ge(tr, k + 1)
                        A.copy(catT[:, k, :], bank(2 * (k % 4), 2)[:, 0:TOK]).then_inc(ev_a, 1)
                    act.drain()

                @block.vector
                def _(dve):
                    for k in range(1, ks, 2):
                        dve.wait_ge(tr, k + 1)
                        V.tensor_copy(catT[:, k, :], bank(2 * (k % 4), 2)[:, 0:TOK]).then_inc(ev_d, 1)
                    dve.drain()

            g1, sc2, sh2, gb, h2 = (at(BIG + 2 * D * n, 2, D) for n in range(5))
            wrt = at(BIG + 10 * D, KD, P)
            tmp = at(BIG + 11 * D, 2, BANK)
            htt = at(HT2, 2, KD, P)
            half, gated, h2_done, h2_last, stored_h2 = (sem(f"{name}_{n}") for n in ("half", "gated", "h2", "h2last", "h2st"))
            g1_in, ln_in, mod_in, wr_zero, wr_in = (sem(f"{name}_{n}") for n in ("g1in", "lnin", "modin", "wrz", "wrin"))
            turned, t_copied, logit = (sem(f"{name}_{n}") for n in ("turned", "tcopied", "logit"))
            norm = Norm(f"{name}_ln", gb)
            E13, E2 = WEIGHTS[0]

            def h2_ready(eng, t):
                if t < NT - 1:
                    eng.wait_ge(h2_done, t + 1)
                else:
                    eng.wait_ge(h2_last, 1)

            with nc.Block(no_gpsimd_drain=True) as block:
                @block.sync
                def _(sp):
                    for c in range(2):
                        sp.dma_start(g1[:, c, :].rearrange("p (k m) -> p k m", k=KD), mod_row(i, 2, c)).then_inc(g1_in, 16)
                    sp.dma_start(gb[:, 0, :], I["ln1_g"][i].partition_broadcast(P)).then_inc(ln_in, 16)
                    sp.dma_start(gb[:, 1, :], I["ln1_b"][i].partition_broadcast(P)).then_inc(ln_in, 16)
                    for c in range(2):
                        sp.dma_start(sh2[:, c, :].rearrange("p (k m) -> p k m", k=KD), mod_row(i, 3, c)).then_inc(mod_in, 16)
                        sp.dma_start(sc2[:, c, :].rearrange("p (k m) -> p k m", k=KD), mod_row(i, 4, c)).then_inc(mod_in, 16)
                    sp.wait_ge(wr_zero, 1)
                    sp.dma_start(wrt[:, :, 0:G], I["moe_w_group"][i].rearrange("(k p) n -> p k n", p=P)).then_inc(wr_in, 16)
                    sp.dma_start(wrt[:, :, G:G + NE], I["moe_w_expert"][i].rearrange("(k p) n -> p k n", p=P)).then_inc(wr_in, 16)
                    sp.dma_start(E13[0], I["moe_w1"][i, 0].rearrange("(k p) f -> p k f", p=P)).then_inc(up_in[0], 16)
                    sp.dma_start(E13[1], I["moe_w3"][i, 0].rearrange("(k p) f -> p k f", p=P)).then_inc(up_in[0], 16)
                    sp.dma_start(E2, I["moe_w2"][i, 0].rearrange("(f p) n -> p f n", p=P)).then_inc(dn_in[0], 16)
                    for t in range(NT):
                        h2_ready(sp, t)
                        sp.dma_start(h2_rows[t * P:(t + 1) * P, :], h2[:, t % 2, :]).then_inc(stored_h2, 16)
                        sp.wait_ge(stored_h2, 16 * (t + 1))

                @block.tensor
                def _(pe):
                    for j in range(2):
                        pe.wait_ge(w_in[j], 16)

                    def heads(t):
                        for j in range(2):
                            g = 2 * t + j
                            if g >= 4:
                                pe.wait_ge(gated, g - 3)
                            for k in range(kt):
                                last = T.matmul(bank(g % 4), feats[k][:, t * P:(t + 1) * P],
                                                wout[:, k, j * BANK:(j + 1) * BANK], start=(k == 0), stop=(k == kt - 1))
                            last.then_inc(half, 1)

                    def turn(t):
                        h2_ready(pe, t)
                        if t:
                            pe.wait_ge(t_copied, t)
                        for k in range(KD):
                            last = T.transpose(bank(4, 2)[:, k * P:(k + 1) * P], h2[:, t % 2, k * P:(k + 1) * P], ident)
                        last.then_inc(turned, 1)

                    def route(t):
                        pe.wait_ge(t_copied, t + 1)
                        if t == 0:
                            pe.wait_ge(wr_in, 32)
                        for k in range(KD):
                            last = T.matmul(bank(6, 2)[:, t * P:(t + 1) * P], htt[:, t % 2, k, :], wrt[:, k, :],
                                            start=(k == 0), stop=(k == KD - 1))
                        last.then_inc(logit, 1)

                    for t in range(NT + 2):
                        if t < NT:
                            heads(t)
                        if 1 <= t <= NT:
                            turn(t - 1)
                        if t >= 2:
                            route(t - 2)

                @block.scalar
                def _(act):
                    def copy(t):
                        act.wait_ge(turned, t + 1)
                        if t >= 2:
                            act.wait_ge(logit, t - 1)
                        A.copy(htt[:, t % 2], bank(4, 2).rearrange("p (k n) -> p k n", k=KD)).then_inc(t_copied, 1)

                    for t in range(NT + 1):
                        if t < NT:
                            norm.scalar(act, t)
                        if t:
                            copy(t - 1)

                def modulate(eng, math, chain, t):
                    c = min(t, 1)
                    chain.step(norm.late(eng, math, chain, t))
                    chain.join(eng)
                    if t == 0 or t == NT - 1:
                        eng.wait_ge(mod_in, 64)
                    if t >= 2:
                        eng.wait_ge(stored_h2, 16 * (t - 1))
                        eng.wait_ge(turned, t - 1)
                    chain.step(math.tensor_tensor(h2[:, t % 2, :], x[:, t, :], sc2[:, c, :], ALU.mult))
                    chain.join(eng)
                    math.tensor_tensor(h2[:, t % 2, :], h2[:, t % 2, :], sh2[:, c, :], ALU.add).then_inc(
                        h2_done if t < NT - 1 else h2_last, 1)

                @block.gpsimd
                def _(pool):
                    nc.gpsimd.memset(wrt, 0.0).then_inc(wr_zero, 1)
                    pool.wait_ge(ln_in, 32)
                    for t in range(NT - 1):
                        modulate(pool, nc.gpsimd, pchain, t)

                @block.vector
                def _(dve):
                    dve.wait_ge(g1_in, 32)
                    for t in range(NT):
                        for j in range(2):
                            g = 2 * t + j
                            dve.wait_ge(half, g + 1)
                            V.tensor_tensor(tmp[:, j, :], bank(g % 4), g1[:, min(t, 1), j * BANK:(j + 1) * BANK],
                                            ALU.mult).then_inc(gated, 1)
                            dve.wait_ge(gated, g + 1)
                            dchain.step(V.scalar_tensor_tensor(x[:, t, j * BANK:(j + 1) * BANK], x[:, t, j * BANK:(j + 1) * BANK],
                                                               ALPHA, tmp[:, j, :], ALU.mult, ALU.add))
                        norm.vector(dve, t)
                    dve.wait_ge(ln_in, 32)
                    modulate(dve, V, dchain, NT - 1)

        def retention():
            o = R
            dt = at(o, RH, P); o += RH * P
            tab = at(o, 2, 2, RH); o += 4 * RH
            lg = at(o, 2, RH); o += 2 * RH
            cd = at(o, RH); o += RH
            tl = at(o, 8, 2 * RH); o += 16 * RH
            st = at(o, NT - 1, RH, RDV); o += (NT - 1) * RH * RDV
            kv = at(o, NT, RH, RDV); o += NT * RH * RDV
            qq = at(o, NT - 1, RH, 2, RDK); o += (NT - 1) * RH * 2 * RDK
            SH = o
            kk = at(o, NT, RH, 2, RDK); o += NT * RH * 2 * RDK
            ex = at(o, 2, RH, P); o += 2 * RH * P
            assert o <= 53200, o
            qv = proj[:, :, RQ:RQ + RH * RDK].rearrange("p t (h d) -> p t h d", h=RH)
            kvw = proj[:, :, RK:RK + RH * RDK].rearrange("p t (h d) -> p t h d", h=RH)
            dec_in, st_in = sem("dec_in"), sem("state_in")
            dv, ac = sem("decay_v"), sem("decay_a")
            kk_done, kv_done, kv_out = sem("kk_done"), sem("kv_done"), sem("kv_copied")
            with nc.Block(no_gpsimd_drain=True) as block:
                @block.sync
                def _(sp):
                    sp.dma_start(tl[:, 0, 0:RH], I["ret_decay_fwd"][0].partition_broadcast(P)).then_inc(dec_in, 16)
                    sp.dma_start(tl[:, 0, RH:2 * RH], I["ret_decay_bwd"][0].partition_broadcast(P)).then_inc(dec_in, 16)
                    sp.dma_start(st[0:RDK, 0], I["state_ret_fwd"][0, 0].rearrange("h k v -> k h v")).then_inc(st_in, 16)
                    sp.dma_start(st[RDK:P, NT - 2], I["state_ret_bwd"][0, 0].rearrange("h k v -> k h v")).then_inc(st_in, 16)
                    sp.wait_ge(kv_out, 1)
                    store(sp, O["new_state_ret_fwd"][0, 0].rearrange("h k v -> k h v"), kv[0:RDK, 0])
                    store(sp, O["new_state_ret_bwd"][0, 0].rearrange("h k v -> k h v"), kv[RDK:P, 0])

                @block.vector
                def _(dve):
                    X, AXX, E, U, Dd, Rr, L, Mn = (tl[:, n, :] for n in range(8))
                    lgf = lg.rearrange("p a h -> p (a h)")
                    dve.wait_ge(dec_in, 32)
                    V.scalar_tensor_tensor(AXX, X, -1.0, X, ALU.mult, ALU.max).then_inc(dv, 1)
                    dve.wait_ge(ac, 1)
                    V.tensor_scalar(U, E, 1.0, None, ALU.add).then_inc(dv, 1)
                    dve.wait_ge(dv, 2)
                    dchain.step(V.tensor_scalar(Dd, U, 1.0, None, ALU.subtract))
                    dchain.step(V.tensor_scalar(Mn, X, 0.0, None, ALU.min))
                    dchain.join(dve)
                    dchain.step(V.tensor_tensor(Rr, E, Dd, ALU.subtract))
                    dchain.step(V.reciprocal(AXX, U))
                    dchain.join(dve)
                    dchain.step(V.tensor_tensor(Rr, Rr, AXX, ALU.mult))
                    dchain.join(dve)
                    dve.wait_ge(ac, 2)
                    dchain.step(V.tensor_tensor(L, L, Rr, ALU.add))
                    dchain.join(dve)
                    dchain.step(V.tensor_tensor(lgf, Mn, L, ALU.subtract))
                    dchain.join(dve)
                    for qk in range(2):
                        for d in range(2):
                            n = C_POS + 2 * qk + d
                            dchain.step(V.tensor_scalar(tab[:, qk, d, :], lg[:, d, :], const[:, n:n + 1], None, ALU.mult))
                    dchain.step(V.tensor_scalar(cd[0:RDK, :], lg[0:RDK, 0, :], float(RC), None, ALU.mult))
                    V.tensor_scalar(cd[RDK:P, :], lg[RDK:P, 1, :], float(RC), None, ALU.mult).then_inc(dv, 1)
                    dve.wait_ge(ac, 4)
                    dchain.step(V.tensor_scalar(tab[:, 1], tab[:, 1], RET_SCALE, None, ALU.mult))
                    dchain.join(dve)
                    for t in range(NT):
                        V.tensor_tensor(kk[:, t], bc(kvw[:, t], 2, 2), bc(tab[:, 1].rearrange("p d h -> p h d"), 3, RDK),
                                        ALU.mult).then_inc(kk_done, 1)
                    for t in range(1, NT):
                        dchain.step(V.tensor_tensor(qq[:, t - 1], bc(qv[:, t], 2, 2),
                                                    bc(tab[:, 0].rearrange("p d h -> p h d"), 3, RDK), ALU.mult))
                    dve.wait_ge(ac, 4 + 2 * RH)
                    for d in range(2):
                        dchain.step(V.tensor_tensor(ex[:, d], ex[:, d], bc(const[:, C_MASK + d * P:C_MASK + (d + 1) * P], 1, RH), ALU.mult))
                    dchain.join(dve)
                    dchain.step(V.tensor_tensor(dt, ex[:, 0], ex[:, 1], ALU.add))
                    dve.wait_ge(st_in, 32)
                    dve.wait_ge(kv_out, NT)
                    for n in range(NT - 2):
                        f, b = n, NT - 2 - n
                        dchain.step(V.tensor_tensor(st[0:RDK, f + 1], st[0:RDK, f], bc(cd[0:RDK], 2, RDV), ALU.mult))
                        dchain.step(V.tensor_tensor(st[RDK:P, b - 1], st[RDK:P, b], bc(cd[RDK:P], 2, RDV), ALU.mult))
                        dchain.join(dve)
                        dchain.step(V.tensor_tensor(st[0:RDK, f + 1], st[0:RDK, f + 1], kv[0:RDK, f + 1], ALU.add))
                        dchain.step(V.tensor_tensor(st[RDK:P, b - 1], st[RDK:P, b - 1], kv[RDK:P, b + 1], ALU.add))
                        dchain.join(dve)

                @block.tensor
                def _(pe):
                    for t in range(NT):
                        pe.wait_ge(kk_done, t + 1)
                        if t >= 4:
                            pe.wait_ge(kv_out, t - 3)
                        for h in range(RH):
                            last = T.matmul(bank(2 * (t % 4), 2)[:, h * RDV:(h + 1) * RDV],
                                            kk[:, t, h].rearrange("p d k -> p (d k)"),
                                            proj[:, t, RV + h * RDV:RV + (h + 1) * RDV], start=True, stop=True)
                        last.then_inc(kv_done, 1)

                @block.scalar
                def _(act):
                    act.wait_ge(dv, 1)
                    A.activation(tl[:, 2, :], tl[:, 1, :], ACT.Exp, scale=-1.0).then_inc(ac, 1)
                    act.wait_ge(dv, 2)
                    A.activation(tl[:, 6, :], tl[:, 3, :], ACT.Ln).then_inc(ac, 1)
                    act.wait_ge(dv, 3)
                    A.activation(tab, tab, ACT.Exp).then_inc(ac, 1)
                    A.activation(cd, cd, ACT.Exp).then_inc(ac, 1)
                    for d in range(2):
                        for h in range(RH):
                            A.activation(ex[:, d, h], const[:, C_REL + d * P:C_REL + (d + 1) * P], ACT.Exp,
                                         scale=lg[:, d, h:h + 1]).then_inc(ac, 1)
                    for t in range(NT):
                        act.wait_ge(kv_done, t + 1)
                        A.copy(kv[:, t], bank(2 * (t % 4), 2).rearrange("p (h v) -> p h v", h=RH)).then_inc(kv_out, 1)
                    for t in range(NT):
                        A.activation(proj[:, t, RG:RG + RH * RDV], proj[:, t, RG:RG + RH * RDV], ACT.Silu)
                    act.drain()

            o = SH
            qt = at(o, 2, 4, P); o += 8 * P
            ktt = at(o, 2, RH, P); o += 2 * RH * P
            qqt = at(o, 2, RH, P); o += 2 * RH * P
            sm = at(o, 2, RH, P); o += 2 * RH * P
            cen = at(o, RH, RDV); o += RH * RDV
            bst = at(o, RH, 6); o += RH * 6
            bmv = at(o, RH, 2); o += RH * 2
            rt = at(o, 2, RH); o += 2 * RH
            assert o <= 53200
            trq, trc, scored, masked = sem("ret_tr"), sem("ret_trc"), sem("ret_scored"), sem("ret_masked")
            padded = sem("ret_padded")
            summed, centred, var, root = sem("ret_summed"), sem("ret_centred"), sem("ret_var"), sem("ret_root")
            with nc.Block(no_gpsimd_drain=True) as block:
                @block.tensor
                def _(pe):
                    def turn(t):
                        if t:
                            pe.wait_ge(trc, t)
                        for j in range(4):
                            T.transpose(bank(0)[:, j * P:(j + 1) * P], proj[:, t, RQ + j * P:RQ + (j + 1) * P], ident)
                            last = T.transpose(bank(1)[:, j * P:(j + 1) * P], proj[:, t, RK + j * P:RK + (j + 1) * P], ident)
                        if t:
                            for h in range(RH):
                                last = T.transpose(bank(2, 2)[:, h * P:(h + 1) * P], qq[:, t - 1, h].rearrange("p d k -> p (d k)"), ident)
                        last.then_inc(trq, 1)

                    turn(0)
                    pe.wait_ge(padded, 2)
                    for t in range(NT):
                        pe.wait_ge(trc, t + 1)
                        if t:
                            pe.wait_ge(masked, t)
                        for h in range(RH):
                            last = T.matmul(bank(4, 2)[:, h * P:(h + 1) * P], ktt[:, t % 2, h, :],
                                            qt[:, t % 2, h // 2, :], start=True, stop=True)
                        last.then_inc(scored, 1)
                        if t + 1 < NT:
                            turn(t + 1)
                        pe.wait_ge(masked, t + 1)
                        if t:
                            pe.wait_ge(centred, t)
                        for h in range(RH):
                            out = bank(6, 2)[:, h * P:(h + 1) * P]
                            last = T.matmul(out, sm[:, t % 2, h, :], proj[:, t, RV + h * RDV:RV + (h + 1) * RDV],
                                            start=True, stop=(t == 0))
                            if t:
                                last = T.matmul(out, qqt[:, t % 2, h, :], st[:, t - 1, h, :], start=False, stop=True)
                        last.then_inc(summed, 1)

                @block.gpsimd
                def _(pool):
                    for r in range(2):
                        rows = slice(RDK * (1 - r), RDK * (2 - r))
                        nc.gpsimd.memset(ktt[rows].rearrange("p a (j r) i -> p r (a j) i", r=2)[:, r], 0.0).then_inc(padded, 1)

                @block.scalar
                def _(act):
                    for t in range(NT):
                        act.wait_ge(trq, t + 1)
                        if t >= 2:
                            act.wait_ge(summed, t - 1)
                        A.copy(qt[:, t % 2], bank(0).rearrange("p (j i) -> p j i", j=4))
                        for r in range(2):
                            rows = slice(RDK * r, RDK * (r + 1))
                            last = A.copy(ktt[rows, t % 2].rearrange("p (j r) i -> p r j i", r=2)[:, r],
                                          bank(1)[rows].rearrange("p (j i) -> p j i", j=4))
                        if t:
                            last = A.copy(qqt[:, t % 2], bank(2, 2).rearrange("p (h i) -> p h i", h=RH))
                        last.then_inc(trc, 1)
                        if t:
                            act.wait_ge(var, t)
                            A.activation(rt[:, 0, :], bmv[:, :, 1], ACT.Sqrt, bias=eps_ln).then_inc(root, 1)
                    act.wait_ge(var, NT)
                    A.activation(rt[:, 0, :], bmv[:, :, 1], ACT.Sqrt, bias=eps_ln).then_inc(root, 1)

                @block.vector
                def _(dve):
                    def mask(t):
                        dve.wait_ge(scored, t + 1)
                        if t >= 2:
                            dve.wait_ge(summed, t - 1)
                        V.tensor_tensor(sm[:, t % 2], bank(4, 2).rearrange("p (h i) -> p h i", h=RH), dt,
                                        ALU.mult).then_inc(masked, 1)

                    def norm(t):
                        dve.wait_ge(summed, t + 1)
                        src = bank(6, 2).rearrange("p (h v) -> p h v", h=RH)
                        for h in range(RH):
                            dchain.step(V.bn_stats(bst[:, h], src[:, h]))
                        dchain.join(dve)
                        for h in range(RH):
                            last = V.bn_aggr(bmv[:, h], bst[:, h])
                        last.then_inc(var, 1)
                        dve.wait_ge(var, t + 1)
                        V.tensor_tensor(cen, src, bc(bmv[:, :, 0], 2, RDV), ALU.subtract).then_inc(centred, 1)
                        dve.wait_ge(root, t + 1)
                        dchain.step(V.reciprocal(rt[:, 1, :], rt[:, 0, :]))
                        dchain.join(dve)
                        dve.wait_ge(centred, t + 1)
                        dchain.step(V.tensor_tensor(cen, cen, bc(rt[:, 1, :], 2, RDV), ALU.mult))
                        dchain.join(dve)
                        g = proj[:, t, RG:RG + RH * RDV].rearrange("p (h v) -> p h v", h=RH)
                        dchain.step(V.tensor_tensor(g, g, cen, ALU.mult))
                        dchain.join(dve)

                    mask(0)
                    for t in range(NT):
                        if t + 1 < NT:
                            mask(t + 1)
                        norm(t)

        def heads_attention(name, units, qT, kT, value, width, e_buf, halves, lamr, put, rsum, nmax, pT, upright):
            scored, maxed, expd = sem(f"{name}_scored"), sem(f"{name}_maxed"), sem(f"{name}_expd")
            mixed = sem(f"{name}_mixed")
            turned, c_a, c_d, valued, put_s = (sem(f"{name}_{n}") for n in ("turned", "ca", "cd", "valued", "put"))
            U = len(units)
            tiles = [[NT] if t == 0 else list(range(NT)) for t, _ in units]

            def view(b, nk):
                if nk == 1:
                    return bank(2 * b)[:, 0:P]
                return bank(2 * b, 2).rearrange("p (a n) -> p a n", a=2)[:, :, 0:KEYS // 2]

            def out_of(u):
                h = units[u][1]
                b = bank(6 + u % 2)
                return b[width * (h % 2):width * (h % 2 + 1), 0:P] if upright else b[:, 0:width]

            def flat(b, nk):
                e = e_buf[:, b, 0:nk * P]
                return e if nk == 1 else e.rearrange("p (a n) -> p a n", a=2)

            with nc.Block(no_gpsimd_drain=True) as block:
                @block.tensor
                def _(pe):
                    def score(u):
                        t, h = units[u]
                        for s in range(halves):
                            v = halves * u + s
                            if v >= 2:
                                pe.wait_ge(expd, v - 1)
                            q = qT(t, h, s)
                            if t == 0:
                                T.matmul(view(v % 2, 1), q, kT(h, s, NT * P, P), start=True, stop=True).then_inc(scored, 1)
                            else:
                                for a in range(2):
                                    last = T.matmul(view(v % 2, NT)[:, a], q, kT(h, s, a * KEYS // 2, KEYS // 2), start=True, stop=True)
                                last.then_inc(scored, 1)

                    def turn(u):
                        pe.wait_ge(mixed, u + 1)
                        if u:
                            pe.wait_ge(c_d, u)
                            pe.wait_ge(c_a, u)
                        src = e_buf[:, (u % 2) * halves, :]
                        for n in range(len(tiles[u])):
                            b, c = (4, n) if n < 3 else (5, n - 3)
                            last = T.transpose(bank(b)[:, c * P:(c + 1) * P], src[:, n * P:(n + 1) * P], ident)
                        last.then_inc(turned, 1)

                    def values(u):
                        t, h = units[u]
                        pe.wait_ge(c_d, u + 1)
                        pe.wait_ge(c_a, u + 1)
                        if u >= 2:
                            pe.wait_ge(put_s, u - 1)
                        for n, kt in enumerate(tiles[u]):
                            w, v = pT[:, u % 2, n, :], value(h, kt)
                            last = T.matmul(out_of(u), v if upright else w, w if upright else v,
                                            start=(n == 0), stop=(n == len(tiles[u]) - 1))
                        last.then_inc(valued, 1)

                    for u in range(U + 2):
                        if u < U:
                            score(u)
                        if u >= 2:
                            values(u - 2)
                        if 1 <= u <= U:
                            turn(u - 1)

                @block.vector
                def _(dve):
                    def top(u):
                        for s in range(halves):
                            v = halves * u + s
                            nk = len(tiles[u])
                            dve.wait_ge(scored, v + 1)
                            src = view(v % 2, nk)
                            V.tensor_reduce(nmax[:, v:v + 1], src, AX.X if nk == 1 else AX.XY, ALU.max,
                                            negate=True).then_inc(maxed, 1)

                    def mix(u):
                        dve.wait_ge(expd, halves * (u + 1))
                        dchain.step(V.reciprocal(rsum[:, 1, halves * u:halves * (u + 1)], rsum[:, 0, halves * u:halves * (u + 1)]))
                        dchain.join(dve)
                        if halves == 2:
                            nk = len(tiles[u]) * P
                            r = rsum[:, 1, 2 * u:2 * u + 2]
                            e1, e2 = (e_buf[:, 2 * (u % 2) + s, 0:nk] for s in range(2))
                            dchain.step(V.tensor_tensor(r[:, 1:2], r[:, 1:2], lamr, ALU.mult))
                            dchain.join(dve)
                            dchain.step(V.tensor_scalar(e2, e2, r[:, 1:2], None, ALU.mult))
                            dchain.join(dve)
                            V.scalar_tensor_tensor(e1, e1, r[:, 0:1], e2, ALU.mult, ALU.subtract).then_inc(mixed, 1)
                        else:
                            e1 = e_buf[:, u % 2, 0:len(tiles[u]) * P]
                            V.tensor_scalar(e1, e1, rsum[:, 1, u:u + 1], None, ALU.mult).then_inc(mixed, 1)

                    def copy_p(u):
                        dve.wait_ge(turned, u + 1)
                        if u >= 2:
                            dve.wait_ge(valued, u - 1)
                        nd = min(3, len(tiles[u]))
                        V.tensor_copy(pT[:, u % 2, 0:nd], bank(4)[:, 0:nd * P].rearrange("p (n q) -> p n q", n=nd)).then_inc(c_d, 1)

                    def out(u):
                        dve.wait_ge(valued, u + 1)
                        V.tensor_copy(put(*units[u]), out_of(u)).then_inc(put_s, 1)

                    for u in range(U + 2):
                        if u < U:
                            top(u)
                        if 1 <= u <= U:
                            mix(u - 1)
                        if u >= 2:
                            out(u - 2)
                        if 1 <= u <= U:
                            copy_p(u - 1)
                    dve.drain()

                @block.scalar
                def _(act):
                    def exps(u):
                        for s in range(halves):
                            v = halves * u + s
                            nk = len(tiles[u])
                            act.wait_ge(maxed, v + 1)
                            if u >= 2:
                                act.wait_ge(turned, u - 1)
                            A.activation(flat((u % 2) * halves + s, nk), view(v % 2, nk), ACT.Exp,
                                         bias=nmax[:, v:v + 1], accum_out=rsum[:, 0, v:v + 1]).then_inc(expd, 1)

                    def copy_p(u):
                        act.wait_ge(turned, u + 1)
                        if u >= 2:
                            act.wait_ge(valued, u - 1)
                        n = len(tiles[u])
                        if n > 3:
                            A.copy(pT[:, u % 2, 3:n], bank(5)[:, 0:(n - 3) * P].rearrange("p (n q) -> p n q", q=P)).then_inc(c_a, 1)
                        else:
                            act.nop().then_inc(c_a, 1)

                    for u in range(U + 1):
                        if u < U:
                            exps(u)
                        if u >= 1:
                            copy_p(u - 1)

        UNITS = [(t, h) for t in range(1, NT) for h in range(8)] + [(0, h) for h in range(8)]

        def latent_attention(mlaT):
            o = R
            kT = at(o, MH, NK * P); o += MH * NK * P
            qT = at(o, MH, TOK); o += MH * TOK
            vm = at(o, NK, MH * MDV); o += NK * MH * MDV
            E_AT = o
            ckc = at(o, MKV); o += MKV
            krp = at(o, NK, MQD); o += NK * MQD
            rope = at(o, 2, NT - 1, MR // 2); o += (NT - 1) * MR
            tmp = at(o, 4, NT - 1, MH, MR // 2); o += 4 * (NT - 1) * MH * MR // 2
            tmk = at(o, 4, NT - 1, MR // 2); o += 4 * (NT - 1) * MR // 2
            ckT = at(o, 2, NK * P); o += 2 * NK * P
            wuk = at(o, 2, MH * MN); o += 2 * MH * MN
            wuv = at(o, 2, MH * MDV); o += 2 * MH * MDV
            junk = at(o, MKV); o += MKV
            ss = at(o, 2, NT); o += 2 * NT
            assert o <= 53200, o
            loaded, w_in, kr_in = sem("mla_loaded"), sem("mla_win"), sem("mla_krin")
            squared, normed, roped, padded = sem("mla_sq"), sem("mla_norm"), sem("mla_rope"), sem("mla_pad")
            tr, ev_a, ev_d = sem("mla_tr"), sem("mla_eva"), sem("mla_evd")
            ck = proj[:, :, CKV:CKV + MKV]
            kr = proj[:, :, KR:KR + MR]
            mq = proj[:, :, MQ:MQ + MH * MQD].rearrange("p t (h d) -> p t h d", h=MH)
            H2 = MR // 2

            items = []
            for c in range(2):
                items.append(("ck", c))
            items.append(("kr", 0))
            for h in range(MH):
                items.append(("q", h))
            for j in range(MH // 2):
                items.append(("k", j))
            for n in range(NK // 2):
                items.append(("v", n))
            def evac(eng, who):
                copy = A.copy if who == 0 else V.tensor_copy
                done = (ev_a, ev_d)[who]
                for n, (kind, j) in enumerate(items):
                    if n % 2 != who:
                        continue
                    eng.wait_ge(tr, n + 1)
                    src = bank(2 * (n % 4), 2)
                    if kind == "ck":
                        copy(ckT[:, j, :], src[:, 0:NK * P]).then_inc(done, 1)
                    elif kind == "kr":
                        copy(kT[MN:MQD], bc(src[MN:MQD, 0:NK * P], 1, MH)).then_inc(done, 1)
                    elif kind == "q":
                        if who == 0:
                            A.mul(qT[0:MQD, j, :], src[0:MQD, 0:TOK], MLA_SCALE).then_inc(done, 1)
                        else:
                            V.tensor_scalar(qT[0:MQD, j, :], src[0:MQD, 0:TOK], MLA_SCALE, None, ALU.mult).then_inc(done, 1)
                    elif kind == "k":
                        s2 = src.rearrange("p (a n) -> p a n", a=2)[:, :, 0:NK * P // 2]
                        for r in range(2):
                            last = copy(kT[0:MN, 2 * j + r, :].rearrange("p (a n) -> p a n", a=2), s2[MN * r:MN * (r + 1)])
                        last.then_inc(done, 1)
                    else:
                        copy(vm[:, 2 * j:2 * j + 2, :], src.rearrange("p (a n) -> p a n", a=2)).then_inc(done, 1)

            with nc.Block(no_gpsimd_drain=True) as block:
                @block.sync
                def _(sp):
                    sp.dma_start(krp[:, 0, MN:MQD], I["cache_mla_krope"][0, 0]).then_inc(kr_in, 16)
                    sp.dma_start(ckc, I["cache_mla_ckv"][0, 0]).then_inc(kr_in, 16)
                    sp.dma_start(rope, I["rope_mla"].rearrange("a (t p) n -> p a t n", p=P)).then_inc(loaded, 16)
                    sp.dma_start(wuk, I["mla_w_uk"][0].rearrange("(k p) n -> p k n", p=P)).then_inc(w_in, 16)
                    sp.dma_start(wuv, I["mla_w_uv"][0].rearrange("(k p) n -> p k n", p=P)).then_inc(w_in, 16)
                    store(sp, O["new_cache_mla_krope"][0, 0], kr[:, 0, :])
                    sp.wait_ge(normed, 1)
                    store(sp, O["new_cache_mla_ckv"][0, 0], ck[:, 0, :])

                @block.scalar
                def _(act):
                    for t in range(NT):
                        achain.step(A.activation(junk, ck[:, t, :], ACT.Square, accum_out=ss[:, 0, t:t + 1]))
                        achain.join(act)
                    A.activation(ss[:, 1, :], ss[:, 0, :], ACT.Sqrt, bias=eps_rms, scale=1.0 / MKV).then_inc(squared, 1)
                    evac(act, 0)
                    act.drain()

                @block.vector
                def _(dve):
                    V.memset(krp[:, :, 0:MN], 0.0).then_inc(padded, 1)
                    dve.wait_ge(squared, 1)
                    dchain.step(V.reciprocal(ss[:, 0, :], ss[:, 1, :]))
                    dchain.join(dve)
                    for t in range(NT):
                        V.scalar_tensor_tensor(ck[:, t, :], ck[:, t, :], ss[:, 0, t:t + 1], kvg, ALU.mult, ALU.mult).then_inc(normed, 1)
                    dve.wait_ge(loaded, 16)
                    for x1, x2, y1, y2, tm, cs in (
                            (mq[:, 1:NT, :, MN:MN + H2], mq[:, 1:NT, :, MN + H2:MQD], mq[:, 1:NT, :, MN:MN + H2],
                             mq[:, 1:NT, :, MN + H2:MQD], tmp, [bc(rope[:, s], 2, MH) for s in range(2)]),
                            (kr[:, 1:NT, 0:H2], kr[:, 1:NT, H2:MR], krp[:, 1:NT, MN:MN + H2], krp[:, 1:NT, MN + H2:MQD],
                             tmk, [rope[:, s] for s in range(2)])):
                        for n, (src, s) in enumerate(((x1, 0), (x2, 1), (x1, 1), (x2, 0))):
                            dchain.step(V.tensor_tensor(tm[:, n], src, cs[s], ALU.mult))
                        dchain.join(dve)
                        dchain.step(V.tensor_tensor(y1, tm[:, 0], tm[:, 1], ALU.subtract))
                        V.tensor_tensor(y2, tm[:, 2], tm[:, 3], ALU.add).then_inc(roped, 1)
                    V.tensor_copy(krp[:, NT, MN:MQD], kr[:, 0, :]).then_inc(roped, 1)
                    evac(dve, 1)
                    dve.drain()

                @block.tensor
                def _(pe):
                    for n, (kind, j) in enumerate(items):
                        if n >= 4:
                            pe.wait_ge((ev_a, ev_d)[n % 2], (n - 4) // 2 + 1)
                        dst = bank(2 * (n % 4), 2)
                        if kind == "ck":
                            if j == 0:
                                pe.wait_ge(kr_in, 32)
                                pe.wait_ge(normed, NT)
                            for m in range(NK):
                                src = ckc if m == 0 else ck[:, m % NT, :]
                                last = T.transpose(dst[:, m * P:(m + 1) * P], src[:, j * P:(j + 1) * P], ident)
                        elif kind == "kr":
                            pe.wait_ge(roped, 3)
                            pe.wait_ge(padded, 1)
                            for m in range(NK):
                                last = T.transpose(dst[0:MQD, m * P:(m + 1) * P], krp[:, m, :], ident)
                        elif kind == "q":
                            for t in range(NT):
                                last = T.transpose(dst[0:MQD, t * P:(t + 1) * P], mq[:, t, j, :], ident)
                        elif kind == "k":
                            if j == 0:
                                pe.wait_ge(ev_a, 1)
                                pe.wait_ge(ev_d, 1)
                                pe.wait_ge(w_in, 32)
                            for a in range(2):
                                for k in range(2):
                                    last = T.matmul(dst[:, a * BANK:a * BANK + NK * P // 2], wuk[:, k, j * P:(j + 1) * P],
                                                    ckT[:, k, a * NK * P // 2:(a + 1) * NK * P // 2], start=(k == 0), stop=(k == 1))
                        else:
                            for a in range(2):
                                m = 2 * j + a
                                for k in range(2):
                                    last = T.matmul(dst[:, a * BANK:(a + 1) * BANK], ckT[:, k, m * P:(m + 1) * P],
                                                    wuv[:, k, :], start=(k == 0), stop=(k == 1))
                        last.then_inc(tr, 1)

            o = E_AT
            e_buf = at(o, 2, KEYS); o += 2 * KEYS
            pT = at(o, 2, NT, P); o += 2 * NT * P
            rsum = at(o, 2, len(UNITS)); o += 2 * len(UNITS)
            nmax = at(o, len(UNITS)); o += len(UNITS)
            heads_attention(
                "mla", UNITS,
                lambda t, h, s: qT[0:MQD, h, t * P:(t + 1) * P],
                lambda h, s, k0, n: kT[0:MQD, h, k0:k0 + n],
                lambda h, kt: vm[:, kt, h * MDV:(h + 1) * MDV],
                MDV, e_buf, 1, None,
                lambda t, h: mlaT[MDV * (h % 2):MDV * (h % 2 + 1), h // 2, t * P:(t + 1) * P], rsum, nmax, pT, True)

        def differential_attention(pj):
            o = R
            kT = at(o, DH, NK * P); o += DH * NK * P
            qT = at(o, DH, 2, TOK); o += 2 * DH * TOK
            vc = at(o, DH, DDV); o += DH * DDV
            kc = at(o, DH, DDV)
            rope = at(o + DH * DDV, 2, NT - 1, DDH // 2)
            tmp = at(R, 4, 32, DDH // 2)
            lp = at(o + 2 * DH * DDV, 4, DDH)
            assert o + 2 * DH * DDV + 256 <= 53200
            H2 = DDH // 2
            QS = 4 * DH
            loaded, k_in = sem("diff_loaded"), sem("diff_kin")
            roped, tr, ev_a, ev_d, lam_v, lam_a = (sem(f"diff_{n}") for n in ("roped", "tr", "eva", "evd", "lamv", "lama"))
            lam1 = small[:, 32:34]
            def evac(eng, who):
                done = (ev_a, ev_d)[who]
                for n, (kind, h) in enumerate(items):
                    if n % 2 != who:
                        continue
                    eng.wait_ge(tr, n + 1)
                    src = bank(2 * (n % 4), 2)
                    if kind == "k":
                        copy = A.copy if who == 0 else V.tensor_copy
                        copy(kT[:, h, :], src[:, 0:NK * P]).then_inc(done, 1)
                        continue
                    for r in range(2):
                        rows = slice(DDH * r, DDH * (r + 1))
                        dst, half = qT[rows, h, r, :], src[rows, 0:TOK]
                        if who == 0:
                            last = A.mul(dst, half, DIFF_SCALE)
                        else:
                            last = V.tensor_scalar(dst, half, DIFF_SCALE, None, ALU.mult)
                    last.then_inc(done, 1)

            with nc.Block(no_gpsimd_drain=True) as block:
                @block.sync
                def _(sp):
                    sp.dma_start(rope, I["rope_diff"].rearrange("a (t p) n -> p a t n", p=P)).then_inc(loaded, 16)
                    sp.dma_start(lp, I["diff_lambda"][0].partition_broadcast(P)).then_inc(loaded, 16)
                    sp.dma_start(kc, I["cache_diff_k"][0, 0].rearrange("h p d -> p h d")).then_inc(k_in, 16)
                    sp.dma_start(vc, I["cache_diff_v"][0, 0].rearrange("h p d -> p h d")).then_inc(k_in, 16)
                    store(sp, O["new_cache_diff_k"][0, 0].rearrange("h p d -> p h d"),
                          pj[:, 0, D:2 * D].rearrange("p (h d) -> p h d", h=DH))
                    store(sp, O["new_cache_diff_v"][0, 0].rearrange("h p d -> p h d"),
                          pj[:, 0, 2 * D:3 * D].rearrange("p (h d) -> p h d", h=DH))

                items = [("q", h) for h in range(DH)] + [("k", h) for h in range(DH)]

                @block.gpsimd
                def _(pool):
                    for r in range(2):
                        rows = slice(DDH * (1 - r), DDH * (2 - r))
                        nc.gpsimd.memset(qT[rows, :, r, :], 0.0)
                    pool.drain()

                @block.vector
                def _(dve):
                    dve.wait_ge(loaded, 32)
                    for t in range(1, NT):
                        xs = pj[:, t, 0:2 * D].rearrange("p (g d) -> p g d", d=DDH)
                        x1, x2 = xs[:, :, 0:H2], xs[:, :, H2:DDH]
                        cs = [bc(rope[:, s, t - 1], 1, QS) for s in range(2)]
                        for n, (src, s) in enumerate(((x1, 0), (x2, 1), (x1, 1), (x2, 0))):
                            dchain.step(V.tensor_tensor(tmp[:, n], src, cs[s], ALU.mult))
                        dchain.join(dve)
                        dchain.step(V.tensor_tensor(x1, tmp[:, 0], tmp[:, 1], ALU.subtract))
                        V.tensor_tensor(x2, tmp[:, 2], tmp[:, 3], ALU.add).then_inc(roped, 1)
                        dve.wait_ge(roped, t)
                    lq = lp.rearrange("p (a b) d -> p a b d", a=2)
                    dchain.step(V.tensor_tensor(lq[:, :, 0], lq[:, :, 0], lq[:, :, 1], ALU.mult))
                    dchain.join(dve)
                    V.tensor_reduce(lam1, lq[:, :, 0], AX.X, ALU.add).then_inc(lam_v, 1)
                    evac(dve, 1)
                    dve.wait_ge(lam_a, 1)
                    dchain.step(V.tensor_tensor(lam[:, 0:1], lam[:, 2:3], lam[:, 3:4], ALU.subtract))
                    dchain.join(dve)
                    dchain.step(V.tensor_scalar(lam[:, 0:1], lam[:, 0:1], LAM_INIT, None, ALU.add))
                    dve.drain()

                @block.scalar
                def _(act):
                    act.wait_ge(lam_v, 1)
                    A.activation(lam[:, 2:4], lam1, ACT.Exp).then_inc(lam_a, 1)
                    evac(act, 0)
                    act.drain()

                @block.tensor
                def _(pe):
                    pe.wait_ge(roped, NT - 1)
                    pe.wait_ge(k_in, 32)
                    for n, (kind, h) in enumerate(items):
                        if n >= 4:
                            pe.wait_ge((ev_a, ev_d)[n % 2], (n - 4) // 2 + 1)
                        dst = bank(2 * (n % 4), 2)
                        if kind == "q":
                            for t in range(NT):
                                last = T.transpose(dst[:, t * P:(t + 1) * P], pj[:, t, h * DDV:(h + 1) * DDV], ident)
                        else:
                            for m in range(NK):
                                src = kc[:, h, :] if m == 0 else pj[:, m % NT, D + h * DDV:D + (h + 1) * DDV]
                                last = T.transpose(dst[:, m * P:(m + 1) * P], src, ident)
                        last.then_inc(tr, 1)

            o = R + DH * NK * P + 2 * DH * TOK + DH * DDV
            e_buf = at(o, 4, KEYS); o += 4 * KEYS
            pT = at(o, 2, NT, P); o += 2 * NT * P
            rsum = at(o, 2, 2 * len(UNITS)); o += 4 * len(UNITS)
            nmax = at(o, 2 * len(UNITS)); o += 2 * len(UNITS)
            heads_attention(
                "diff", UNITS,
                lambda t, h, s: qT[:, h, s, t * P:(t + 1) * P],
                lambda h, s, k0, n: kT[:, h, k0:k0 + n],
                lambda h, kt: vc[:, h, :] if kt == 0 else pj[:, kt % NT, 2 * D + h * DDV:2 * D + (h + 1) * DDV],
                DDV, e_buf, 2, lam[:, 0:1],
                lambda t, h: pj[:, t, h * DDV:(h + 1) * DDV], rsum, nmax, pT, False)

            sq = at(R, 2, D)
            ss = at(R + 2 * D, NT, DH)
            rt = at(R + 2 * D + NT * DH, 2, NT, DH)
            squared, rooted, freed, gs = sem("dn_squared"), sem("dn_root"), sem("dn_freed"), sem("dn_sums")
            with nc.Block(no_gpsimd_drain=True) as block:
                @block.scalar
                def _(act):
                    for t in range(NT):
                        if t >= 2:
                            act.wait_ge(freed, t - 1)
                        A.activation(sq[:, t % 2, :], pj[:, t, 0:D], ACT.Square).then_inc(squared, 1)
                    act.wait_ge(freed, NT)
                    A.activation(rt[:, 0], ss, ACT.Sqrt, bias=eps_rms, scale=1.0 / DDV).then_inc(rooted, 1)

                @block.vector
                def _(dve):
                    dchain.step(V.tensor_scalar(dng, dng, 1.0 - LAM_INIT, None, ALU.mult))
                    for t in range(NT):
                        dve.wait_ge(squared, t + 1)
                        V.tensor_reduce(ss[:, t, :], sq[:, t % 2, :].rearrange("p (h v) -> p h v", h=DH), AX.X,
                                        ALU.add).then_inc(freed, 1)
                    dve.wait_ge(rooted, 1)
                    dchain.step(V.reciprocal(rt[:, 1], rt[:, 0]))
                    dchain.join(dve)
                    for t in range(NT):
                        ov = pj[:, t, 0:D].rearrange("p (h v) -> p h v", h=DH)
                        dchain.step(V.tensor_tensor(ov, ov, bc(rt[:, 1, t, :], 2, DDV), ALU.mult))
                        dchain.join(dve)
                        dchain.step(V.tensor_tensor(ov, ov, bc(dng, 1, DH), ALU.mult))
                    dve.drain()

        def router(i):
            w = R + W_EXP
            lo = at(w, NT, G + NE)
            w += 256

            def b4(n):
                return at(w + n * 64, NT, G)

            def b1(n):
                return at(w + 1024 + n * 8, NT)

            sel, pg, pe_, ohg, oh1, oh2, t4, p2 = (b4(n) for n in range(8))
            gm, gs_, em, s1, s2, gp, a1, a2, tm1 = (b1(n) for n in range(9))
            prod = at(w + 2048, NT, G, EG)
            ohk = at(w + 2304, 2, NT, NE)
            every = at(w + 2560, NT, NE)
            slot = at(w + 2816, NT, NE)
            pre = at(w + 3072, NT + 1, NE)
            cnt = pre[:, NT, :]
            over, incl, tmi, excl, jump = (at(w + 3328 + 16 * n, NE) for n in range(5))
            pos = at(w + 3456, 2, NT)
            tokf = at(w + 3584, P)
            far = at(w + 3712, NT, NE)
            tie4 = bc(const[:, C_TIE:C_TIE + 4], 1, NT)
            nm, ex, picked, ranked = sem(f"r{i}_neg"), sem(f"r{i}_exp"), sem(f"r{i}_picked"), sem(f"r{i}_ranked")
            placed, sent, listed, turned = sem(f"r{i}_placed"), sem(f"r{i}_sent"), sem(f"r{i}_listed"), sem(f"r{i}_turned")
            E13, E2 = WEIGHTS[1]
            with nc.Block(no_gpsimd_drain=True) as block:
                @block.sync
                def _(sp):
                    sp.dma_start(E13[0], I["moe_w1"][i, 1].rearrange("(k p) f -> p k f", p=P)).then_inc(up_in[1], 16)
                    sp.dma_start(E13[1], I["moe_w3"][i, 1].rearrange("(k p) f -> p k f", p=P)).then_inc(up_in[1], 16)
                    sp.dma_start(E2, I["moe_w2"][i, 1].rearrange("(f p) n -> p f n", p=P)).then_inc(dn_in[1], 16)
                    sp.wait_ge(sent, 16 * 2 * NT)
                    sp.dma_start(tokf[0:CHUNKS, :], slot_tok.rearrange("(a b) o -> a (b o)", b=P)).then_inc(listed, 16)

                @block.gpsimd
                def _(pool):
                    pool.wait_ge(placed, 1)
                    for k in range(2):
                        for t in range(NT):
                            pool.indirect_dma_start(out=slot_tok, out_offset=bass.IndirectOffsetOnAxis(ap=slot_i[:, k, t:t + 1], axis=0),
                                                    in_=const[:, C_TOK + t:C_TOK + t + 1], in_offset=None).then_inc(sent, 16)

                @block.tensor
                def _(pe):
                    pe.wait_ge(picked, 1)
                    m = every.rearrange("p t e -> p (t e)")
                    T.matmul(bank(0)[:, 0:NT * NE], const[:, C_TRI:C_TRI + P], m, start=True, stop=True)
                    T.matmul(bank(1)[:, 0:NT * NE], ones, m, start=True, stop=True).then_inc(ranked, 1)
                    pe.wait_ge(listed, 16)
                    T.transpose(bank(2)[:, 0:CHUNKS], tokf[0:CHUNKS, :], ident[0:CHUNKS, 0:CHUNKS]).then_inc(turned, 1)

                @block.vector
                def _(dve):
                    def do(ins):
                        dchain.step(ins)
                        dchain.join(dve)

                    def first_of(out, vals, top):
                        do(V.tensor_tensor(out, vals, bc(top, 2, 4), ALU.is_equal))
                        do(V.tensor_tensor(out, out, tie4, ALU.mult))
                        do(V.tensor_reduce(tm1, out, AX.X, ALU.max))
                        do(V.tensor_tensor(out, out, bc(tm1, 2, 4), ALU.is_equal))

                    do(V.tensor_tensor(lo, bank(6, 2)[:, 0:NT * P].rearrange("p (t n) -> p t n", t=NT)[:, :, 0:G + NE],
                                       bc(br[:, i, :], 1, NT), ALU.add))
                    lgp = lo[:, :, 0:G]
                    do(V.tensor_reduce(gm, lgp, AX.X, ALU.max))
                    first_of(ohg, lgp, gm)
                    V.tensor_tensor(pg, lgp, bc(gm, 2, G), ALU.subtract).then_inc(nm, 1)
                    do(V.tensor_tensor(prod, lo[:, :, G:].rearrange("p t (g e) -> p t g e", g=G), bc(ohg, 3, EG), ALU.mult))
                    do(V.tensor_reduce(sel, prod.rearrange("p t g e -> p t e g"), AX.X, ALU.add))
                    do(V.tensor_reduce(em, sel, AX.X, ALU.max))
                    V.tensor_tensor(pe_, sel, bc(em, 2, EG), ALU.subtract).then_inc(nm, 1)
                    dve.wait_ge(ex, 2)
                    do(V.tensor_reduce(s1, pe_, AX.X, ALU.max))
                    first_of(oh1, pe_, s1)
                    do(V.tensor_tensor(t4, pe_, oh1, ALU.mult))
                    do(V.tensor_tensor(p2, pe_, t4, ALU.subtract))
                    do(V.tensor_tensor(p2, p2, oh1, ALU.subtract))
                    do(V.tensor_reduce(s2, p2, AX.X, ALU.max))
                    first_of(oh2, p2, s2)
                    for k, oh in enumerate((oh1, oh2)):
                        dchain.step(V.tensor_tensor(ohk[:, k].rearrange("p t (g e) -> p t g e", g=G), bc(oh, 2, G), bc(ohg, 3, EG), ALU.mult))
                    dchain.join(dve)
                    V.tensor_tensor(every, ohk[:, 0], ohk[:, 1], ALU.add).then_inc(picked, 1)
                    do(V.tensor_reduce(gs_, pg, AX.X, ALU.add))
                    do(V.reciprocal(gp, gs_))
                    do(V.tensor_tensor(a1, s1, s2, ALU.add))
                    do(V.reciprocal(a2, a1))
                    do(V.tensor_tensor(gp, gp, a2, ALU.mult))
                    dchain.step(V.tensor_tensor(gates[:, 0], gp, s1, ALU.mult))
                    dchain.step(V.tensor_tensor(gates[:, 1], gp, s2, ALU.mult))
                    dchain.step(V.memset(pre[:, 0, :], 0.0))
                    dchain.join(dve)
                    dve.wait_ge(ranked, 1)
                    tot = bank(1)[:, 0:NT * NE].rearrange("p (t e) -> p t e", t=NT)
                    for t in range(NT):
                        do(V.tensor_tensor(pre[:, t + 1, :], pre[:, t, :], tot[:, t, :], ALU.add))
                    do(V.tensor_tensor(slot, pre[:, 0:NT, :], bank(0)[:, 0:NT * NE].rearrange("p (t e) -> p t e", t=NT), ALU.add))
                    do(V.tensor_scalar(over, cnt, float(P), None, ALU.is_gt))
                    for c in range(2, NT):
                        do(V.scalar_tensor_tensor(over, cnt, float(c * P), over, ALU.is_gt, ALU.add))
                    src, dst_ = over, incl
                    for d in (1, 2, 4, 8):
                        dchain.step(V.tensor_tensor(dst_[:, d:], src[:, d:], src[:, 0:NE - d], ALU.add))
                        dchain.step(V.tensor_copy(dst_[:, 0:d], src[:, 0:d]))
                        dchain.join(dve)
                        src, dst_ = dst_, (tmi if dst_ is incl else incl)
                    do(V.tensor_tensor(excl, src, over, ALU.subtract))
                    first_slot = const[:, C_SLOT:C_SLOT + NE]
                    do(V.scalar_tensor_tensor(jump, excl, float(P), first_slot, ALU.mult, ALU.subtract))
                    do(V.tensor_scalar(jump, jump, float((NE - 1) * P), None, ALU.add))
                    do(V.scalar_tensor_tensor(far, slot, float(P), bc(jump, 1, NT), ALU.is_ge, ALU.mult))
                    do(V.tensor_tensor(slot, slot, bc(first_slot, 1, NT), ALU.add))
                    do(V.tensor_tensor(slot, slot, far, ALU.add))
                    for k in range(2):
                        dchain.step(V.tensor_tensor(ohk[:, k], ohk[:, k], slot, ALU.mult))
                    dchain.join(dve)
                    do(V.tensor_reduce(pos, ohk, AX.X, ALU.add))
                    V.tensor_copy(slot_i, pos).then_inc(placed, 1)
                    dchain.step(V.tensor_copy(tables[:, 0], over))
                    dchain.step(V.tensor_copy(tables[:, 1], excl))
                    dchain.step(V.tensor_scalar(tables[:, 2], src, 1.0, None, ALU.add))
                    dve.wait_ge(turned, 1)
                    dchain.step(V.tensor_copy(tok_i, bank(2)[:, 0:CHUNKS]))
                    dchain.join(dve)
                    dve.drain()

                @block.scalar
                def _(act):
                    act.wait_ge(nm, 1)
                    A.activation(pg, pg, ACT.Exp).then_inc(ex, 1)
                    act.wait_ge(nm, 2)
                    A.activation(pe_, pe_, ACT.Exp).then_inc(ex, 1)

        def experts(i):
            o = R + W_EXP
            xg, xt, yb = at(o, 2, D), at(o + 2 * D, 2, KD, P), at(o + 4 * D, 2, D)
            o += 6 * D
            hid, gate = at(o, 2, 2, P), at(o + 4 * P, 2, 2, P)
            o += 8 * P
            xg_o, xt_o, yb_o = at(o, D), at(o + D, KD, P), at(o + 2 * D, D)
            hid_o, gate_o = at(o + 3 * D, 2, P), at(o + 3 * D + 2 * P, 2, P)
            o += 3 * D + 4 * P
            rows = at(o, 4).bitcast(I32)
            assert o + 4 <= 53200
            xg_in = [sem(f"x{i}_xg{b}") for b in range(2)]
            y_out = [sem(f"x{i}_yout{b}") for b in range(2)]
            turned, xt_a, xt_d, up_s, silu_s, hid_s, y_s, y_a, y_d = (
                sem(f"x{i}_{n}") for n in ("turned", "xta", "xtd", "up", "silu", "hid", "y", "ya", "yd"))
            o_in, o_turned, o_xt, o_up, o_silu, o_hid, o_y, o_yc, o_out = (
                sem(f"o{i}_{n}") for n in ("in", "turned", "xt", "up", "silu", "hid", "y", "yc", "out"))
            W1 = I["moe_w1"][i].rearrange("e (k p) f -> e p k f", p=P)
            W3 = I["moe_w3"][i].rearrange("e (k p) f -> e p k f", p=P)
            W2 = I["moe_w2"][i].rearrange("e (f p) n -> e p f n", p=P)
            y_chunks = y_rows.rearrange("(c p) n -> c p n", p=P)
            HALF = NE // 2

            def one(ap, e):
                return ap[bass.ds(e, 1)].rearrange("a p k f -> p (a k) f")

            def chunk_rows(c):
                return y_chunks[bass.ds(c, 1)].rearrange("a p n -> p (a n)")

            def up(dst, weights, xT):
                for f in range(2):
                    for m in range(2):
                        for k in range(KD):
                            last = T.matmul(dst[:, (2 * f + m) * P:(2 * f + m + 1) * P], weights[m][:, k, f * P:(f + 1) * P],
                                            xT[:, k, :], start=(k == 0), stop=(k == KD - 1))
                return last

            def down(b0, h, w2):
                for j in range(2):
                    for f in range(2):
                        last = T.matmul(bank(b0 + j), h[:, f, :], w2[:, f, j * BANK:(j + 1) * BANK], start=(f == 0), stop=(f == 1))
                return last

            def w13_part(b, m):
                return bank(b).rearrange("p (f m n) -> p m f n", f=2, m=2)[:, m]

            def loop(eng, expert):
                expert(0, 0, True)
                expert(1, 1, True)
                with eng.Fori(1, HALF) as pair:
                    expert(pair * 2, 0, False)
                    expert(pair * 2 + 1, 1, False)

            def entry(eng, row, e):
                col = tables[0:1, row, e:e + 1] if isinstance(e, int) else tables[0:1, row, bass.ds(e, 1)]
                return eng.value_load(col, min_val=0, max_val=(NT - 1) if row == 0 else FURTHER + 1)

            def further(eng, e, chunk):
                n = entry(eng, 0, e)
                first = entry(eng, 1, e)
                with eng.If(n > 0):
                    with eng.Fori(0, n) as c:
                        chunk(nc.s_assert_within(first + c, 0, FURTHER - 1, skip_runtime_bounds_check_because=(
                            "two experts for each token fill at most FURTHER chunks beyond the first ones")), c)
                eng.nop()

            with nc.Block(no_gpsimd_drain=True) as block:
                @block.sync
                def _(sp):
                    def expert(e, b, more):
                        E13, E2 = WEIGHTS[b]
                        done = entry(sp, 2, e)
                        dst = chunk_rows(e)
                        if more:
                            w1, w3, w2 = one(W1, e + 2), one(W3, e + 2), one(W2, e + 2)
                            sp.wait_ge(up_s, e + 1)
                            sp.wait_ge(o_up, done)
                            sp.dma_start(E13[0], w1).then_inc(up_in[b], 16)
                            sp.dma_start(E13[1], w3).then_inc(up_in[b], 16)
                            sp.wait_ge(y_s, e + 1)
                            sp.wait_ge(o_y, done)
                            sp.dma_start(E2, w2).then_inc(dn_in[b], 16)
                        sp.wait_ge(y_a, e + 1)
                        sp.dma_start(dst[:, 0:BANK], yb[:, b, 0:BANK]).then_inc(y_out[b], 16)
                        sp.wait_ge(y_d, e + 1)
                        sp.dma_start(dst[:, BANK:D], yb[:, b, BANK:D]).then_inc(y_out[b], 16)

                    with sp.Fori(0, HALF - 1) as pair:
                        expert(pair * 2, 0, True)
                        expert(pair * 2 + 1, 1, True)
                    expert(NE - 2, 0, False)
                    expert(NE - 1, 1, False)
                    for b in range(2):
                        sp.wait_ge(y_out[b], 32 * HALF)

                @block.gpsimd
                def _(pool):
                    def gather(e, b):
                        col = tok_i[:, e:e + 1] if isinstance(e, int) else tok_i[:, bass.ds(e, 1)]
                        nc.gpsimd.tensor_copy(rows[:, b:b + 1], col)
                        pool.drain()
                        pool.indirect_dma_start(out=xg[:, b, :], out_offset=None, in_=h2_rows, in_offset=bass.IndirectOffsetOnAxis(
                            ap=rows[:, b:b + 1], axis=0)).then_inc(xg_in[b], 16)

                    def expert(e, b, first):
                        if not (first and e == 0):
                            pool.wait_ge(turned, e + 0 if isinstance(e, int) else e)
                        gather(e + 1, 1 - b)

                        def chunk(q, c):
                            pool.wait_ge(o_turned, q + 1)
                            nc.gpsimd.tensor_copy(rows[:, 2:3], tok_i[:, bass.ds(q + NE, 1)])
                            pool.drain()
                            pool.indirect_dma_start(out=xg_o, out_offset=None, in_=h2_rows, in_offset=bass.IndirectOffsetOnAxis(
                                ap=rows[:, 2:3], axis=0)).then_inc(o_in, 16)
                        further(pool, e, chunk)

                    gather(0, 0)
                    loop(pool, expert)
                    pool.wait_ge(o_out, entry(pool, 2, NE - 1) * 16)

                @block.tensor
                def _(pe):
                    pe.nop().then_inc(o_turned, 1)
                    pe.nop().then_inc(o_up, 1)
                    pe.nop().then_inc(o_y, 1)

                    def turn(e, b, first):
                        pe.wait_ge(xg_in[b], (e + 2 - b) * 8)
                        for k in range(KD):
                            last = T.transpose(bank(0, 2)[:, k * P:(k + 1) * P], xg[:, b, k * P:(k + 1) * P], ident)
                        last.then_inc(turned, 1)

                    def expert(e, b, first):
                        E13, E2 = WEIGHTS[b]
                        pe.wait_ge(xt_a, e + 1)
                        pe.wait_ge(xt_d, e + 1)
                        pe.wait_ge(up_in[b], (e + 2 - b) * 16)
                        if not first:
                            pe.wait_ge(hid_s, e - 1)
                        up(bank(2 + b), E13, xt[:, b]).then_inc(up_s, 1)
                        turn(e + 1, 1 - b, first)
                        pe.wait_ge(hid_s, e + 1)
                        pe.wait_ge(dn_in[b], (e + 2 - b) * 8)
                        if not (first and e == 0):
                            pe.wait_ge(y_a, e + 0)
                            pe.wait_ge(y_d, e + 0)
                        down(4, hid[:, b], E2).then_inc(y_s, 1)

                        def chunk(q, c):
                            pe.wait_ge(o_in, (q + 1) * 16)
                            pe.wait_ge(o_yc, q + 1)
                            for k in range(KD):
                                last = T.transpose(bank(6, 2)[:, k * P:(k + 1) * P], xg_o[:, k * P:(k + 1) * P], ident)
                            last.then_inc(o_turned, 1)
                            pe.wait_ge(o_xt, q + 1)
                            up(bank(6), E13, xt_o).then_inc(o_up, 1)
                            pe.wait_ge(o_hid, q + 1)
                            down(6, hid_o, E2).then_inc(o_y, 1)
                        further(pe, e, chunk)

                    turn(0, 0, True)
                    loop(pe, expert)

                @block.scalar
                def _(act):
                    act.nop().then_inc(o_out, 16)

                    def copy_x(e, b):
                        act.wait_ge(turned, e + 1)
                        A.copy(xt[:, b, 0:4], bank(0).rearrange("p (k n) -> p k n", k=4)).then_inc(xt_a, 1)

                    def expert(e, b, first):
                        act.wait_ge(up_s, e + 1)
                        if not first:
                            act.wait_ge(hid_s, e - 1)
                        A.activation(gate[:, b], w13_part(2 + b, 0), ACT.Silu).then_inc(silu_s, 1)
                        copy_x(e + 1, 1 - b)
                        act.wait_ge(y_s, e + 1)
                        if not first:
                            act.wait_ge(y_out[b], (e - b) * 16)
                        A.copy(yb[:, b, 0:BANK], bank(4)).then_inc(y_a, 1)

                        def chunk(q, c):
                            act.wait_ge(o_up, q + 2)
                            A.activation(gate_o, w13_part(6, 0), ACT.Silu).then_inc(o_silu, 1)
                            act.wait_ge(o_yc, q + 2)
                            act.dma_start(chunk_rows(q + NE), yb_o).then_inc(o_out, 16)
                        further(act, e, chunk)

                    copy_x(0, 0)
                    loop(act, expert)

                @block.vector
                def _(dve):
                    dve.nop().then_inc(o_yc, 1)

                    def copy_x(e, b):
                        dve.wait_ge(turned, e + 1)
                        V.tensor_copy(xt[:, b, 4:8], bank(1).rearrange("p (k n) -> p k n", k=4)).then_inc(xt_d, 1)

                    def expert(e, b, first):
                        dve.wait_ge(silu_s, e + 1)
                        V.tensor_tensor(hid[:, b], w13_part(2 + b, 1), gate[:, b], ALU.mult).then_inc(hid_s, 1)
                        copy_x(e + 1, 1 - b)
                        dve.wait_ge(y_s, e + 1)
                        if not first:
                            dve.wait_ge(y_out[b], (e - b) * 16)
                        V.tensor_copy(yb[:, b, BANK:D], bank(5)).then_inc(y_d, 1)

                        def chunk(q, c):
                            dve.wait_ge(o_turned, q + 2)
                            V.tensor_copy(xt_o, bank(6, 2).rearrange("p (k n) -> p k n", k=KD)).then_inc(o_xt, 1)
                            dve.wait_ge(o_silu, q + 1)
                            V.tensor_tensor(hid_o, w13_part(6, 1), gate_o, ALU.mult).then_inc(o_hid, 1)
                            dve.wait_ge(o_y, q + 2)
                            dve.wait_ge(o_out, (q + 1) * 16)
                            V.tensor_copy(yb_o, bank(6, 2)).then_inc(o_yc, 1)
                        further(dve, e, chunk)

                    copy_x(0, 0)
                    loop(dve, expert)
                    dve.drain()

        def combine(i):
            g2 = at(BIG, 2, D)
            gb = at(BIG + 2 * D, 2, D)
            yg = at(BIG + 4 * D, 2, 2, D)
            ln_in, g2_in = sem(f"l{i}_ln2in"), sem(f"l{i}_g2in")
            y_in = [sem(f"l{i}_yin{b}") for b in range(2)]
            best, mixed, whole, whole_last = (sem(f"l{i}_{n}") for n in ("best", "mixed", "whole", "wholelast"))
            norm = Norm(f"l{i}_ln2", gb)
            with nc.Block(no_gpsimd_drain=True) as block:
                @block.sync
                def _(sp):
                    for c in range(2):
                        sp.dma_start(g2[:, c, :].rearrange("p (k m) -> p k m", k=KD), mod_row(i, 5, c)).then_inc(g2_in, 16)
                    sp.dma_start(gb[:, 0, :], I["ln2_g"][i].partition_broadcast(P)).then_inc(ln_in, 16)
                    sp.dma_start(gb[:, 1, :], I["ln2_b"][i].partition_broadcast(P)).then_inc(ln_in, 16)
                    if i == DEPTH - 1:
                        for t in range(NT):
                            if t < NT - 1:
                                sp.wait_ge(whole, t + 1)
                            else:
                                sp.wait_ge(whole_last, 1)
                            dst = O["y_prompt"][0] if t == 0 else O["y_sample"][0, (t - 1) * P:t * P, :]
                            store(sp, dst, x[:, t, :])

                @block.gpsimd
                def _(pool):
                    def gather(t):
                        if t >= 2:
                            pool.wait_ge(mixed, t - 1)
                        for k in range(2):
                            pool.indirect_dma_start(out=yg[:, t % 2, k, :], out_offset=None, in_=y_rows,
                                                    in_offset=bass.IndirectOffsetOnAxis(ap=slot_i[:, k, t:t + 1], axis=0)).then_inc(y_in[t % 2], 16)

                    gather(0)
                    gather(1)
                    pool.wait_ge(ln_in, 32)
                    for t in range(NT - 1):
                        if t + 2 < NT:
                            gather(t + 2)
                        norm.late(pool, nc.gpsimd, pchain, t).then_inc(whole, 1)

                @block.scalar
                def _(act):
                    for t in range(NT):
                        act.wait_ge(y_in[t % 2], 32 * (t // 2 + 1))
                        A.mul(yg[:, t % 2, 0, :], yg[:, t % 2, 0, :], gates[:, 0, t:t + 1]).then_inc(best, 1)
                        if t:
                            norm.scalar(act, t - 1)
                    norm.scalar(act, NT - 1)

                @block.vector
                def _(dve):
                    dve.wait_ge(g2_in, 32)
                    for t in range(NT):
                        a, b = yg[:, t % 2, 0, :], yg[:, t % 2, 1, :]
                        dve.wait_ge(best, t + 1)
                        dchain.step(V.scalar_tensor_tensor(a, b, gates[:, 1, t:t + 1], a, ALU.mult, ALU.add))
                        dchain.join(dve)
                        dchain.step(V.tensor_tensor(a, a, g2[:, min(t, 1), :], ALU.mult))
                        dchain.join(dve)
                        V.scalar_tensor_tensor(x[:, t, :], x[:, t, :], ALPHA, a, ALU.mult, ALU.add).then_inc(mixed, 1)
                        dve.wait_ge(mixed, t + 1)
                        norm.vector(dve, t)
                    dve.wait_ge(ln_in, 32)
                    norm.late(dve, V, dchain, NT - 1).then_inc(whole_last, 1)

        up_in, dn_in = [None, None], [None, None]

        def new_weight_sems(i):
            for b in range(2):
                up_in[b], dn_in[b] = sem(f"x{i}_upin{b}"), sem(f"x{i}_dnin{b}")

        setup()
        new_weight_sems(0)
        ht = at(R, KD, TOK)
        stream("ada", [("ada", 0, c) for c in range(4)], None, None, R + KD * TOK)
        finish_modulation("fm0", [(0, 0, 2 * KD)], [])
        modulated("l0_h1", 0, ht, 0, 1)
        rest = [("ada", 0, c) for c in range(4, ADA_CH)] + [("ada", 1, c) for c in range(ADA_CH)]
        jobs = []
        for job in w_jobs(I["ev_w_in"][0], EV_IN):
            jobs += [job] + rest[:3]
            rest = rest[3:]
        stream("ev", jobs + rest, ht, proj, R + KD * TOK)
        finish_modulation("fm1", [(0, 2 * KD, NMOD), (1, 0, NMOD)], list(range(DEPTH)))
        retention()
        mlaT = at(R + 17408, MH // 2, TOK)
        latent_attention(mlaT)
        mix_out("ev_out", 0, I["ev_w_out"][0], [proj[:, :, RG + k * P:RG + (k + 1) * P] for k in range(RH * RDV // P)],
                [mlaT[:, k, :] for k in range(MH // 2)])
        router(0)
        experts(0)
        combine(0)
        recycle_sems()
        new_weight_sems(1)
        modulated("l1_h1", 1, ht, 0, 1)
        pj = at(BIG, NT, OD_IN)
        stream("od", w_jobs(I["od_w_in"][0], OD_IN), ht, pj, R + KD * TOK)
        differential_attention(pj)
        mix_out("od_out", 1, I["od_w_out"][0], [pj[:, :, k * P:(k + 1) * P] for k in range(KD)], [])
        router(1)
        experts(1)
        combine(1)
        with nc.Block(no_gpsimd_drain=True) as block:
            @block.sync
            def _(sp):
                sp.wait_ge(stored, stores[0])


INPUTS = ["x_prompt", "x_sample", "state_ret_fwd", "state_ret_bwd", "cache_mla_ckv", "cache_mla_krope",
          "cache_diff_k", "cache_diff_v", "c", "c_ctx", "ada_w", "ada_b", "ln1_g", "ln1_b", "ln2_g", "ln2_b",
          "ev_w_in", "ev_w_out", "ret_decay_fwd", "ret_decay_bwd", "mla_kv_norm_g", "mla_w_uk", "mla_w_uv",
          "od_w_in", "od_w_out", "diff_lambda", "diff_norm_g", "moe_w_group", "moe_b_group", "moe_w_expert",
          "moe_b_expert", "moe_w1", "moe_w3", "moe_w2"]
OUTPUTS = [("y_prompt", (1, SEQ, D)), ("y_sample", (1, LAT, D)),
           ("new_state_ret_fwd", (1, 1, RH, RDK, RDV)), ("new_state_ret_bwd", (1, 1, RH, RDK, RDV)),
           ("new_cache_mla_ckv", (1, 1, SEQ, MKV)), ("new_cache_mla_krope", (1, 1, SEQ, MR)),
           ("new_cache_diff_k", (1, 1, DH, SEQ, DDV)), ("new_cache_diff_v", (1, 1, DH, SEQ, DDV))]


def kernel(**inputs):
    import concourse.bacc as bacc
    from concourse.bass_utils import run_bass_kernel_spmd

    nc = bacc.Bacc("TRN2", target_bir_lowering=False, num_devices=1)
    arrays = {f"in_{n}": np.ascontiguousarray(inputs[n]) for n in INPUTS}
    consts, rope_mla, rope_diff = constants()
    arrays.update({"in_consts": consts, "in_rope_mla": rope_mla, "in_rope_diff": rope_diff})
    I = {n[3:]: nc.dram_tensor(n, a.shape, F32, kind="ExternalInput").ap() for n, a in arrays.items()}
    O = {n: nc.dram_tensor(f"out_{n}", s, F32, kind="ExternalOutput").ap() for n, s in OUTPUTS}
    build(nc, I, O)
    r = run_bass_kernel_spmd(nc, [arrays], core_ids=[0])
    return tuple(r.results[0][f"out_{n}"] for n, _ in OUTPUTS)
```

```python
import math
from contextlib import ExitStack

import numpy as np
import concourse.bass as bass
from concourse import mybir

F32 = mybir.dt.float32
F32R = mybir.dt.float32r
I32 = mybir.dt.int32
ALU = mybir.AluOpType
ACT = mybir.ActivationFunctionType
AX = mybir.AxisListType

P = 128
D = 1024
KD = D // P
SEQ, LAT, PAST = 128, 512, 128
NT = (SEQ + LAT) // P
TOK = NT * P
NK = NT + 1
KEYS = PAST + LAT
DEPTH = 2
GRID_W = 64
LN_EPS, RMS_EPS = 1e-5, 1e-6
ALPHA = (2.0 * DEPTH) ** 0.25
RH, RDK, RDV, RC = 8, 64, 128, 128
MH, MN, MR, MDV, MKV = 8, 64, 32, 64, 256
MQD = MN + MR
DH, DDH = 8, 64
DDV = 2 * DDH
G, EG = 4, 4
NE = G * EG
FF = 256
EV_W = (RH * RDK, RH * RDK, RH * RDV, RH * RDV, MH * MQD, MKV, MR)
EV_AT = [sum(EV_W[:n]) for n in range(len(EV_W))]
EV_IN = sum(EV_W)
EV_OUT = RH * RDV + MH * MDV
RQ, RK, RV, RG, MQ, CKV, KR = EV_AT
OD_IN = 3 * D
LAM_INIT = 0.8 - 0.6 * math.exp(-0.3)
NMOD = 6 * KD
BANK = 512
ARENA = 53208
R = 27824
ADA_CW = 512
IN_CW = 258
OD_CW = 256
SPLIT = 2 * KD * TOK + 4 * KD * IN_CW
ADA_CH = 6 * D // ADA_CW
FURTHER = 2 * NT
CHUNKS = NE + FURTHER
RET_SCALE = RDK ** -0.5
MLA_SCALE = MQD ** -0.5
DIFF_SCALE = DDH ** -0.5

C_ID, C_ONE, C_REL, C_MASK, C_TRI, C_POS, C_TIE, C_EPS, C_TOK, C_SLOT = 0, 128, 256, 512, 768, 896, 900, 904, 906, 911
C_IOTA = 928
C_N = 1056


def constants():
    i = np.arange(P, dtype=np.float32)
    c = np.zeros((P, C_N), np.float32)
    c[:, C_ID:C_ID + P] = np.eye(P)
    c[:, C_ONE:C_ONE + P] = 1.0
    rel = i[None, :] - i[:, None]
    c[:, C_REL:C_REL + P] = np.maximum(rel, 0)
    c[:, C_REL + P:C_REL + 2 * P] = np.maximum(-rel, 0)
    c[:, C_MASK:C_MASK + P] = (rel >= 0) * RET_SCALE
    c[:, C_MASK + P:C_MASK + 2 * P] = (rel <= 0) * RET_SCALE
    for n, pos in enumerate((i + 1, RC - i, RC - 1 - i, i)):
        c[:, C_POS + n] = pos
    c[:, C_TIE:C_TIE + 4] = np.arange(4, 0, -1)
    c[:, C_EPS], c[:, C_EPS + 1] = LN_EPS, RMS_EPS
    c[:, C_TRI:C_TRI + P] = rel > 0
    c[:, C_TOK:C_TOK + NT] = i[:, None] + P * np.arange(NT)
    c[:, C_SLOT:C_SLOT + NE] = P * np.arange(NE)
    c[:, C_IOTA:C_IOTA + P] = np.arange(P)

    def rope(dim):
        row = np.repeat(np.arange(LAT // GRID_W, dtype=np.float32), GRID_W)
        col = np.tile(np.arange(GRID_W, dtype=np.float32), LAT // GRID_W)
        nf = dim // 4
        inv = np.float32(10000.0) ** (-np.arange(nf, dtype=np.float32) / np.float32(nf))
        ang = np.concatenate([row[:, None] * inv, col[:, None] * inv], -1).astype(np.float32)
        return np.stack([np.cos(ang), np.sin(ang)]).astype(np.float32)

    return c, rope(MR), rope(DDH)


class Chain:

    def __init__(self, sem):
        self.sem, self.n = sem, 0

    def step(self, ins):
        self.n += 1
        ins.then_inc(self.sem, 1)
        return ins

    def join(self, eng):
        eng.wait_ge(self.sem, self.n)


def bc(ap, dim, n):
    a = ap.unsqueeze(dim)
    shape = list(a.shape)
    shape[dim] = n
    return a.to_broadcast(shape)


def build(nc, I, O):
    ctx = ExitStack()
    with ctx:
        arena = ctx.enter_context(nc.sbuf_tensor("arena", [P, R], F32))
        upper_ctx, upper = ctx.enter_context(ExitStack()), {}

        def take_upper(name, split=0):
            upper_ctx.close()
            if split:
                upper["parts"] = upper_ctx.enter_context(nc.sbuf_tensor(f"{name}_parts", [P, split], F32R))
            upper["plain"] = upper_ctx.enter_context(nc.sbuf_tensor(name, [P, ARENA - R - split], F32))
            upper["end"] = ARENA - split

        psum = ctx.enter_context(nc.psum_tensor("psum", [P, 8 * BANK], F32))

        def lasting_sem(name):
            return ctx.enter_context(nc.semaphore(name))

        stage_sems = []

        def sem(name):
            stage_sems.append(nc.alloc_semaphore(name=name))
            return stage_sems[-1]

        def recycle_sems():
            with nc.Block(no_gpsimd_drain=True) as block:
                @block.gpsimd
                def _(pool):
                    nc.clear_and_free_semaphores(stage_sems)
            stage_sems.clear()

        def at(off, *dims):
            n = int(np.prod(dims))
            if off >= R:
                assert off + n <= upper["end"], (off + n, upper["end"])
                v = upper["plain"][:, off - R:off - R + n]
            else:
                v = arena[:, off:off + n]
            return shaped(v, dims)

        def shaped(v, dims):
            if len(dims) == 1:
                return v
            names = "abcd"[:len(dims)]
            return v.rearrange(f"p ({' '.join(names)}) -> p {' '.join(names)}",
                               **{names[i]: dims[i] for i in range(1, len(dims))})

        def parts(off, *dims):
            return shaped(upper["parts"][:, off:off + int(np.prod(dims))], dims)

        def bank(b, n=1):
            return psum[:, b * BANK:(b + n) * BANK]

        off = [0]

        def keep(*dims):
            o = off[0]
            off[0] += int(np.prod(dims))
            return at(o, *dims)

        x = keep(NT, D)
        const = keep(C_N)
        modc = keep(DEPTH, NMOD, 2)
        adab = keep(2, NMOD)
        cond = keep(KD, 32)
        kvg = keep(MKV)
        dng = keep(2)[:, 0:1]
        br = keep(DEPTH, G + NE)
        gates = keep(2, NT)
        slot_i = keep(2, NT).bitcast(I32)
        tables = keep(3, NE).bitcast(I32)
        tok_i = keep(CHUNKS).bitcast(I32)
        lam = keep(4)
        small = keep(64)
        BIG = off[0]
        proj = at(BIG, NT, EV_IN)
        assert BIG + NT * EV_IN <= R, BIG
        ident = const[:, C_ID:C_ID + P]
        ones = const[:, C_ONE:C_ONE + P]
        mod_rows = nc.dram_tensor("mod_rows", (DEPTH, 2 * NMOD, P), F32).ap()
        h2_rows = nc.dram_tensor("h2_rows", (TOK, D), F32).ap()
        zero_row = nc.dram_tensor("zero_row", (D,), F32).ap()
        y_rows = nc.dram_tensor("y_rows", (CHUNKS * P, D), F32).ap()
        eps_ln, eps_rms = const[:, C_EPS:C_EPS + 1], const[:, C_EPS + 1:C_EPS + 2]

        dchain, achain, pchain = Chain(lasting_sem("vector_step")), Chain(lasting_sem("scalar_step")), Chain(lasting_sem("pool_step"))
        stored = lasting_sem("stored")
        stores = [0]

        def store(eng, out, in_):
            eng.dma_start(out, in_).then_inc(stored, 16)
            stores[0] += 16

        V, A, T = nc.vector, nc.scalar, nc.tensor

        further_zero, x_in, zeros_out = (lasting_sem(n) for n in ("further_chunks_zero", "x_and_gains_loaded", "zero_row_stored"))

        def ada_raw(b):
            return at(R + KD * IN_CW + b * (KD // 2) * ADA_CW, KD // 2, ADA_CW)

        def ada_source(i, c, half):
            return I["ada_w"][i].rearrange("(h k p) n -> h p k n", p=P, k=KD // 2)[half, :, :, c * ADA_CW:(c + 1) * ADA_CW]

        FIRST_ADA = [("ada", 0, c, half) for c in range(4) for half in range(2)]
        first_ada_in = [sem(f"first_ada{a}") for a in range(len(FIRST_ADA))]

        def setup():
            rows_in = sem("rows_loaded")
            rows_t, cond_done, zeroed = sem("rows_transposed"), sem("cond_done"), sem("zeroed")
            nil = at(BIG + 3 * P, P)
            crow = at(BIG, P)
            brow = at(BIG + P, 2, P)
            with nc.Block(no_gpsimd_drain=True) as block:
                @block.sync
                def _(sp):
                    sp.dma_start(const, I["consts"]).then_inc(rows_in, 16)
                    sp.dma_start(crow[0:KD, :], I["c_ctx"].rearrange("(k p) -> k p", p=P)).then_inc(rows_in, 16)
                    sp.dma_start(crow[KD:2 * KD, :], I["c"].rearrange("a (k p) -> (a k) p", p=P)).then_inc(rows_in, 16)
                    sp.dma_start(brow[0:NMOD, :, :], I["ada_b"].rearrange("i (k p) -> k i p", p=P)).then_inc(rows_in, 16)
                    for a, (_, i, c, half) in enumerate(FIRST_ADA):
                        sp.dma_start(ada_raw(a), ada_source(i, c, half)).then_inc(first_ada_in[a], 16)
                    sp.wait_ge(zeroed, 2)
                    sp.dma_start(zero_row.rearrange("(a b) -> a b", b=P), nil[0:KD, :]).then_inc(zeros_out, 16)

                @block.gpsimd
                def _(pool):
                    pool.dma_start(x[:, 0, :], I["x_prompt"].rearrange("a p d -> p (a d)")).then_inc(x_in, 16)
                    pool.dma_start(x[:, 1:NT, :], I["x_sample"].rearrange("a (t p) d -> p (a t) d", p=P)).then_inc(x_in, 16)
                    pool.dma_start(kvg, I["mla_kv_norm_g"][0].partition_broadcast(P)).then_inc(x_in, 16)
                    pool.dma_start(dng, I["diff_norm_g"][0].rearrange("(p o) -> p o", o=1)).then_inc(x_in, 16)
                    for i in range(DEPTH):
                        pool.dma_start(br[:, i, 0:G], I["moe_b_group"][i].partition_broadcast(P)).then_inc(x_in, 16)
                        pool.dma_start(br[:, i, G:], I["moe_b_expert"][i].partition_broadcast(P)).then_inc(x_in, 16)

                @block.vector
                def _(dve):
                    V.memset(nil, 0.0).then_inc(zeroed, 1)
                    V.memset(cond, 0.0).then_inc(zeroed, 1)

                @block.tensor
                def _(pe):
                    pe.wait_ge(rows_in, 64)
                    T.transpose(bank(0)[:, 0:2 * KD], crow[0:2 * KD, :], ident[0:2 * KD, 0:2 * KD])
                    for i in range(DEPTH):
                        T.transpose(bank(0)[:, 64 + i * 64:64 + i * 64 + NMOD], brow[0:NMOD, i, :],
                                    ident[0:NMOD, 0:NMOD]).then_inc(rows_t, 1)

                @block.scalar
                def _(act):
                    act.wait_ge(rows_t, DEPTH)
                    act.wait_ge(zeroed, 2)
                    A.activation(cond[:, :, 0:2].rearrange("p k c -> p c k"), bank(0)[:, 0:2 * KD].rearrange("p (c k) -> p c k", c=2),
                                 ACT.Silu).then_inc(cond_done, 1)
                    for i in range(DEPTH):
                        A.activation(adab[:, i, :], bank(0)[:, 64 + i * 64:64 + i * 64 + NMOD], ACT.Copy)
                    act.drain()

        def whole(ap):
            return ap.bitcast(F32)

        SIDES = ((slice(0, P), 0), (slice(P, TOK), 1))

        W_FIRST = at(R - KD * IN_CW, KD * IN_CW)

        def chunk_of_k(buf, cw):
            return buf[:, 0:KD * cw].rearrange("p (k n) -> p k n", k=KD)

        def w_part(w, n, cw):
            return chunk_of_k(parts(2 * KD * TOK + (2 * (w % 2) + n) * KD * IN_CW, KD * IN_CW), cw)

        def modulated(name, i, halves, sh, sc, w, cw):
            tr, ev_a, ev_d, high = (sem(f"{name}_{n}") for n in ("tr", "eva", "evd", "high"))
            hi, lo = halves
            full = at(R, KD, TOK)
            first_in, first_high = sem(f"{name}_firstin"), sem(f"{name}_firsthigh")
            with nc.Block(no_gpsimd_drain=True) as block:
                @block.sync
                def _(sp):
                    sp.dma_start(chunk_of_k(W_FIRST, cw), w.rearrange("(k p) n -> p k n", p=P)[:, :, 0:cw]).then_inc(first_in, 16)

                @block.tensor
                def _(pe):
                    for k in range(KD):
                        if k >= 4:
                            pe.wait_ge((ev_a, ev_d)[k % 2], 2 * ((k - 4) // 2 + 1))
                        for t in range(NT):
                            last = T.transpose(bank(2 * (k % 4), 2)[:, t * P:(t + 1) * P], x[:, t, k * P:(k + 1) * P], ident)
                        last.then_inc(tr, 1)

                @block.scalar
                def _(act):
                    for k in range(KD):
                        if k % 2 == 0:
                            act.wait_ge(tr, k + 1)
                            src = bank(2 * (k % 4), 2)
                            for cols, c in SIDES:
                                A.activation(full[:, k, cols], src[:, cols], ACT.Identity, bias=modc[:, i, sh * KD + k, c:c + 1],
                                             scale=modc[:, i, sc * KD + k, c:c + 1]).then_inc(ev_a, 1)
                        act.wait_ge((ev_a, ev_d)[k % 2], 2 * (k // 2 + 1))
                        A.copy(hi[:, k, :], full[:, k, :]).then_inc(high, 1)
                        if k == 2:
                            act.wait_ge(first_in, 16)
                            A.copy(w_part(0, 0, cw), chunk_of_k(W_FIRST, cw)).then_inc(first_high, 1)

                @block.gpsimd
                def _(pool):
                    pool.wait_ge(first_high, 1)
                    nc.gpsimd.tensor_tensor(w_part(0, 1, cw), chunk_of_k(W_FIRST, cw), whole(w_part(0, 0, cw)), ALU.subtract)
                    pool.drain()

                @block.vector
                def _(dve):
                    for k in range(KD):
                        if k % 2:
                            dve.wait_ge(tr, k + 1)
                            src = bank(2 * (k % 4), 2)
                            for cols, c in SIDES:
                                V.tensor_scalar(full[:, k, cols], src[:, cols], modc[:, i, sc * KD + k, c:c + 1],
                                                modc[:, i, sh * KD + k, c:c + 1], ALU.mult, ALU.add).then_inc(ev_d, 1)
                        if k:
                            dve.wait_ge(high, k)
                            V.tensor_tensor(lo[:, k - 1, :], full[:, k - 1, :], whole(hi[:, k - 1, :]), ALU.subtract)
                    dve.wait_ge(high, KD)
                    V.tensor_tensor(lo[:, KD - 1, :], full[:, KD - 1, :], whole(hi[:, KD - 1, :]), ALU.subtract)
                    dve.drain()

        def stream(name, jobs, ht, dst, zeros=False, rotate=None):
            HK = KD // 2
            w_at = [n for n, j in enumerate(jobs) if j[0] == "w" and j[5][0] == 0]
            first = jobs is FIRST_ADA
            NA = len(FIRST_ADA) if first else 2
            CB = KD * IN_CW
            w_raw = at(R, CB)
            a_raw = [ada_raw(b) for b in range(NA)]
            part = at(R + CB + NA * HK * ADA_CW, ADA_CW)
            w_in = sem(f"{name}_win")
            a_in = first_ada_in if first else [sem(f"{name}_ain{b}") for b in range(NA)]
            used_a, group, ev_a, ev_d = (sem(f"{name}_{n}") for n in ("useda", "group", "eva", "evd"))
            copied, turned, added, high, low = (sem(f"{name}_{n}") for n in ("acopied", "aturned", "aadded", "high", "low"))
            rope_in = sem(f"{name}_ropein")

            def w_parts(w, cw):
                return [w_part(w, n, cw) for n in range(2)]

            W_BANKS = 6
            sums, turns = bank(6), bank(7)
            upto = [sum(j[0] == "ada" for j in jobs[:n + 1]) for n in range(len(jobs))]

            def groups(job, first):
                return [g for g in (NT * job[4] + t for t in job[5]) if g % 2 == first]

            def next_chunk(n):
                return [w + 1 for w in range(len(w_at) - 1) if w_at[w] == n]

            with nc.Block(no_gpsimd_drain=True) as block:
                @block.sync
                def _(sp):
                    def load_w(w):
                        _, m, n0, cw, _, _ = jobs[w_at[w]]
                        if w >= 2:
                            sp.wait_ge(low, w - 1)
                        sp.dma_start(chunk_of_k(w_raw, cw), m.rearrange("(k p) n -> p k n", p=P)[:, :, n0:n0 + cw]).then_inc(w_in, 16)

                    if rotate:
                        sp.dma_start(rotate[0], I["rope_diff"].rearrange("a (t p) n -> p a t n", p=P)).then_inc(rope_in, 16)
                    for n, job in enumerate(jobs):
                        if job[0] == "w":
                            for w in next_chunk(n):
                                load_w(w)
                            continue
                        if first:
                            continue
                        _, i, c, half = job
                        a = upto[n] - 1
                        if a >= NA:
                            sp.wait_ge(used_a, a - NA + 1)
                        sp.dma_start(a_raw[a % NA], ada_source(i, c, half)).then_inc(a_in[a % NA], 16)
                    if zeros:
                        sp.dma_start(y_rows[NE * P:, :], zero_row.partition_broadcast(FURTHER * P)
                                     ).then_inc(further_zero, 16)

                @block.tensor
                def _(pe):
                    def turn(n):
                        a = upto[n] // 2
                        pe.wait_ge(copied, a)
                        if a > 1:
                            pe.wait_ge(added, a - 1)
                        for q in range(4):
                            last = T.transpose(turns[:, q * P:(q + 1) * P], part[:, q * P:(q + 1) * P], ident)
                        last.then_inc(turned, 1)

                    for n, job in enumerate(jobs):
                        if job[0] == "w":
                            _, _, _, cw, w, tiles = job
                            if w:
                                pe.wait_ge(high, w)
                                pe.wait_ge(low, w)
                            w_h, w_l = w_parts(w, cw)
                            for t in tiles:
                                g = NT * w + t
                                if g >= W_BANKS:
                                    pe.wait_ge((ev_a, ev_d)[g % 2], (g - W_BANKS) // 2 + 1)
                                for k in range(KD):
                                    x_h, x_l = (p[:, k, t * P:(t + 1) * P] for p in ht)
                                    for m, (a, b) in enumerate(((x_h, w_h), (x_h, w_l), (x_l, w_h))):
                                        last = T.matmul(bank(g % W_BANKS)[:, 0:cw], a, b[:, k], start=(k == 0 and m == 0),
                                                        stop=(k == KD - 1 and m == 2))
                                last.then_inc(group, 1)
                        else:
                            a, half = upto[n], job[3]
                            pe.wait_ge(a_in[(a - 1) % NA], 16 * ((a - 1) // NA + 1))
                            if half == 0 and a > 1:
                                pe.wait_ge(copied, (a - 1) // 2)
                            for k in range(HK):
                                last = T.matmul(sums[32 * k:32 * k + 32, :], cond[:, half * HK + k, :], a_raw[(a - 1) % NA][:, k],
                                                start=(half == 0), stop=(half == 1))
                            last.then_inc(used_a, 1)
                        if n and jobs[n - 1][0] == "ada" and jobs[n - 1][3] == 1:
                            turn(n - 1)
                    if jobs[-1][0] == "ada":
                        turn(len(jobs) - 1)

                def split_high(act, w):
                    cw = jobs[w_at[w]][3]
                    act.wait_ge(w_in, 16 * w)
                    if w >= 2:
                        act.wait_ge(group, NT * (w - 1))
                    A.copy(w_parts(w, cw)[0], chunk_of_k(w_raw, cw)).then_inc(high, 1)

                def split_low(dve, w):
                    cw = jobs[w_at[w]][3]
                    hi, lo = w_parts(w, cw)
                    dve.wait_ge(high, w)
                    V.tensor_tensor(lo, chunk_of_k(w_raw, cw), whole(hi), ALU.subtract).then_inc(low, 1)

                @block.scalar
                def _(act):
                    for n, job in enumerate(jobs):
                        if job[0] == "w":
                            _, _, n0, cw, _, _ = job
                            for w in next_chunk(n):
                                split_high(act, w)
                            for g in groups(job, 0):
                                act.wait_ge(group, g + 1)
                                A.copy(dst[:, g % NT, n0:n0 + cw], bank(g % W_BANKS)[:, 0:cw]).then_inc(ev_a, 1)
                        elif job[3] == 1:
                            a = upto[n] // 2
                            act.wait_ge(used_a, 2 * a)
                            if a > 1:
                                act.wait_ge(turned, a - 1)
                            A.copy(part, sums).then_inc(copied, 1)
                    act.drain()

                @block.vector
                def _(dve):
                    def add(n):
                        _, i, c, _ = jobs[n]
                        dve.wait_ge(turned, upto[n] // 2)
                        V.tensor_reduce(modc[:, i, 4 * c:4 * c + 4, :],
                                        turns.rearrange("p (q j m) -> p q m j", q=4, j=4)[:, :, 0:2, :],
                                        AX.X, ALU.add).then_inc(added, 1)

                    def rope(table, tmp, xs):
                        if not rotated:
                            dve.wait_ge(rope_in, 16)
                        rotated.append(1)
                        H2 = xs.shape[-1] // 2
                        x1, x2 = xs[:, :, :, 0:H2], xs[:, :, :, H2:]
                        cs = [bc(table[:, s], 2, xs.shape[2]) for s in range(2)]
                        for n, (src, s) in enumerate(((x1, 0), (x2, 1), (x1, 1), (x2, 0))):
                            dchain.step(V.tensor_tensor(tmp[:, n], src, cs[s], ALU.mult))
                        dchain.join(dve)
                        dchain.step(V.tensor_tensor(x1, tmp[:, 0], tmp[:, 1], ALU.subtract))
                        dchain.step(V.tensor_tensor(x2, tmp[:, 2], tmp[:, 3], ALU.add))
                        dchain.join(dve)

                    rotated = []
                    for n, job in enumerate(jobs):
                        if job[0] == "w":
                            _, _, n0, cw, _, _ = job
                            for w in next_chunk(n):
                                split_low(dve, w)
                            for g in groups(job, 1):
                                dve.wait_ge(group, g + 1)
                                V.tensor_copy(dst[:, g % NT, n0:n0 + cw], bank(g % W_BANKS)[:, 0:cw]).then_inc(ev_d, 1)
                            w = job[4]
                            if rotate and job[5][0] == 2 and 0 < w <= len(rotate[1]):
                                dve.wait_ge(ev_a, (NT * w + 1) // 2)
                                dve.wait_ge(ev_d, NT * w // 2)
                                rope(rotate[0], rotate[2], rotate[1][w - 1])
                        if n and jobs[n - 1][0] == "ada" and jobs[n - 1][3] == 1:
                            add(n - 1)
                    if jobs[-1][0] == "ada":
                        add(len(jobs) - 1)
                    dve.drain()

        def w_jobs(w, width, cw):
            return [[("w", w, c, cw, c // cw, tiles) for tiles in ((0, 1), (2, 3), (4,))] for c in range(0, width, cw)]

        def finish_modulation(name, spans, rows_of):
            biased, turned, copied, out_in = (sem(f"{name}_{n}") for n in ("biased", "turned", "copied", "out"))
            rowbuf = at(R, DEPTH, P)
            with nc.Block(no_gpsimd_drain=True) as block:
                @block.vector
                def _(dve):
                    for i, a, b in spans:
                        dchain.step(V.tensor_tensor(modc[:, i, a:b, :], modc[:, i, a:b, :], bc(adab[:, i, a:b], 2, 2), ALU.add))
                    dchain.join(dve)
                    for i, a, b in spans:
                        for s in (1, 4):
                            if a <= s * KD < b:
                                m = modc[:, i, s * KD:(s + 1) * KD, :]
                                dchain.step(V.tensor_scalar(m, m, 1.0, None, ALU.add))
                    dchain.join(dve)
                    dve.drain().then_inc(biased, 1)

                if not rows_of:
                    @block.sync
                    def _(sp):
                        sp.wait_ge(x_in, 16 * (4 + 2 * DEPTH))
                        sp.wait_ge(zeros_out, 16)

                if rows_of:
                    @block.tensor
                    def _(pe):
                        pe.wait_ge(biased, 1)
                        for i in rows_of:
                            T.transpose(bank(i)[0:2 * NMOD, 0:P], modc[:, i].rearrange("p n c -> p (n c)"), ident).then_inc(turned, 1)

                    @block.scalar
                    def _(act):
                        for n, i in enumerate(rows_of):
                            act.wait_ge(turned, n + 1)
                            A.copy(rowbuf[0:2 * NMOD, i, :], bank(i)[0:2 * NMOD, 0:P]).then_inc(copied, 1)

                    @block.sync
                    def _(sp):
                        for n, i in enumerate(rows_of):
                            sp.wait_ge(copied, n + 1)
                            sp.dma_start(mod_rows[i], rowbuf[0:2 * NMOD, i, :]).then_inc(out_in, 16)
                        sp.wait_ge(further_zero, 16)
                        sp.wait_ge(out_in, 16 * len(rows_of))

        def mod_row(i, v, c):
            return mod_rows[i].rearrange("(v k c) m -> v c k m", v=6, c=2)[v, c].partition_broadcast(P)

        class Norm:

            def __init__(self, name, gb):
                self.var, self.root, self.flat = sem(f"{name}_var"), sem(f"{name}_root"), sem(f"{name}_flat")
                self.g, self.b = gb[:, 0, :], gb[:, 1, :]
                self.scaled = sem(f"{name}_scaled")
                self.stats, self.mv, self.rt = small[:, 0:12], small[:, 16:16 + 2 * NT], small[:, 28:28 + 3 * NT]

            def statistics(self, dve, t):
                dchain.join(dve)
                for h in range(2):
                    dchain.step(V.bn_stats(self.stats[:, 6 * h:6 * h + 6], x[:, t, h * BANK:(h + 1) * BANK]))
                dchain.join(dve)
                V.bn_aggr(self.mv[:, 2 * t:2 * t + 2], self.stats).then_inc(self.var, 1)

            def scales(self, dve, t):
                mean, (dev, inv, shift) = self.mv[:, 2 * t:2 * t + 1], (self.rt[:, 3 * t + n:3 * t + n + 1] for n in range(3))
                dve.wait_ge(self.root, t + 1)
                dchain.step(V.reciprocal(inv, dev))
                dchain.join(dve)
                V.tensor_scalar(shift, mean, inv, -1.0, ALU.mult, ALU.mult).then_inc(self.scaled, 1)

            def root_of(self, act, t):
                act.wait_ge(self.var, t + 1)
                A.activation(self.rt[:, 3 * t:3 * t + 1], self.mv[:, 2 * t + 1:2 * t + 2], ACT.Sqrt, bias=eps_ln).then_inc(self.root, 1)

            def normalise(self, act, t):
                act.wait_ge(self.scaled, t + 1)
                A.activation(x[:, t, :], x[:, t, :], ACT.Identity, bias=self.rt[:, 3 * t + 2:3 * t + 3],
                             scale=self.rt[:, 3 * t + 1:3 * t + 2]).then_inc(self.flat, 1)

            def late(self, eng, math, chain, t):
                eng.wait_ge(self.flat, t + 1)
                chain.step(math.tensor_tensor(x[:, t, :], x[:, t, :], self.g, ALU.mult))
                chain.join(eng)
                return math.tensor_tensor(x[:, t, :], x[:, t, :], self.b, ALU.add)

        WOUT, HT2 = R + KD * TOK, R + 19968
        EXP_A = BIG + NT * EV_IN - 6144 - 160
        W_EXP = 2 * KD * FF + 2 * D

        def expert_weights(o):
            return [at(o + m * KD * FF, KD, FF) for m in range(2)], at(o + 2 * KD * FF, 2, D)

        WEIGHTS_AT = [EXP_A, R]

        def mix_out(name, i, w, srcs, direct, gain=1.0):
            ks, kt = len(srcs), len(srcs) + len(direct)
            catT = at(R, ks, TOK)
            feats = [catT[:, k, :] for k in range(ks)] + direct
            wout = at(WOUT, kt, D)
            w_in = [[sem(f"{name}_win{j}{q}") for q in range(2)] for j in range(2)]
            HT = kt // 2
            tr, ev_a, ev_d = (sem(f"{name}_{n}") for n in ("tr", "eva", "evd"))
            wv = w.rearrange("(k p) n -> p k n", p=P)
            with nc.Block(no_gpsimd_drain=True) as block:
                @block.sync
                def _(sp):
                    for j in range(2):
                        for q in range(2):
                            ks_, ns = slice(q * HT, (q + 1) * HT), slice(j * BANK, (j + 1) * BANK)
                            sp.dma_start(wout[:, ks_, ns], wv[:, ks_, ns]).then_inc(w_in[j][q], 16)

                @block.tensor
                def _(pe):
                    for k in range(ks):
                        if k >= 4:
                            pe.wait_ge((ev_a, ev_d)[k % 2], (k - 4) // 2 + 1)
                        for t in range(NT):
                            last = T.transpose(bank(2 * (k % 4), 2)[:, t * P:(t + 1) * P], srcs[k][:, t, :], ident)
                        last.then_inc(tr, 1)

                @block.scalar
                def _(act):
                    for k in range(0, ks, 2):
                        act.wait_ge(tr, k + 1)
                        A.mul(catT[:, k, :], bank(2 * (k % 4), 2)[:, 0:TOK], gain).then_inc(ev_a, 1)
                    act.drain()

                @block.vector
                def _(dve):
                    for k in range(1, ks, 2):
                        dve.wait_ge(tr, k + 1)
                        V.tensor_scalar(catT[:, k, :], bank(2 * (k % 4), 2)[:, 0:TOK], gain, None, ALU.mult).then_inc(ev_d, 1)
                    dve.drain()

            g1, sc2, sh2, gb, h2 = (at(BIG + 2 * D * n, 2, D) for n in range(5))
            wrt = at(BIG + 10 * D, KD, P)
            tmp = at(BIG + 11 * D, 2, BANK)
            htt = at(HT2, 2, KD, P)
            half, gated, h2_done, stored_h2 = (sem(f"{name}_{n}") for n in ("half", "gated", "h2", "h2st"))
            g1_in, ln_in, mod_in, wr_zero, wr_in = (sem(f"{name}_{n}") for n in ("g1in", "lnin", "modin", "wrz", "wrin"))
            turned, t_copied, logit = (sem(f"{name}_{n}") for n in ("turned", "tcopied", "logit"))
            norm = Norm(f"{name}_ln", gb)
            E13, E2 = expert_weights(WEIGHTS_AT[0])

            with nc.Block(no_gpsimd_drain=True) as block:
                @block.sync
                def _(sp):
                    for c in range(2):
                        sp.dma_start(g1[:, c, :].rearrange("p (k m) -> p k m", k=KD), mod_row(i, 2, c)).then_inc(g1_in, 16)
                    sp.dma_start(gb[:, 0, :], I["ln1_g"][i].partition_broadcast(P)).then_inc(ln_in, 16)
                    sp.dma_start(gb[:, 1, :], I["ln1_b"][i].partition_broadcast(P)).then_inc(ln_in, 16)
                    for c in range(2):
                        sp.dma_start(sh2[:, c, :].rearrange("p (k m) -> p k m", k=KD), mod_row(i, 3, c)).then_inc(mod_in, 16)
                        sp.dma_start(sc2[:, c, :].rearrange("p (k m) -> p k m", k=KD), mod_row(i, 4, c)).then_inc(mod_in, 16)
                    sp.wait_ge(wr_zero, 1)
                    sp.dma_start(wrt[:, :, 0:G], I["moe_w_group"][i].rearrange("(k p) n -> p k n", p=P)).then_inc(wr_in, 16)
                    sp.dma_start(wrt[:, :, G:G + NE], I["moe_w_expert"][i].rearrange("(k p) n -> p k n", p=P)).then_inc(wr_in, 16)
                    sp.dma_start(E13[0], I["moe_w1"][i, 0].rearrange("(k p) f -> p k f", p=P)).then_inc(up_in[0], 16)
                    sp.dma_start(E13[1], I["moe_w3"][i, 0].rearrange("(k p) f -> p k f", p=P)).then_inc(up_in[0], 16)
                    sp.dma_start(E2, I["moe_w2"][i, 0].rearrange("(f p) n -> p f n", p=P)).then_inc(dn_in[0], 16)
                    for t in range(NT):
                        sp.wait_ge(h2_done, t + 1)
                        sp.dma_start(h2_rows[t * P:(t + 1) * P, :], h2[:, t % 2, :]).then_inc(stored_h2, 16)
                        sp.wait_ge(stored_h2, 16 * (t + 1))

                @block.tensor
                def _(pe):
                    def heads(t):
                        for j in range(2):
                            g = 2 * t + j
                            if g >= 4:
                                pe.wait_ge(gated, g - 3)
                            for k in range(kt):
                                if t == 0 and k % HT == 0:
                                    pe.wait_ge(w_in[j][k // HT], 16)
                                last = T.matmul(bank(g % 4), feats[k][:, t * P:(t + 1) * P],
                                                wout[:, k, j * BANK:(j + 1) * BANK], start=(k == 0), stop=(k == kt - 1))
                            last.then_inc(half, 1)

                    def turn(t):
                        pe.wait_ge(h2_done, t + 1)
                        if t:
                            pe.wait_ge(t_copied, t)
                        for k in range(KD):
                            last = T.transpose(bank(4, 2)[:, k * P:(k + 1) * P], h2[:, t % 2, k * P:(k + 1) * P], ident)
                        last.then_inc(turned, 1)

                    def route(t):
                        pe.wait_ge(t_copied, t + 1)
                        if t == 0:
                            pe.wait_ge(wr_in, 32)
                        for k in range(KD):
                            last = T.matmul(bank(6, 2)[:, t * P:(t + 1) * P], htt[:, t % 2, k, :], wrt[:, k, :],
                                            start=(k == 0), stop=(k == KD - 1))
                        last.then_inc(logit, 1)

                    for t in range(NT):
                        heads(t)
                        if t >= 1:
                            turn(t - 1)
                        if t >= 2:
                            route(t - 2)
                    route(NT - 2)
                    turn(NT - 1)
                    route(NT - 1)

                @block.scalar
                def _(act):
                    def copy(t):
                        act.wait_ge(turned, t + 1)
                        if t >= 2:
                            act.wait_ge(logit, t - 1)
                        A.copy(htt[:, t % 2], bank(4, 2).rearrange("p (k n) -> p k n", k=KD)).then_inc(t_copied, 1)

                    for t in range(NT + 1):
                        if t:
                            copy(t - 1)
                        if t < NT:
                            norm.root_of(act, t)
                            norm.normalise(act, t)

                @block.gpsimd
                def _(pool):
                    nc.gpsimd.memset(wrt, 0.0).then_inc(wr_zero, 1)
                    pool.wait_ge(ln_in, 32)
                    for t in range(NT):
                        pool.wait_ge(h2_done, t + 1)
                        pchain.step(norm.late(pool, nc.gpsimd, pchain, t))
                    pool.drain()

                @block.vector
                def _(dve):
                    def modulate(t):
                        c = min(t, 1)
                        dve.wait_ge(norm.flat, t + 1)
                        if t >= 2:
                            dve.wait_ge(stored_h2, 16 * (t - 1))
                            dve.wait_ge(turned, t - 1)
                        dchain.step(V.tensor_tensor(h2[:, t % 2, :], x[:, t, :], sc2[:, c, :], ALU.mult))
                        dchain.join(dve)
                        V.tensor_tensor(h2[:, t % 2, :], h2[:, t % 2, :], sh2[:, c, :], ALU.add).then_inc(h2_done, 1)

                    dve.wait_ge(ln_in, 32)
                    dve.wait_ge(mod_in, 64)
                    for c in range(2):
                        dchain.step(V.tensor_tensor(h2[:, c, :], gb[:, 1, :], sc2[:, c, :], ALU.mult))
                    dchain.join(dve)
                    dchain.step(V.tensor_tensor(sh2, sh2, h2, ALU.add))
                    dchain.step(V.tensor_tensor(sc2, sc2, bc(gb[:, 0, :], 1, 2), ALU.mult))
                    dchain.join(dve)
                    dve.wait_ge(g1_in, 32)
                    for t in range(NT):
                        for j in range(2):
                            g = 2 * t + j
                            dve.wait_ge(half, g + 1)
                            V.tensor_tensor(tmp[:, j, :], bank(g % 4), g1[:, min(t, 1), j * BANK:(j + 1) * BANK],
                                            ALU.mult).then_inc(gated, 1)
                            dve.wait_ge(gated, g + 1)
                            dchain.step(V.scalar_tensor_tensor(x[:, t, j * BANK:(j + 1) * BANK], x[:, t, j * BANK:(j + 1) * BANK],
                                                               ALPHA, tmp[:, j, :], ALU.mult, ALU.add))
                        norm.statistics(dve, t)
                        norm.scales(dve, t)
                        modulate(t)

        def retention():
            o = R
            dt = at(o, RH, P); o += RH * P
            tab = at(o, 2, 2, RH); o += 4 * RH
            lg = at(o, 2, RH); o += 2 * RH
            cd = at(o, RH); o += RH
            tl = at(o, 8, 2 * RH); o += 16 * RH
            st = at(o, NT - 1, RH, RDV); o += (NT - 1) * RH * RDV
            kv = at(o, NT, RH, RDV); o += NT * RH * RDV
            qq = at(o, NT - 1, RH, 2, RDK); o += (NT - 1) * RH * 2 * RDK
            SH = o
            kk = at(o, NT, RH, 2, RDK); o += NT * RH * 2 * RDK
            ex = at(o, 2, RH, P); o += 2 * RH * P
            assert o <= ARENA, o
            qv = proj[:, :, RQ:RQ + RH * RDK].rearrange("p t (h d) -> p t h d", h=RH)
            kvw = proj[:, :, RK:RK + RH * RDK].rearrange("p t (h d) -> p t h d", h=RH)
            dec_in, st_in = sem("dec_in"), sem("state_in")
            dv, ac = sem("decay_v"), sem("decay_a")
            kk_done, kv_done, kv_out = sem("kk_done"), sem("kv_done"), sem("kv_copied")
            with nc.Block(no_gpsimd_drain=True) as block:
                @block.sync
                def _(sp):
                    sp.dma_start(tl[:, 0, 0:RH], I["ret_decay_fwd"][0].partition_broadcast(P)).then_inc(dec_in, 16)
                    sp.dma_start(tl[:, 0, RH:2 * RH], I["ret_decay_bwd"][0].partition_broadcast(P)).then_inc(dec_in, 16)
                    sp.dma_start(st[0:RDK, 0], I["state_ret_fwd"][0, 0].rearrange("h k v -> k h v")).then_inc(st_in, 16)
                    sp.dma_start(st[RDK:P, NT - 2], I["state_ret_bwd"][0, 0].rearrange("h k v -> k h v")).then_inc(st_in, 16)
                    sp.wait_ge(kv_out, 1)
                    store(sp, O["new_state_ret_fwd"][0, 0].rearrange("h k v -> k h v"), kv[0:RDK, 0])
                    store(sp, O["new_state_ret_bwd"][0, 0].rearrange("h k v -> k h v"), kv[RDK:P, 0])

                @block.vector
                def _(dve):
                    X, AXX, E, U, Dd, Rr, L, Mn = (tl[:, n, :] for n in range(8))
                    lgf = lg.rearrange("p a h -> p (a h)")
                    dve.wait_ge(dec_in, 32)
                    V.scalar_tensor_tensor(AXX, X, -1.0, X, ALU.mult, ALU.max).then_inc(dv, 1)
                    dve.wait_ge(ac, 1)
                    V.tensor_scalar(U, E, 1.0, None, ALU.add).then_inc(dv, 1)
                    dve.wait_ge(dv, 2)
                    dchain.step(V.tensor_scalar(Dd, U, 1.0, None, ALU.subtract))
                    dchain.step(V.tensor_scalar(Mn, X, 0.0, None, ALU.min))
                    dchain.join(dve)
                    dchain.step(V.tensor_tensor(Rr, E, Dd, ALU.subtract))
                    dchain.step(V.reciprocal(AXX, U))
                    dchain.join(dve)
                    dchain.step(V.tensor_tensor(Rr, Rr, AXX, ALU.mult))
                    dchain.join(dve)
                    dve.wait_ge(ac, 2)
                    dchain.step(V.tensor_tensor(L, L, Rr, ALU.add))
                    dchain.join(dve)
                    dchain.step(V.tensor_tensor(lgf, Mn, L, ALU.subtract))
                    dchain.join(dve)
                    for qk in range(2):
                        for d in range(2):
                            n = C_POS + 2 * qk + d
                            dchain.step(V.tensor_scalar(tab[:, qk, d, :], lg[:, d, :], const[:, n:n + 1], None, ALU.mult))
                    dchain.step(V.tensor_scalar(cd[0:RDK, :], lg[0:RDK, 0, :], float(RC), None, ALU.mult))
                    V.tensor_scalar(cd[RDK:P, :], lg[RDK:P, 1, :], float(RC), None, ALU.mult).then_inc(dv, 1)
                    dve.wait_ge(ac, 4)
                    dchain.step(V.tensor_scalar(tab[:, 1], tab[:, 1], RET_SCALE, None, ALU.mult))
                    dchain.join(dve)
                    for t in range(NT):
                        V.tensor_tensor(kk[:, t], bc(kvw[:, t], 2, 2), bc(tab[:, 1].rearrange("p d h -> p h d"), 3, RDK),
                                        ALU.mult).then_inc(kk_done, 1)
                    dve.wait_ge(ac, 4 + 2 * RH)
                    for d in range(2):
                        dchain.step(V.tensor_tensor(ex[:, d], ex[:, d], bc(const[:, C_MASK + d * P:C_MASK + (d + 1) * P], 1, RH), ALU.mult))
                    dchain.join(dve)
                    dchain.step(V.tensor_tensor(dt, ex[:, 0], ex[:, 1], ALU.add))
                    dve.wait_ge(st_in, 32)
                    dve.wait_ge(kv_out, NT)
                    for n in range(NT - 2):
                        f, b = n, NT - 2 - n
                        dchain.step(V.tensor_tensor(st[0:RDK, f + 1], st[0:RDK, f], bc(cd[0:RDK], 2, RDV), ALU.mult))
                        dchain.step(V.tensor_tensor(st[RDK:P, b - 1], st[RDK:P, b], bc(cd[RDK:P], 2, RDV), ALU.mult))
                        dchain.join(dve)
                        dchain.step(V.tensor_tensor(st[0:RDK, f + 1], st[0:RDK, f + 1], kv[0:RDK, f + 1], ALU.add))
                        dchain.step(V.tensor_tensor(st[RDK:P, b - 1], st[RDK:P, b - 1], kv[RDK:P, b + 1], ALU.add))
                        dchain.join(dve)

                @block.gpsimd
                def _(pool):
                    pool.wait_ge(ac, 4)
                    for t in range(1, NT):
                        nc.gpsimd.tensor_tensor(qq[:, t - 1], bc(qv[:, t], 2, 2),
                                                bc(tab[:, 0].rearrange("p d h -> p h d"), 3, RDK), ALU.mult)
                    pool.drain()

                @block.tensor
                def _(pe):
                    for t in range(NT):
                        pe.wait_ge(kk_done, t + 1)
                        if t >= 4:
                            pe.wait_ge(kv_out, t - 3)
                        for h in range(RH):
                            last = T.matmul(bank(2 * (t % 4), 2)[:, h * RDV:(h + 1) * RDV],
                                            kk[:, t, h].rearrange("p d k -> p (d k)"),
                                            proj[:, t, RV + h * RDV:RV + (h + 1) * RDV], start=True, stop=True)
                        last.then_inc(kv_done, 1)

                @block.scalar
                def _(act):
                    act.wait_ge(dv, 1)
                    A.activation(tl[:, 2, :], tl[:, 1, :], ACT.Exp, scale=-1.0).then_inc(ac, 1)
                    act.wait_ge(dv, 2)
                    A.activation(tl[:, 6, :], tl[:, 3, :], ACT.Ln).then_inc(ac, 1)
                    act.wait_ge(dv, 3)
                    A.activation(tab, tab, ACT.Exp).then_inc(ac, 1)
                    A.activation(cd, cd, ACT.Exp).then_inc(ac, 1)
                    for d in range(2):
                        for h in range(RH):
                            A.activation(ex[:, d, h], const[:, C_REL + d * P:C_REL + (d + 1) * P], ACT.Exp,
                                         scale=lg[:, d, h:h + 1]).then_inc(ac, 1)
                    for t in range(NT):
                        act.wait_ge(kv_done, t + 1)
                        A.copy(kv[:, t], bank(2 * (t % 4), 2).rearrange("p (h v) -> p h v", h=RH)).then_inc(kv_out, 1)
                    for t in range(NT):
                        A.activation(proj[:, t, RG:RG + RH * RDV], proj[:, t, RG:RG + RH * RDV], ACT.Silu)
                    act.drain()

            o = SH
            qt = at(o, 2, 4, P); o += 8 * P
            ktt = at(o, 2, RH, P); o += 2 * RH * P
            qqt = at(o, 2, RH, P); o += 2 * RH * P
            sm = at(o, 2, RH, P); o += 2 * RH * P
            cens = at(o, 2, RH, RDV); o += 2 * RH * RDV
            bst = at(o, RH, 6); o += RH * 6
            bmv = at(o, RH, 2); o += RH * 2
            rt = at(o, 2, RH); o += 2 * RH
            assert o <= ARENA
            trq, trc, scored, masked = sem("ret_tr"), sem("ret_trc"), sem("ret_scored"), sem("ret_masked")
            padded, flat, gated = sem("ret_padded"), sem("ret_flat"), sem("ret_gated")
            summed, centred, var, root = sem("ret_summed"), sem("ret_centred"), sem("ret_var"), sem("ret_root")
            with nc.Block(no_gpsimd_drain=True) as block:
                @block.tensor
                def _(pe):
                    def turn(t):
                        if t:
                            pe.wait_ge(trc, t)
                        for j in range(4):
                            T.transpose(bank(0)[:, j * P:(j + 1) * P], proj[:, t, RQ + j * P:RQ + (j + 1) * P], ident)
                            last = T.transpose(bank(1)[:, j * P:(j + 1) * P], proj[:, t, RK + j * P:RK + (j + 1) * P], ident)
                        if t:
                            for h in range(RH):
                                last = T.transpose(bank(2, 2)[:, h * P:(h + 1) * P], qq[:, t - 1, h].rearrange("p d k -> p (d k)"), ident)
                        last.then_inc(trq, 1)

                    def score(t):
                        pe.wait_ge(trc, t + 1)
                        if t:
                            pe.wait_ge(masked, t)
                        for h in range(RH):
                            last = T.matmul(bank(4, 2)[:, h * P:(h + 1) * P], ktt[:, t % 2, h, :],
                                            qt[:, t % 2, h // 2, :], start=True, stop=True)
                        last.then_inc(scored, 1)

                    def total(t):
                        pe.wait_ge(masked, t + 1)
                        if t:
                            pe.wait_ge(centred, t)
                        for h in range(RH):
                            out = bank(6, 2)[:, h * P:(h + 1) * P]
                            last = T.matmul(out, sm[:, t % 2, h, :], proj[:, t, RV + h * RDV:RV + (h + 1) * RDV],
                                            start=True, stop=(t == 0))
                            if t:
                                last = T.matmul(out, qqt[:, t % 2, h, :], st[:, t - 1, h, :], start=False, stop=True)
                        last.then_inc(summed, 1)

                    turn(0)
                    pe.wait_ge(padded, 2)
                    score(0)
                    turn(1)
                    for t in range(NT):
                        total(t)
                        if t + 1 < NT:
                            score(t + 1)
                        if t + 2 < NT:
                            turn(t + 2)

                @block.gpsimd
                def _(pool):
                    for r in range(2):
                        rows = slice(RDK * (1 - r), RDK * (2 - r))
                        nc.gpsimd.memset(ktt[rows].rearrange("p a (j r) i -> p r (a j) i", r=2)[:, r], 0.0).then_inc(padded, 1)
                    for t in range(NT):
                        pool.wait_ge(flat, t + 1)
                        g = proj[:, t, RG:RG + RH * RDV].rearrange("p (h v) -> p h v", h=RH)
                        nc.gpsimd.tensor_tensor(g, g, cens[:, t % 2], ALU.mult).then_inc(gated, 1)

                @block.scalar
                def _(act):
                    def copy(t):
                        act.wait_ge(trq, t + 1)
                        if t >= 2:
                            act.wait_ge(summed, t - 1)
                        A.copy(qt[:, t % 2], bank(0).rearrange("p (j i) -> p j i", j=4))
                        for r in range(2):
                            rows = slice(RDK * r, RDK * (r + 1))
                            last = A.copy(ktt[rows, t % 2].rearrange("p (j r) i -> p r j i", r=2)[:, r],
                                          bank(1)[rows].rearrange("p (j i) -> p j i", j=4))
                        if t:
                            last = A.copy(qqt[:, t % 2], bank(2, 2).rearrange("p (h i) -> p h i", h=RH))
                        last.then_inc(trc, 1)

                    copy(0)
                    for t in range(NT):
                        if t + 1 < NT:
                            copy(t + 1)
                        act.wait_ge(var, t + 1)
                        A.activation(rt[:, 0, :], bmv[:, :, 1], ACT.Sqrt, bias=eps_ln).then_inc(root, 1)

                @block.vector
                def _(dve):
                    def mask(t):
                        dve.wait_ge(scored, t + 1)
                        if t >= 2:
                            dve.wait_ge(summed, t - 1)
                        V.tensor_tensor(sm[:, t % 2], bank(4, 2).rearrange("p (h i) -> p h i", h=RH), dt,
                                        ALU.mult).then_inc(masked, 1)

                    def norm(t):
                        dve.wait_ge(summed, t + 1)
                        src = bank(6, 2).rearrange("p (h v) -> p h v", h=RH)
                        cen = cens[:, t % 2]
                        for h in range(RH):
                            dchain.step(V.bn_stats(bst[:, h], src[:, h]))
                        dchain.join(dve)
                        for h in range(RH):
                            last = V.bn_aggr(bmv[:, h], bst[:, h])
                        last.then_inc(var, 1)
                        if t + 1 < NT:
                            mask(t + 1)
                        dve.wait_ge(var, t + 1)
                        if t >= 2:
                            dve.wait_ge(gated, t - 1)
                        V.tensor_tensor(cen, src, bc(bmv[:, :, 0], 2, RDV), ALU.subtract).then_inc(centred, 1)
                        dve.wait_ge(root, t + 1)
                        dchain.step(V.reciprocal(rt[:, 1, :], rt[:, 0, :]))
                        dchain.join(dve)
                        dve.wait_ge(centred, t + 1)
                        V.tensor_tensor(cen, cen, bc(rt[:, 1, :], 2, RDV), ALU.mult).then_inc(flat, 1)

                    mask(0)
                    for t in range(NT):
                        norm(t)

        def heads_attention(name, units, qT, kT, value, width, e_buf, halves, lamr, put, rsum, nmax, pT, upright, squares=None):
            scored, maxed, expd = sem(f"{name}_scored"), sem(f"{name}_maxed"), sem(f"{name}_expd")
            mixed = sem(f"{name}_mixed")
            turned, c_a, c_d, valued, put_s = (sem(f"{name}_{n}") for n in ("turned", "ca", "cd", "valued", "put"))
            U = len(units)
            tiles = [[NT] if t == 0 else list(range(NT)) for t, _ in units]

            def view(b, nk):
                if nk == 1:
                    return bank(2 * b)[:, 0:P]
                return bank(2 * b, 2).rearrange("p (a n) -> p a n", a=2)[:, :, 0:KEYS // 2]

            def out_of(u):
                h = units[u][1]
                b = bank(6 + u % 2)
                return b[width * (h % 2):width * (h % 2 + 1), 0:P] if upright else b[:, 0:width]

            def flat(b, nk):
                e = e_buf[:, b, 0:nk * P]
                return e if nk == 1 else e.rearrange("p (a n) -> p a n", a=2)

            with nc.Block(no_gpsimd_drain=True) as block:
                @block.tensor
                def _(pe):
                    def score(u):
                        t, h = units[u]
                        for s in range(halves):
                            v = halves * u + s
                            if v >= 2:
                                pe.wait_ge(expd, v - 1)
                            q = qT(t, h, s)
                            if t == 0:
                                T.matmul(view(v % 2, 1), q, kT(h, s, NT * P, P), start=True, stop=True).then_inc(scored, 1)
                            else:
                                for a in range(2):
                                    last = T.matmul(view(v % 2, NT)[:, a], q, kT(h, s, a * KEYS // 2, KEYS // 2), start=True, stop=True)
                                last.then_inc(scored, 1)

                    def turn(u):
                        pe.wait_ge(mixed, u + 1)
                        if u:
                            pe.wait_ge(c_d, u)
                            pe.wait_ge(c_a, u)
                        src = e_buf[:, (u % 2) * halves, :]
                        for n in range(len(tiles[u])):
                            b, c = (4, n) if n < 3 else (5, n - 3)
                            last = T.transpose(bank(b)[:, c * P:(c + 1) * P], src[:, n * P:(n + 1) * P], ident)
                        last.then_inc(turned, 1)

                    def values(u):
                        t, h = units[u]
                        pe.wait_ge(c_d, u + 1)
                        pe.wait_ge(c_a, u + 1)
                        if u >= 2:
                            pe.wait_ge(put_s, u - 1)
                        for n, kt in enumerate(tiles[u]):
                            w, v = pT[:, u % 2, n, :], value(h, kt)
                            last = T.matmul(out_of(u), v if upright else w, w if upright else v,
                                            start=(n == 0), stop=(n == len(tiles[u]) - 1))
                        last.then_inc(valued, 1)

                    for u in range(U + 2):
                        if u < U:
                            score(u)
                        if u >= 2:
                            values(u - 2)
                        if 1 <= u <= U:
                            turn(u - 1)

                @block.vector
                def _(dve):
                    def top(u):
                        for s in range(halves):
                            v = halves * u + s
                            nk = len(tiles[u])
                            dve.wait_ge(scored, v + 1)
                            src = view(v % 2, nk)
                            V.tensor_reduce(nmax[:, v:v + 1], src, AX.X if nk == 1 else AX.XY, ALU.max,
                                            negate=True).then_inc(maxed, 1)

                    def mix(u):
                        dve.wait_ge(expd, halves * (u + 1))
                        sums, r = (rsum[:, n, halves * u:halves * (u + 1)] for n in range(2))
                        dchain.step(V.reciprocal(r, sums))
                        dchain.join(dve)
                        if halves == 2:
                            nk = len(tiles[u]) * P
                            e1, e2 = (e_buf[:, 2 * (u % 2) + s, 0:nk] for s in range(2))
                            dchain.step(V.scalar_tensor_tensor(r[:, 1:2], r[:, 1:2], lamr, sums[:, 0:1], ALU.mult, ALU.mult))
                            dchain.join(dve)
                            V.scalar_tensor_tensor(e1, e2, r[:, 1:2], e1, ALU.mult, ALU.add).then_inc(mixed, 1)
                        else:
                            e1 = e_buf[:, u % 2, 0:len(tiles[u]) * P]
                            V.tensor_scalar(e1, e1, rsum[:, 1, u:u + 1], None, ALU.mult).then_inc(mixed, 1)

                    def copy_p(u):
                        dve.wait_ge(turned, u + 1)
                        if u >= 2:
                            dve.wait_ge(valued, u - 1)
                        nd = min(3, len(tiles[u]))
                        V.tensor_copy(pT[:, u % 2, 0:nd], bank(4)[:, 0:nd * P].rearrange("p (n q) -> p n q", n=nd)).then_inc(c_d, 1)

                    def out(u):
                        dve.wait_ge(valued, u + 1)
                        if halves == 2:
                            V.tensor_scalar(put(*units[u]), out_of(u), rsum[:, 1, 2 * u:2 * u + 1], None, ALU.mult).then_inc(put_s, 1)
                        else:
                            V.tensor_copy(put(*units[u]), out_of(u)).then_inc(put_s, 1)

                    for u in range(U + 2):
                        if 1 <= u <= U:
                            mix(u - 1)
                        if u < U:
                            top(u)
                        if u >= 2:
                            out(u - 2)
                        if 1 <= u <= U:
                            copy_p(u - 1)
                    dve.drain()

                @block.scalar
                def _(act):
                    def exps(u):
                        for s in range(halves):
                            v = halves * u + s
                            nk = len(tiles[u])
                            act.wait_ge(maxed, v + 1)
                            if u >= 2:
                                act.wait_ge(turned, u - 1)
                            A.activation(flat((u % 2) * halves + s, nk), view(v % 2, nk), ACT.Exp,
                                         bias=nmax[:, v:v + 1], accum_out=rsum[:, 0, v:v + 1]).then_inc(expd, 1)

                    def copy_p(u):
                        act.wait_ge(turned, u + 1)
                        if u >= 2:
                            act.wait_ge(valued, u - 1)
                        n = len(tiles[u])
                        if n > 3:
                            A.copy(pT[:, u % 2, 3:n], bank(5)[:, 0:(n - 3) * P].rearrange("p (n q) -> p n q", q=P)).then_inc(c_a, 1)
                        else:
                            act.nop().then_inc(c_a, 1)

                    def square(u):
                        act.wait_ge(put_s, u + 1)
                        t, h = units[u]
                        achain.join(act)
                        achain.step(A.activation(squares[0], put(t, h), ACT.Square, accum_out=squares[1][:, t, h:h + 1]))

                    for u in range(U + 2):
                        if u < U:
                            exps(u)
                        if 1 <= u <= U:
                            copy_p(u - 1)
                        if squares and u >= 2:
                            square(u - 2)
                    act.drain()

        UNITS = [(t, h) for t in range(1, NT) for h in range(8)] + [(0, h) for h in range(8)]

        def latent_attention(mlaT):
            o = R
            kT = at(o, MH, NK * P); o += MH * NK * P
            qT = at(o, MH, TOK); o += MH * TOK
            vm = at(o, NK, MH * MDV); o += NK * MH * MDV
            E_AT = o
            ckc = at(o, MKV); o += MKV
            krp = at(o, NK, MQD); o += NK * MQD
            rope = at(o, 2, NT - 1, MR // 2); o += (NT - 1) * MR
            tmp = at(o, 4, NT - 1, MH, MR // 2); o += 4 * (NT - 1) * MH * MR // 2
            tmk = at(o, 4, NT - 1, MR // 2); o += 4 * (NT - 1) * MR // 2
            ckT = at(o, 2, NK * P); o += 2 * NK * P
            wuk = at(o, 2, MH * MN); o += 2 * MH * MN
            wuv = at(o, 2, MH * MDV); o += 2 * MH * MDV
            junk = at(o, MKV); o += MKV
            ss = at(o, 2, NT); o += 2 * NT
            assert o <= ARENA, o
            loaded, w_in, kr_in = sem("mla_loaded"), sem("mla_win"), sem("mla_krin")
            squared, normed, roped, padded = sem("mla_sq"), sem("mla_norm"), sem("mla_rope"), sem("mla_pad")
            tr, ev_a, ev_d = sem("mla_tr"), sem("mla_eva"), sem("mla_evd")
            ck = proj[:, :, CKV:CKV + MKV]
            kr = proj[:, :, KR:KR + MR]
            mq = proj[:, :, MQ:MQ + MH * MQD].rearrange("p t (h d) -> p t h d", h=MH)
            H2 = MR // 2

            items = []
            for c in range(2):
                items.append(("ck", c))
            items.append(("kr", 0))
            for h in range(MH):
                items.append(("q", h))
            for j in range(MH // 2):
                items.append(("k", j))
            for n in range(NK // 2):
                items.append(("v", n))
            def evac(eng, who):
                copy = A.copy if who == 0 else V.tensor_copy
                done = (ev_a, ev_d)[who]
                for n, (kind, j) in enumerate(items):
                    if n % 2 != who:
                        continue
                    eng.wait_ge(tr, n + 1)
                    src = bank(2 * (n % 4), 2)
                    if kind == "ck":
                        copy(ckT[:, j, :], src[:, 0:NK * P]).then_inc(done, 1)
                    elif kind == "kr":
                        copy(kT[MN:MQD], bc(src[MN:MQD, 0:NK * P], 1, MH)).then_inc(done, 1)
                    elif kind == "q":
                        if who == 0:
                            A.mul(qT[0:MQD, j, :], src[0:MQD, 0:TOK], MLA_SCALE).then_inc(done, 1)
                        else:
                            V.tensor_scalar(qT[0:MQD, j, :], src[0:MQD, 0:TOK], MLA_SCALE, None, ALU.mult).then_inc(done, 1)
                    elif kind == "k":
                        s2 = src.rearrange("p (a n) -> p a n", a=2)[:, :, 0:NK * P // 2]
                        for r in range(2):
                            last = copy(kT[0:MN, 2 * j + r, :].rearrange("p (a n) -> p a n", a=2), s2[MN * r:MN * (r + 1)])
                        last.then_inc(done, 1)
                    else:
                        copy(vm[:, 2 * j:2 * j + 2, :], src.rearrange("p (a n) -> p a n", a=2)).then_inc(done, 1)

            with nc.Block(no_gpsimd_drain=True) as block:
                @block.sync
                def _(sp):
                    sp.dma_start(krp[:, 0, MN:MQD], I["cache_mla_krope"][0, 0]).then_inc(kr_in, 16)
                    sp.dma_start(ckc, I["cache_mla_ckv"][0, 0]).then_inc(kr_in, 16)
                    sp.dma_start(rope, I["rope_mla"].rearrange("a (t p) n -> p a t n", p=P)).then_inc(loaded, 16)
                    sp.dma_start(wuk, I["mla_w_uk"][0].rearrange("(k p) n -> p k n", p=P)).then_inc(w_in, 16)
                    sp.dma_start(wuv, I["mla_w_uv"][0].rearrange("(k p) n -> p k n", p=P)).then_inc(w_in, 16)
                    store(sp, O["new_cache_mla_krope"][0, 0], kr[:, 0, :])
                    sp.wait_ge(normed, 1)
                    store(sp, O["new_cache_mla_ckv"][0, 0], ck[:, 0, :])

                @block.scalar
                def _(act):
                    for t in range(NT):
                        achain.step(A.activation(junk, ck[:, t, :], ACT.Square, accum_out=ss[:, 0, t:t + 1]))
                        achain.join(act)
                    A.activation(ss[:, 1, :], ss[:, 0, :], ACT.Sqrt, bias=eps_rms, scale=1.0 / MKV).then_inc(squared, 1)
                    evac(act, 0)
                    act.drain()

                @block.vector
                def _(dve):
                    V.memset(krp[:, :, 0:MN], 0.0).then_inc(padded, 1)
                    dve.wait_ge(squared, 1)
                    dchain.step(V.reciprocal(ss[:, 0, :], ss[:, 1, :]))
                    dchain.join(dve)
                    for t in range(NT):
                        V.scalar_tensor_tensor(ck[:, t, :], ck[:, t, :], ss[:, 0, t:t + 1], kvg, ALU.mult, ALU.mult).then_inc(normed, 1)
                    dve.wait_ge(loaded, 16)
                    for x1, x2, y1, y2, tm, cs in (
                            (mq[:, 1:NT, :, MN:MN + H2], mq[:, 1:NT, :, MN + H2:MQD], mq[:, 1:NT, :, MN:MN + H2],
                             mq[:, 1:NT, :, MN + H2:MQD], tmp, [bc(rope[:, s], 2, MH) for s in range(2)]),
                            (kr[:, 1:NT, 0:H2], kr[:, 1:NT, H2:MR], krp[:, 1:NT, MN:MN + H2], krp[:, 1:NT, MN + H2:MQD],
                             tmk, [rope[:, s] for s in range(2)])):
                        for n, (src, s) in enumerate(((x1, 0), (x2, 1), (x1, 1), (x2, 0))):
                            dchain.step(V.tensor_tensor(tm[:, n], src, cs[s], ALU.mult))
                        dchain.join(dve)
                        dchain.step(V.tensor_tensor(y1, tm[:, 0], tm[:, 1], ALU.subtract))
                        V.tensor_tensor(y2, tm[:, 2], tm[:, 3], ALU.add).then_inc(roped, 1)
                    V.tensor_copy(krp[:, NT, MN:MQD], kr[:, 0, :]).then_inc(roped, 1)
                    evac(dve, 1)
                    dve.drain()

                @block.tensor
                def _(pe):
                    for n, (kind, j) in enumerate(items):
                        if n >= 4:
                            pe.wait_ge((ev_a, ev_d)[n % 2], (n - 4) // 2 + 1)
                        dst = bank(2 * (n % 4), 2)
                        if kind == "ck":
                            if j == 0:
                                pe.wait_ge(kr_in, 32)
                                pe.wait_ge(normed, NT)
                            for m in range(NK):
                                src = ckc if m == 0 else ck[:, m % NT, :]
                                last = T.transpose(dst[:, m * P:(m + 1) * P], src[:, j * P:(j + 1) * P], ident)
                        elif kind == "kr":
                            pe.wait_ge(roped, 3)
                            pe.wait_ge(padded, 1)
                            for m in range(NK):
                                last = T.transpose(dst[0:MQD, m * P:(m + 1) * P], krp[:, m, :], ident)
                        elif kind == "q":
                            for t in range(NT):
                                last = T.transpose(dst[0:MQD, t * P:(t + 1) * P], mq[:, t, j, :], ident)
                        elif kind == "k":
                            if j == 0:
                                pe.wait_ge(ev_a, 1)
                                pe.wait_ge(ev_d, 1)
                                pe.wait_ge(w_in, 32)
                            for a in range(2):
                                for k in range(2):
                                    last = T.matmul(dst[:, a * BANK:a * BANK + NK * P // 2], wuk[:, k, j * P:(j + 1) * P],
                                                    ckT[:, k, a * NK * P // 2:(a + 1) * NK * P // 2], start=(k == 0), stop=(k == 1))
                        else:
                            for a in range(2):
                                m = 2 * j + a
                                for k in range(2):
                                    last = T.matmul(dst[:, a * BANK:(a + 1) * BANK], ckT[:, k, m * P:(m + 1) * P],
                                                    wuv[:, k, :], start=(k == 0), stop=(k == 1))
                        last.then_inc(tr, 1)

            o = E_AT
            e_buf = at(o, 2, KEYS); o += 2 * KEYS
            pT = at(o, 2, NT, P); o += 2 * NT * P
            rsum = at(o, 2, len(UNITS)); o += 2 * len(UNITS)
            nmax = at(o, len(UNITS)); o += len(UNITS)
            heads_attention(
                "mla", UNITS,
                lambda t, h, s: qT[0:MQD, h, t * P:(t + 1) * P],
                lambda h, s, k0, n: kT[0:MQD, h, k0:k0 + n],
                lambda h, kt: vm[:, kt, h * MDV:(h + 1) * MDV],
                MDV, e_buf, 1, None,
                lambda t, h: mlaT[MDV * (h % 2):MDV * (h % 2 + 1), h // 2, t * P:(t + 1) * P], rsum, nmax, pT, True)

        def differential_attention(pj):
            o = R
            kT = at(o, DH, NK * P); o += DH * NK * P
            qT = at(o, DH, 2, TOK); o += 2 * DH * TOK
            vc = at(o, DH, DDV); o += DH * DDV
            kc = at(o, DH, DDV)
            lp = at(o + 2 * DH * DDV, 4, DDH)
            assert o + 2 * DH * DDV + 256 <= ARENA
            loaded, k_in = sem("diff_loaded"), sem("diff_kin")
            tr, ev_a, ev_d, lam_v, lam_a = (sem(f"diff_{n}") for n in ("tr", "eva", "evd", "lamv", "lama"))
            lam1 = small[:, 32:34]
            def evac(eng, who):
                done = (ev_a, ev_d)[who]
                for n, (kind, h) in enumerate(items):
                    if n % 2 != who:
                        continue
                    eng.wait_ge(tr, n + 1)
                    src = bank(2 * (n % 4), 2)
                    if kind == "k":
                        copy = A.copy if who == 0 else V.tensor_copy
                        copy(kT[:, h, :], src[:, 0:NK * P]).then_inc(done, 1)
                        continue
                    for r in range(2):
                        rows = slice(DDH * r, DDH * (r + 1))
                        dst, half = qT[rows, h, r, :], src[rows, 0:TOK]
                        if who == 0:
                            last = A.mul(dst, half, DIFF_SCALE)
                        else:
                            last = V.tensor_scalar(dst, half, DIFF_SCALE, None, ALU.mult)
                    last.then_inc(done, 1)

            with nc.Block(no_gpsimd_drain=True) as block:
                @block.sync
                def _(sp):
                    sp.dma_start(lp, I["diff_lambda"][0].partition_broadcast(P)).then_inc(loaded, 16)
                    sp.dma_start(kc, I["cache_diff_k"][0, 0].rearrange("h p d -> p h d")).then_inc(k_in, 16)
                    sp.dma_start(vc, I["cache_diff_v"][0, 0].rearrange("h p d -> p h d")).then_inc(k_in, 16)
                    store(sp, O["new_cache_diff_k"][0, 0].rearrange("h p d -> p h d"),
                          pj[:, 0, D:2 * D].rearrange("p (h d) -> p h d", h=DH))
                    store(sp, O["new_cache_diff_v"][0, 0].rearrange("h p d -> p h d"),
                          pj[:, 0, 2 * D:3 * D].rearrange("p (h d) -> p h d", h=DH))

                items = [("q", h) for h in range(DH)] + [("k", h) for h in range(DH)]

                @block.gpsimd
                def _(pool):
                    for r in range(2):
                        rows = slice(DDH * (1 - r), DDH * (2 - r))
                        nc.gpsimd.memset(qT[rows, :, r, :], 0.0)
                    pool.drain()

                @block.vector
                def _(dve):
                    dve.wait_ge(loaded, 16)
                    lq = lp.rearrange("p (a b) d -> p a b d", a=2)
                    dchain.step(V.tensor_tensor(lq[:, :, 0], lq[:, :, 0], lq[:, :, 1], ALU.mult))
                    dchain.join(dve)
                    V.tensor_reduce(lam1, lq[:, :, 0], AX.X, ALU.add).then_inc(lam_v, 1)
                    evac(dve, 1)
                    dve.wait_ge(lam_a, 1)
                    dchain.step(V.tensor_tensor(lam[:, 0:1], lam[:, 2:3], lam[:, 3:4], ALU.subtract))
                    dchain.join(dve)
                    dchain.step(V.tensor_scalar(lam[:, 0:1], lam[:, 0:1], -1.0, -LAM_INIT, ALU.mult, ALU.add))
                    dve.drain()

                @block.scalar
                def _(act):
                    act.wait_ge(lam_v, 1)
                    A.activation(lam[:, 2:4], lam1, ACT.Exp).then_inc(lam_a, 1)
                    evac(act, 0)
                    act.drain()

                @block.tensor
                def _(pe):
                    for n, (kind, h) in enumerate(items):
                        if n >= 4:
                            pe.wait_ge((ev_a, ev_d)[n % 2], (n - 4) // 2 + 1)
                        dst = bank(2 * (n % 4), 2)
                        if (kind, h) == ("k", 0):
                            pe.wait_ge(k_in, 32)
                        if kind == "q":
                            for t in range(NT):
                                last = T.transpose(dst[:, t * P:(t + 1) * P], pj[:, t, h * DDV:(h + 1) * DDV], ident)
                        else:
                            for m in range(NK):
                                src = kc[:, h, :] if m == 0 else pj[:, m % NT, D + h * DDV:D + (h + 1) * DDV]
                                last = T.transpose(dst[:, m * P:(m + 1) * P], src, ident)
                        last.then_inc(tr, 1)

            o = R + DH * NK * P + 2 * DH * TOK + DH * DDV
            e_buf = at(o, 4, KEYS); o += 4 * KEYS
            pT = at(o, 2, NT, P); o += 2 * NT * P
            rsum = at(o, 2, 2 * len(UNITS)); o += 4 * len(UNITS)
            nmax = at(o, 2 * len(UNITS)); o += 2 * len(UNITS)
            ss, rt, junk = at(o, NT, DH), at(o + 64, 2, NT, DH), at(o + 192, DDV)
            heads_attention(
                "diff", UNITS,
                lambda t, h, s: qT[:, h, s, t * P:(t + 1) * P],
                lambda h, s, k0, n: kT[:, h, k0:k0 + n],
                lambda h, kt: vc[:, h, :] if kt == 0 else pj[:, kt % NT, 2 * D + h * DDV:2 * D + (h + 1) * DDV],
                DDV, e_buf, 2, lam[:, 0:1],
                lambda t, h: pj[:, t, h * DDV:(h + 1) * DDV], rsum, nmax, pT, False, (junk, ss))

            rooted = sem("dn_root")
            with nc.Block(no_gpsimd_drain=True) as block:
                @block.scalar
                def _(act):
                    A.activation(rt[:, 0], ss, ACT.Sqrt, bias=eps_rms, scale=1.0 / DDV).then_inc(rooted, 1)

                @block.vector
                def _(dve):
                    dchain.step(V.tensor_scalar(dng, dng, 1.0 - LAM_INIT, None, ALU.mult))
                    dve.wait_ge(rooted, 1)
                    dchain.step(V.reciprocal(rt[:, 1], rt[:, 0]))
                    dchain.join(dve)
                    for t in range(NT):
                        ov = pj[:, t, 0:D].rearrange("p (h v) -> p h v", h=DH)
                        V.tensor_tensor(ov, ov, bc(rt[:, 1, t, :], 2, DDV), ALU.mult)
                    dve.drain()

        def router(i):
            w = R + W_EXP
            lo = at(w, NT, G + NE)
            w += 256

            def b4(n):
                return at(w + n * 64, NT, G)

            def b1(n):
                return at(w + 1024 + n * 8, NT)

            sel, pg, pe_, ohg, oh1, oh2, t4, p2 = (b4(n) for n in range(8))
            gm, gs_, em, s1, s2, gp, a1, a2, tm1 = (b1(n) for n in range(9))
            prod = at(w + 2048, NT, G, EG)
            ohk = at(w + 2304, 2, NT, NE)
            every = at(w + 2560, NT, NE)
            slot = at(w + 2816, NT, NE)
            pre = at(w + 3072, NT + 1, NE)
            cnt = pre[:, NT, :]
            over, incl, tmi, excl, jump = (at(w + 3328 + 16 * n, NE) for n in range(5))
            pos = at(w + 3456, 2, NT)
            far = at(w + 3584, NT, NE)
            within, chunk_of = at(w + 3712, 2, NT), at(w + 3728, 2, NT)
            in_i, of_i = at(w + 3744, 2, NT).bitcast(I32), at(w + 3760, 2, NT).bitcast(I32)
            at_slot = at(w + 3840, 2, NT, P)
            tok_of = at(w + 3840 + 2 * NT * P, 2, NT, CHUNKS)
            tie4 = bc(const[:, C_TIE:C_TIE + 4], 1, NT)
            nm, ex, picked, ranked = sem(f"r{i}_neg"), sem(f"r{i}_exp"), sem(f"r{i}_picked"), sem(f"r{i}_ranked")
            placed, listed = sem(f"r{i}_placed"), sem(f"r{i}_listed")
            E13, E2 = expert_weights(WEIGHTS_AT[1])
            with nc.Block(no_gpsimd_drain=True) as block:
                @block.sync
                def _(sp):
                    sp.dma_start(E13[0], I["moe_w1"][i, 1].rearrange("(k p) f -> p k f", p=P)).then_inc(up_in[1], 16)
                    sp.dma_start(E13[1], I["moe_w3"][i, 1].rearrange("(k p) f -> p k f", p=P)).then_inc(up_in[1], 16)
                    sp.dma_start(E2, I["moe_w2"][i, 1].rearrange("(f p) n -> p f n", p=P)).then_inc(dn_in[1], 16)

                @block.tensor
                def _(pe):
                    pe.wait_ge(picked, 1)
                    m = every.rearrange("p t e -> p (t e)")
                    T.matmul(bank(0)[:, 0:NT * NE], const[:, C_TRI:C_TRI + P], m, start=True, stop=True)
                    T.matmul(bank(1)[:, 0:NT * NE], ones, m, start=True, stop=True).then_inc(ranked, 1)
                    for n in range(2 * NT):
                        k, t = n // NT, n % NT
                        pe.wait_ge(placed, n + 1)
                        last = T.matmul(bank(2)[:, 0:CHUNKS], at_slot[:, k, t, :], tok_of[:, k, t, :],
                                        start=(n == 0), stop=(n == 2 * NT - 1))
                    last.then_inc(listed, 1)

                @block.vector
                def _(dve):
                    def do(ins):
                        dchain.step(ins)
                        dchain.join(dve)

                    def first_of(out, vals, top):
                        do(V.tensor_tensor(out, vals, bc(top, 2, 4), ALU.is_equal))
                        do(V.tensor_tensor(out, out, tie4, ALU.mult))
                        do(V.tensor_reduce(tm1, out, AX.X, ALU.max))
                        do(V.tensor_tensor(out, out, bc(tm1, 2, 4), ALU.is_equal))

                    do(V.tensor_tensor(lo, bank(6, 2)[:, 0:NT * P].rearrange("p (t n) -> p t n", t=NT)[:, :, 0:G + NE],
                                       bc(br[:, i, :], 1, NT), ALU.add))
                    lgp = lo[:, :, 0:G]
                    do(V.tensor_reduce(gm, lgp, AX.X, ALU.max))
                    first_of(ohg, lgp, gm)
                    V.tensor_tensor(pg, lgp, bc(gm, 2, G), ALU.subtract).then_inc(nm, 1)
                    do(V.tensor_tensor(prod, lo[:, :, G:].rearrange("p t (g e) -> p t g e", g=G), bc(ohg, 3, EG), ALU.mult))
                    do(V.tensor_reduce(sel, prod.rearrange("p t g e -> p t e g"), AX.X, ALU.add))
                    do(V.tensor_reduce(em, sel, AX.X, ALU.max))
                    V.tensor_tensor(pe_, sel, bc(em, 2, EG), ALU.subtract).then_inc(nm, 1)
                    dve.wait_ge(ex, 2)
                    do(V.tensor_reduce(s1, pe_, AX.X, ALU.max))
                    first_of(oh1, pe_, s1)
                    do(V.tensor_tensor(t4, pe_, oh1, ALU.mult))
                    do(V.tensor_tensor(p2, pe_, t4, ALU.subtract))
                    do(V.tensor_tensor(p2, p2, oh1, ALU.subtract))
                    do(V.tensor_reduce(s2, p2, AX.X, ALU.max))
                    first_of(oh2, p2, s2)
                    for k, oh in enumerate((oh1, oh2)):
                        dchain.step(V.tensor_tensor(ohk[:, k].rearrange("p t (g e) -> p t g e", g=G), bc(oh, 2, G), bc(ohg, 3, EG), ALU.mult))
                    dchain.join(dve)
                    V.tensor_tensor(every, ohk[:, 0], ohk[:, 1], ALU.add).then_inc(picked, 1)
                    dchain.step(V.memset(pre[:, 0, :], 0.0))
                    dchain.join(dve)
                    dve.wait_ge(ranked, 1)
                    tot = bank(1)[:, 0:NT * NE].rearrange("p (t e) -> p t e", t=NT)
                    for t in range(NT):
                        do(V.tensor_tensor(pre[:, t + 1, :], pre[:, t, :], tot[:, t, :], ALU.add))
                    do(V.tensor_tensor(slot, pre[:, 0:NT, :], bank(0)[:, 0:NT * NE].rearrange("p (t e) -> p t e", t=NT), ALU.add))
                    do(V.tensor_scalar(over, cnt, float(P), None, ALU.is_gt))
                    for c in range(2, NT):
                        do(V.scalar_tensor_tensor(over, cnt, float(c * P), over, ALU.is_gt, ALU.add))
                    src, dst_ = over, incl
                    for d in (1, 2, 4, 8):
                        dchain.step(V.tensor_tensor(dst_[:, d:], src[:, d:], src[:, 0:NE - d], ALU.add))
                        dchain.step(V.tensor_copy(dst_[:, 0:d], src[:, 0:d]))
                        dchain.join(dve)
                        src, dst_ = dst_, (tmi if dst_ is incl else incl)
                    do(V.tensor_tensor(excl, src, over, ALU.subtract))
                    first_slot = const[:, C_SLOT:C_SLOT + NE]
                    do(V.scalar_tensor_tensor(jump, excl, float(P), first_slot, ALU.mult, ALU.subtract))
                    do(V.tensor_scalar(jump, jump, float((NE - 1) * P), None, ALU.add))
                    do(V.scalar_tensor_tensor(far, slot, float(P), bc(jump, 1, NT), ALU.is_ge, ALU.mult))
                    do(V.tensor_tensor(slot, slot, bc(first_slot, 1, NT), ALU.add))
                    do(V.tensor_tensor(slot, slot, far, ALU.add))
                    for k in range(2):
                        dchain.step(V.tensor_tensor(ohk[:, k], ohk[:, k], slot, ALU.mult))
                    dchain.join(dve)
                    do(V.tensor_reduce(pos, ohk, AX.X, ALU.add))
                    do(V.tensor_copy(slot_i, pos))
                    dchain.step(V.tensor_scalar(in_i, slot_i, P - 1, None, ALU.bitwise_and))
                    dchain.step(V.tensor_scalar(of_i, slot_i, 7, None, ALU.logical_shift_right))
                    dchain.join(dve)
                    dchain.step(V.tensor_copy(within, in_i))
                    dchain.step(V.tensor_copy(chunk_of, of_i))
                    dchain.join(dve)
                    iota = const[:, C_IOTA:C_IOTA + P]
                    for k in range(2):
                        for t in range(NT):
                            dchain.step(V.tensor_scalar(tok_of[:, k, t, :], iota[:, 0:CHUNKS], chunk_of[:, k, t:t + 1],
                                                        const[:, C_TOK + t:C_TOK + t + 1], ALU.is_equal, ALU.mult))
                    dchain.join(dve)
                    for k in range(2):
                        for t in range(NT):
                            V.tensor_scalar(at_slot[:, k, t, :], iota, within[:, k, t:t + 1], None, ALU.is_equal).then_inc(placed, 1)
                    dchain.step(V.tensor_copy(tables[:, 0], over))
                    dchain.step(V.tensor_copy(tables[:, 1], excl))
                    dchain.step(V.tensor_scalar(tables[:, 2], src, 1.0, None, ALU.add))
                    do(V.tensor_reduce(gs_, pg, AX.X, ALU.add))
                    do(V.reciprocal(gp, gs_))
                    do(V.tensor_tensor(a1, s1, s2, ALU.add))
                    do(V.reciprocal(a2, a1))
                    do(V.tensor_tensor(gp, gp, a2, ALU.mult))
                    dchain.step(V.tensor_tensor(gates[:, 0], gp, s1, ALU.mult))
                    dchain.step(V.tensor_tensor(gates[:, 1], gp, s2, ALU.mult))
                    dve.wait_ge(listed, 1)
                    dchain.step(V.tensor_copy(tok_i, bank(2)[:, 0:CHUNKS]))
                    dchain.join(dve)
                    dve.drain()

                @block.scalar
                def _(act):
                    act.wait_ge(nm, 1)
                    A.activation(pg, pg, ACT.Exp).then_inc(ex, 1)
                    act.wait_ge(nm, 2)
                    A.activation(pe_, pe_, ACT.Exp).then_inc(ex, 1)

        def experts(i):
            o = R + W_EXP
            xg, xt, yb = at(o, 2, D), at(o + 2 * D, 2, KD, P), at(o + 4 * D, 2, D)
            o += 6 * D
            hid, gate = at(o, 2, 2, P), at(o + 4 * P, 2, 2, P)
            o += 8 * P
            xg_o, xt_o, yb_o = at(o, D), at(o + D, KD, P), at(o + 2 * D, D)
            hid_o, gate_o = at(o + 3 * D, 2, P), at(o + 3 * D + 2 * P, 2, P)
            o += 3 * D + 4 * P
            rows = at(o, 4).bitcast(I32)
            assert o + 4 <= ARENA
            xg_in = [sem(f"x{i}_xg{b}") for b in range(2)]
            y_out = [sem(f"x{i}_yout{b}") for b in range(2)]
            turned, xt_a, xt_d, up_s, silu_s, hid_s, y_s, y_a, y_d = (
                sem(f"x{i}_{n}") for n in ("turned", "xta", "xtd", "up", "silu", "hid", "y", "ya", "yd"))
            o_in, o_turned, o_xa, o_xd, o_up, o_silu, o_hid, o_y, o_yc, o_out = (
                sem(f"o{i}_{n}") for n in ("in", "turned", "xa", "xd", "up", "silu", "hid", "y", "yc", "out"))
            W1 = I["moe_w1"][i].rearrange("e (k p) f -> e p k f", p=P)
            W3 = I["moe_w3"][i].rearrange("e (k p) f -> e p k f", p=P)
            W2 = I["moe_w2"][i].rearrange("e (f p) n -> e p f n", p=P)
            y_chunks = y_rows.rearrange("(c p) n -> c p n", p=P)
            HALF = NE // 2

            def one(ap, e):
                return ap[bass.ds(e, 1)].rearrange("a p k f -> p (a k) f")

            def chunk_rows(c):
                return y_chunks[bass.ds(c, 1)].rearrange("a p n -> p (a n)")

            def up(dst, weights, xT):
                for f in range(2):
                    for m in range(2):
                        for k in range(KD):
                            last = T.matmul(dst[:, (2 * f + m) * P:(2 * f + m + 1) * P], weights[m][:, k, f * P:(f + 1) * P],
                                            xT[:, k, :], start=(k == 0), stop=(k == KD - 1))
                return last

            def down(b0, h, w2):
                for j in range(2):
                    for f in range(2):
                        last = T.matmul(bank(b0 + j), h[:, f, :], w2[:, f, j * BANK:(j + 1) * BANK], start=(f == 0), stop=(f == 1))
                return last

            def w13_part(b, m):
                return bank(b).rearrange("p (f m n) -> p m f n", f=2, m=2)[:, m]

            def loop(eng, expert):
                expert(0, 0, True)
                expert(1, 1, True)
                with eng.Fori(1, HALF) as pair:
                    expert(pair * 2, 0, False)
                    expert(pair * 2 + 1, 1, False)

            def entry(eng, row, e):
                col = tables[0:1, row, e:e + 1] if isinstance(e, int) else tables[0:1, row, bass.ds(e, 1)]
                return eng.value_load(col, min_val=0, max_val=(NT - 1) if row == 0 else FURTHER + 1)

            def further(eng, e, chunk):
                n = entry(eng, 0, e)
                first = entry(eng, 1, e)
                with eng.If(n > 0):
                    with eng.Fori(0, n) as c:
                        chunk(nc.s_assert_within(first + c, 0, FURTHER - 1, skip_runtime_bounds_check_because=(
                            "two experts for each token fill at most FURTHER chunks beyond the first ones")), c)
                eng.nop()

            with nc.Block(no_gpsimd_drain=True) as block:
                @block.sync
                def _(sp):
                    def expert(e, b, more):
                        E13, E2 = expert_weights(WEIGHTS_AT[b])
                        done = entry(sp, 2, e)
                        dst = chunk_rows(e)
                        if more:
                            w1, w3, w2 = one(W1, e + 2), one(W3, e + 2), one(W2, e + 2)
                            sp.wait_ge(up_s, e + 1)
                            sp.wait_ge(o_up, done)
                            sp.dma_start(E13[0], w1).then_inc(up_in[b], 16)
                            sp.dma_start(E13[1], w3).then_inc(up_in[b], 16)
                            sp.wait_ge(y_s, e + 1)
                            sp.wait_ge(o_y, done)
                            sp.dma_start(E2, w2).then_inc(dn_in[b], 16)
                        sp.wait_ge(y_a, e + 1)
                        sp.dma_start(dst[:, 0:BANK], yb[:, b, 0:BANK]).then_inc(y_out[b], 16)
                        sp.wait_ge(y_d, e + 1)
                        sp.dma_start(dst[:, BANK:D], yb[:, b, BANK:D]).then_inc(y_out[b], 16)

                    g2, gb = COMBINE
                    for c in range(2):
                        sp.dma_start(g2[:, c, :].rearrange("p (k m) -> p k m", k=KD), mod_row(i, 5, c)).then_inc(g2_in[i], 16)
                    sp.dma_start(gb[:, 0, :], I["ln2_g"][i].partition_broadcast(P)).then_inc(ln2_in[i], 16)
                    sp.dma_start(gb[:, 1, :], I["ln2_b"][i].partition_broadcast(P)).then_inc(ln2_in[i], 16)
                    with sp.Fori(0, HALF - 1) as pair:
                        expert(pair * 2, 0, True)
                        expert(pair * 2 + 1, 1, True)
                    expert(NE - 2, 0, False)
                    expert(NE - 1, 1, False)
                    for b in range(2):
                        sp.wait_ge(y_out[b], 32 * HALF)

                @block.gpsimd
                def _(pool):
                    def gather(e, b):
                        col = tok_i[:, e:e + 1] if isinstance(e, int) else tok_i[:, bass.ds(e, 1)]
                        nc.gpsimd.tensor_copy(rows[:, b:b + 1], col)
                        pool.drain()
                        pool.indirect_dma_start(out=xg[:, b, :], out_offset=None, in_=h2_rows, in_offset=bass.IndirectOffsetOnAxis(
                            ap=rows[:, b:b + 1], axis=0)).then_inc(xg_in[b], 16)

                    def expert(e, b, first):
                        if not (first and e == 0):
                            pool.wait_ge(turned, e + 0 if isinstance(e, int) else e)
                        gather(e + 1, 1 - b)

                        def chunk(q, c):
                            pool.wait_ge(o_turned, q + 1)
                            nc.gpsimd.tensor_copy(rows[:, 2:3], tok_i[:, bass.ds(q + NE, 1)])
                            pool.drain()
                            pool.indirect_dma_start(out=xg_o, out_offset=None, in_=h2_rows, in_offset=bass.IndirectOffsetOnAxis(
                                ap=rows[:, 2:3], axis=0)).then_inc(o_in, 16)
                        further(pool, e, chunk)

                    gather(0, 0)
                    loop(pool, expert)
                    pool.wait_ge(o_out, entry(pool, 2, NE - 1) * 16)

                @block.tensor
                def _(pe):
                    pe.nop().then_inc(o_turned, 1)
                    pe.nop().then_inc(o_up, 1)
                    pe.nop().then_inc(o_y, 1)

                    def turn(e, b, first):
                        pe.wait_ge(xg_in[b], (e + 2 - b) * 8)
                        for k in range(KD):
                            last = T.transpose(bank(0, 2)[:, k * P:(k + 1) * P], xg[:, b, k * P:(k + 1) * P], ident)
                        last.then_inc(turned, 1)

                    def expert(e, b, first):
                        E13, E2 = expert_weights(WEIGHTS_AT[b])
                        pe.wait_ge(xt_a, e + 1)
                        pe.wait_ge(xt_d, e + 1)
                        pe.wait_ge(up_in[b], (e + 2 - b) * 16)
                        if not first:
                            pe.wait_ge(hid_s, e - 1)
                        up(bank(2 + b), E13, xt[:, b]).then_inc(up_s, 1)
                        turn(e + 1, 1 - b, first)
                        pe.wait_ge(hid_s, e + 1)
                        pe.wait_ge(dn_in[b], (e + 2 - b) * 8)
                        if not (first and e == 0):
                            pe.wait_ge(y_a, e + 0)
                            pe.wait_ge(y_d, e + 0)
                        down(4, hid[:, b], E2).then_inc(y_s, 1)

                        def chunk(q, c):
                            pe.wait_ge(o_in, (q + 1) * 16)
                            pe.wait_ge(o_yc, q + 1)
                            for k in range(KD):
                                last = T.transpose(bank(6, 2)[:, k * P:(k + 1) * P], xg_o[:, k * P:(k + 1) * P], ident)
                            last.then_inc(o_turned, 1)
                            pe.wait_ge(o_xa, q + 1)
                            pe.wait_ge(o_xd, q + 1)
                            up(bank(6), E13, xt_o).then_inc(o_up, 1)
                            pe.wait_ge(o_hid, q + 1)
                            down(6, hid_o, E2).then_inc(o_y, 1)
                        further(pe, e, chunk)

                    turn(0, 0, True)
                    loop(pe, expert)

                @block.scalar
                def _(act):
                    act.nop().then_inc(o_out, 16)

                    def copy_x(e, b):
                        act.wait_ge(turned, e + 1)
                        A.copy(xt[:, b, 0:4], bank(0).rearrange("p (k n) -> p k n", k=4)).then_inc(xt_a, 1)

                    def expert(e, b, first):
                        act.wait_ge(up_s, e + 1)
                        if not first:
                            act.wait_ge(hid_s, e - 1)
                        A.activation(gate[:, b], w13_part(2 + b, 0), ACT.Silu).then_inc(silu_s, 1)
                        copy_x(e + 1, 1 - b)
                        act.wait_ge(y_s, e + 1)
                        if not first:
                            act.wait_ge(y_out[b], (e - b) * 16)
                        A.copy(yb[:, b, 0:BANK], bank(4)).then_inc(y_a, 1)

                        def chunk(q, c):
                            act.wait_ge(o_turned, q + 2)
                            A.copy(xt_o[:, 0:4], bank(6).rearrange("p (k n) -> p k n", k=4)).then_inc(o_xa, 1)
                            act.wait_ge(o_up, q + 2)
                            A.activation(gate_o, w13_part(6, 0), ACT.Silu).then_inc(o_silu, 1)
                            act.wait_ge(o_yc, q + 2)
                            act.dma_start(chunk_rows(q + NE), yb_o).then_inc(o_out, 16)
                        further(act, e, chunk)

                    copy_x(0, 0)
                    loop(act, expert)

                @block.vector
                def _(dve):
                    dve.nop().then_inc(o_yc, 1)

                    def copy_x(e, b):
                        dve.wait_ge(turned, e + 1)
                        V.tensor_copy(xt[:, b, 4:8], bank(1).rearrange("p (k n) -> p k n", k=4)).then_inc(xt_d, 1)

                    def expert(e, b, first):
                        dve.wait_ge(silu_s, e + 1)
                        V.tensor_tensor(hid[:, b], w13_part(2 + b, 1), gate[:, b], ALU.mult).then_inc(hid_s, 1)
                        copy_x(e + 1, 1 - b)
                        dve.wait_ge(y_s, e + 1)
                        if not first:
                            dve.wait_ge(y_out[b], (e - b) * 16)
                        V.tensor_copy(yb[:, b, BANK:D], bank(5)).then_inc(y_d, 1)

                        def chunk(q, c):
                            dve.wait_ge(o_turned, q + 2)
                            V.tensor_copy(xt_o[:, 4:8], bank(7).rearrange("p (k n) -> p k n", k=4)).then_inc(o_xd, 1)
                            dve.wait_ge(o_silu, q + 1)
                            V.tensor_tensor(hid_o, w13_part(6, 1), gate_o, ALU.mult).then_inc(o_hid, 1)
                            dve.wait_ge(o_y, q + 2)
                            dve.wait_ge(o_out, (q + 1) * 16)
                            V.tensor_copy(yb_o, bank(6, 2)).then_inc(o_yc, 1)
                        further(dve, e, chunk)

                    copy_x(0, 0)
                    loop(dve, expert)
                    dve.drain()

        def combine(i):
            g2, gb = COMBINE
            yg = at(BIG + 4 * D, NT, 2, D)
            y_in = [sem(f"l{i}_yin{t}") for t in range(NT)]
            best, whole, whole_last = (sem(f"l{i}_{n}") for n in ("best", "whole", "wholelast"))
            norm = Norm(f"l{i}_ln2", gb)
            with nc.Block(no_gpsimd_drain=True) as block:
                if i == DEPTH - 1:
                    @block.sync
                    def _(sp):
                        for t in range(NT):
                            if t < NT - 1:
                                sp.wait_ge(whole, t + 1)
                            else:
                                sp.wait_ge(whole_last, 1)
                            dst = O["y_prompt"][0] if t == 0 else O["y_sample"][0, (t - 1) * P:t * P, :]
                            store(sp, dst, x[:, t, :])

                @block.gpsimd
                def _(pool):
                    for t in range(NT):
                        for k in range(2):
                            pool.indirect_dma_start(out=yg[:, t, k, :], out_offset=None, in_=y_rows,
                                                    in_offset=bass.IndirectOffsetOnAxis(ap=slot_i[:, k, t:t + 1], axis=0)).then_inc(y_in[t], 16)
                    pool.wait_ge(ln2_in[i], 32)
                    for t in range(NT - 1):
                        norm.late(pool, nc.gpsimd, pchain, t).then_inc(whole, 1)
                    pool.drain()

                @block.scalar
                def _(act):
                    for t in range(NT):
                        act.wait_ge(y_in[t], 32)
                        A.mul(yg[:, t, 0, :], yg[:, t, 0, :], gates[:, 0, t:t + 1]).then_inc(best, 1)
                        if t:
                            norm.root_of(act, t - 1)
                            norm.normalise(act, t - 1)
                    norm.root_of(act, NT - 1)
                    norm.normalise(act, NT - 1)

                @block.vector
                def _(dve):
                    dve.wait_ge(g2_in[i], 32)
                    for t in range(NT):
                        a, b = yg[:, t, 0, :], yg[:, t, 1, :]
                        dve.wait_ge(best, t + 1)
                        dchain.step(V.scalar_tensor_tensor(a, b, gates[:, 1, t:t + 1], a, ALU.mult, ALU.add))
                        if t:
                            norm.scales(dve, t - 1)
                        dchain.join(dve)
                        dchain.step(V.tensor_tensor(a, a, g2[:, min(t, 1), :], ALU.mult))
                        dchain.join(dve)
                        dchain.step(V.scalar_tensor_tensor(x[:, t, :], x[:, t, :], ALPHA, a, ALU.mult, ALU.add))
                        norm.statistics(dve, t)
                    norm.scales(dve, NT - 1)
                    dve.wait_ge(ln2_in[i], 32)
                    norm.late(dve, V, dchain, NT - 1).then_inc(whole_last, 1)

        COMBINE = at(BIG, 2, D), at(BIG + 2 * D, 2, D)
        g2_in, ln2_in = ([lasting_sem(f"{n}{i}") for i in range(DEPTH)] for n in ("g2_loaded", "ln2_loaded"))
        up_in, dn_in = [None, None], [None, None]

        def new_weight_sems(i):
            for b in range(2):
                up_in[b], dn_in[b] = sem(f"x{i}_upin{b}"), sem(f"x{i}_dnin{b}")

        take_upper("start")
        setup()
        stream("ada", FIRST_ADA, None, None)
        finish_modulation("fm0", [(0, 0, 2 * KD)], [])
        take_upper("in0", SPLIT)
        ht = [parts(n * KD * TOK, KD, TOK) for n in range(2)]
        modulated("l0_h1", 0, ht, 0, 1, I["ev_w_in"][0], EV_IN // 16)
        rest = [("ada", i, c, half) for i, c0 in ((0, 4), (1, 0)) for c in range(c0, ADA_CH) for half in range(2)]
        jobs = []
        main = w_jobs(I["ev_w_in"][0], EV_IN, EV_IN // 16)
        for n, chunk_jobs in enumerate(main):
            take = -(-len(rest) // (len(main) - n))
            for m, job in enumerate(chunk_jobs):
                jobs += [job] + rest[m:m + 1] * (m < take)
            rest = rest[take:]
        assert not rest
        stream("ev", jobs, ht, proj, True)
        finish_modulation("fm1", [(0, 2 * KD, NMOD), (1, 0, NMOD)], list(range(DEPTH)))
        take_upper("layer0")
        retention()
        mlaT = at(R + 17408, MH // 2, TOK)
        latent_attention(mlaT)
        recycle_sems()
        new_weight_sems(0)
        mix_out("ev_out", 0, I["ev_w_out"][0], [proj[:, :, RG + k * P:RG + (k + 1) * P] for k in range(RH * RDV // P)],
                [mlaT[:, k, :] for k in range(MH // 2)])
        router(0)
        experts(0)
        combine(0)
        recycle_sems()
        new_weight_sems(1)
        take_upper("in1", SPLIT)
        ht = [parts(n * KD * TOK, KD, TOK) for n in range(2)]
        modulated("l1_h1", 1, ht, 0, 1, I["od_w_in"][0], OD_CW)
        pj = at(BIG, NT, OD_IN)
        rope = at(R + KD * IN_CW, 2, NT - 1, DDH // 2)
        rope_tmp = at(R + KD * IN_CW + 256, 4, NT - 1, OD_CW // DDH, DDH // 2)
        stream("od", [job for jobs_ in w_jobs(I["od_w_in"][0], OD_IN, OD_CW) for job in jobs_], ht, pj,
               rotate=(rope, [pj[:, 1:NT, c:c + OD_CW].rearrange("p t (g d) -> p t g d", d=DDH) for c in range(0, 2 * D, OD_CW)],
                       rope_tmp))
        take_upper("layer1")
        differential_attention(pj)
        mix_out("od_out", 1, I["od_w_out"][0], [pj[:, :, k * P:(k + 1) * P] for k in range(KD)], [], dng)
        router(1)
        experts(1)
        combine(1)
        with nc.Block(no_gpsimd_drain=True) as block:
            @block.sync
            def _(sp):
                sp.wait_ge(stored, stores[0])


INPUTS = ["x_prompt", "x_sample", "state_ret_fwd", "state_ret_bwd", "cache_mla_ckv", "cache_mla_krope",
          "cache_diff_k", "cache_diff_v", "c", "c_ctx", "ada_w", "ada_b", "ln1_g", "ln1_b", "ln2_g", "ln2_b",
          "ev_w_in", "ev_w_out", "ret_decay_fwd", "ret_decay_bwd", "mla_kv_norm_g", "mla_w_uk", "mla_w_uv",
          "od_w_in", "od_w_out", "diff_lambda", "diff_norm_g", "moe_w_group", "moe_b_group", "moe_w_expert",
          "moe_b_expert", "moe_w1", "moe_w3", "moe_w2"]
OUTPUTS = [("y_prompt", (1, SEQ, D)), ("y_sample", (1, LAT, D)),
           ("new_state_ret_fwd", (1, 1, RH, RDK, RDV)), ("new_state_ret_bwd", (1, 1, RH, RDK, RDV)),
           ("new_cache_mla_ckv", (1, 1, SEQ, MKV)), ("new_cache_mla_krope", (1, 1, SEQ, MR)),
           ("new_cache_diff_k", (1, 1, DH, SEQ, DDV)), ("new_cache_diff_v", (1, 1, DH, SEQ, DDV))]


def kernel(**inputs):
    import concourse.bacc as bacc
    from concourse.bass_utils import run_bass_kernel_spmd

    nc = bacc.Bacc("TRN2", target_bir_lowering=False, num_devices=1)
    arrays = {f"in_{n}": np.ascontiguousarray(inputs[n]) for n in INPUTS}
    consts, rope_mla, rope_diff = constants()
    arrays.update({"in_consts": consts, "in_rope_mla": rope_mla, "in_rope_diff": rope_diff})
    I = {n[3:]: nc.dram_tensor(n, a.shape, F32, kind="ExternalInput").ap() for n, a in arrays.items()}
    O = {n: nc.dram_tensor(f"out_{n}", s, F32, kind="ExternalOutput").ap() for n, s in OUTPUTS}
    build(nc, I, O)
    r = run_bass_kernel_spmd(nc, [arrays], core_ids=[0])
    return tuple(r.results[0][f"out_{n}"] for n, _ in OUTPUTS)
```
